# Optimizing a Trainium2 kernel written in Bass

```python
import jax, jax.numpy as jnp
from jax import lax
import numpy as np

D_MODEL = 1024
BATCH = 1
SEQ = 256
DEPTH = 2
DEC_BATCH = 8
DEC_SEQ = 1
PAST_LEN = 2048
PAGE_SIZE = 128

D_INNER = D_MODEL
SSM_HEAD_DIM = 64
SSM_HEADS = D_INNER // SSM_HEAD_DIM
SSM_GROUPS = 2
SSM_HPG = SSM_HEADS // SSM_GROUPS
D_STATE = 128
CONV_WIDTH = 4
CONV_DIM = D_INNER + 2 * SSM_GROUPS * D_STATE
SSD_CHUNK = 128
MLA_HEADS = 8
QK_NOPE = 64
QK_ROPE = 32
V_HEAD = 64
Q_LORA = 384
KV_LORA = 256
ROPE_THETA = 10000.0
Q_BLOCK = 128
ATTN_SCALE = (QK_NOPE + QK_ROPE) ** -0.5
PEER_HEADS = 8
N_KEYS = 128
N_EXPERTS = N_KEYS * N_KEYS
PEER_D_KEY = 256
PEER_TOPK = 16
PEER_BLOCK = 128
EPS = 1e-6

_SIZES = (D_MODEL, D_MODEL, D_INNER, CONV_DIM, SSM_HEADS, Q_LORA, KV_LORA, QK_ROPE)
IN_DIM = sum(_SIZES)
SPLIT_POINTS = tuple(int(s) for s in np.cumsum(_SIZES)[:-1])

kernel_name = "hybrid_ssd_mla_peer_step"

def rmsnorm(x, w):
    xf = x.astype(jnp.float32)
    xf = xf * lax.rsqrt(jnp.mean(xf * xf, axis=-1, keepdims=True) + EPS)
    return (xf * w.astype(jnp.float32)).astype(x.dtype)

def rope(x, pos):
    half = x.shape[-1] // 2
    inv = ROPE_THETA ** (-jnp.arange(half, dtype=jnp.float32) / half)
    ang = pos.astype(jnp.float32)[:, None] * inv[None, :]
    shape = (1, ang.shape[0]) + (1,) * (x.ndim - 3) + (half,)
    cos = jnp.cos(ang).reshape(shape)
    sin = jnp.sin(ang).reshape(shape)
    xf = x.astype(jnp.float32)
    x1, x2 = xf[..., :half], xf[..., half:]
    return jnp.concatenate([x1 * cos - x2 * sin, x1 * sin + x2 * cos], axis=-1).astype(x.dtype)

def causal_conv(xbc, prev, w, b):
    L = xbc.shape[1]
    xpad = jnp.concatenate([prev.astype(xbc.dtype), xbc], axis=1)
    out = b
    for k in range(CONV_WIDTH):
        out = out + xpad[:, k:k + L] * w[k]
    return jax.nn.silu(out), xpad[:, L:]

def ssd_scan(xh, dt, A, Bm, Cm, h0):
    b, L = xh.shape[:2]
    cl = SSD_CHUNK if L % SSD_CHUNK == 0 else L
    nc = L // cl
    f32 = jnp.float32
    x_c = xh.astype(f32).reshape((b, nc, cl) + xh.shape[2:])
    dt_c = dt.astype(f32).reshape((b, nc, cl) + dt.shape[2:])
    B_c = Bm.astype(f32).reshape((b, nc, cl) + Bm.shape[2:])
    C_c = Cm.astype(f32).reshape((b, nc, cl) + Cm.shape[2:])
    a_cs = jnp.cumsum(dt_c * A.astype(f32), axis=2)
    seg = a_cs[:, :, :, None] - a_cs[:, :, None, :]
    causal = (jnp.arange(cl)[:, None] >= jnp.arange(cl)[None, :])[None, None, :, :, None, None]
    Lmat = jnp.exp(jnp.where(causal, seg, -jnp.inf))
    xdt = x_c * dt_c[..., None]
    CB = jnp.einsum('bclgn,bcsgn->bclsg', C_c, B_c)
    y_diag = jnp.einsum('bclsg,bclsge,bcsgep->bclgep', CB, Lmat, xdt)
    decay_to_end = jnp.exp(a_cs[:, :, -1:] - a_cs)
    chunk_states = jnp.einsum('bclgn,bclge,bclgep->bcgepn', B_c, decay_to_end, xdt)
    chunk_decay = jnp.exp(a_cs[:, :, -1])

    def step(h, inp):
        dec, st = inp
        return dec[..., None, None] * h + st, h

    h_final, h_prev = lax.scan(step, h0.astype(f32),
                               (jnp.moveaxis(chunk_decay, 1, 0), jnp.moveaxis(chunk_states, 1, 0)))
    h_prev = jnp.moveaxis(h_prev, 0, 1)
    y_off = jnp.einsum('bclgn,bcgepn,bclge->bclgep', C_c, h_prev, jnp.exp(a_cs))
    y = (y_diag + y_off).reshape(xh.shape)
    return y.astype(xh.dtype), h_final.astype(h0.dtype)

def ssd_branch(z, xbc_raw, dt_raw, h0, conv_prev, conv_w, conv_b, dt_bias, a_log, d_skip, ssm_norm, w_ssm_proj):
    b, L = z.shape[:2]
    xbc, conv_new = causal_conv(xbc_raw, conv_prev, conv_w, conv_b)
    xs = xbc[..., :D_INNER]
    Bm = xbc[..., D_INNER:D_INNER + SSM_GROUPS * D_STATE].reshape(b, L, SSM_GROUPS, D_STATE)
    Cm = xbc[..., D_INNER + SSM_GROUPS * D_STATE:].reshape(b, L, SSM_GROUPS, D_STATE)
    xh = xs.reshape(b, L, SSM_GROUPS, SSM_HPG, SSM_HEAD_DIM)
    dt = jax.nn.softplus(dt_raw + dt_bias).reshape(b, L, SSM_GROUPS, SSM_HPG)
    A = -jnp.exp(a_log).reshape(SSM_GROUPS, SSM_HPG)
    y, h_new = ssd_scan(xh, dt, A, Bm, Cm, h0)
    y = y + d_skip.reshape(SSM_GROUPS, SSM_HPG)[..., None] * xh
    y = y.reshape(b, L, D_INNER) * jax.nn.silu(z)
    y = rmsnorm(y.reshape(b, L, SSM_GROUPS, D_INNER // SSM_GROUPS),
                ssm_norm.reshape(SSM_GROUPS, D_INNER // SSM_GROUPS)).reshape(b, L, D_INNER)
    return y @ w_ssm_proj, h_new, conv_new

def mla_attention(q_lat, q_pe, kv, kr, q_pos, k_pos):
    b, L = q_lat.shape[:2]
    blk = Q_BLOCK if L % Q_BLOCK == 0 else L
    nb = L // blk

    def to_blocks(a):
        return jnp.moveaxis(a.reshape((b, nb, blk) + a.shape[2:]), 1, 0)

    def one(args):
        ql, qp, qpos = args
        s = (jnp.einsum('bqhr,btr->bhqt', ql, kv) + jnp.einsum('bqhd,btd->bhqt', qp, kr)).astype(jnp.float32) * ATTN_SCALE
        mask = k_pos[None, :] <= qpos[:, None]
        p = jax.nn.softmax(jnp.where(mask, s, -jnp.inf), axis=-1).astype(kv.dtype)
        return jnp.einsum('bhqt,btr->bqhr', p, kv)

    o = lax.map(one, (to_blocks(q_lat), to_blocks(q_pe), q_pos.reshape(nb, blk)))
    return jnp.moveaxis(o, 0, 1).reshape(b, L, MLA_HEADS, KV_LORA)

def mla_branch(c_q, c_kv, kr_raw, pos, past_lat, past_kr, q_norm, w_qb, kv_norm, w_kvb, w_mla_proj):
    b, L = c_q.shape[:2]
    q = (rmsnorm(c_q, q_norm) @ w_qb).reshape(b, L, MLA_HEADS, QK_NOPE + QK_ROPE)
    q_nope = q[..., :QK_NOPE]
    q_pe = rope(q[..., QK_NOPE:], pos)
    lat = rmsnorm(c_kv, kv_norm)
    kpe = rope(kr_raw[:, :, None, :], pos)[:, :, 0]
    wkv = w_kvb.reshape(KV_LORA, MLA_HEADS, QK_NOPE + V_HEAD)
    w_kb, w_vb = wkv[..., :QK_NOPE], wkv[..., QK_NOPE:]
    q_lat = jnp.einsum('blhd,rhd->blhr', q_nope, w_kb)
    if past_lat is None:
        kv_all, kr_all, k_pos = lat, kpe, pos
    else:
        kv_all = jnp.concatenate([past_lat.astype(lat.dtype), lat], axis=1)
        kr_all = jnp.concatenate([past_kr.astype(kpe.dtype), kpe], axis=1)
        k_pos = jnp.arange(past_lat.shape[1] + L, dtype=jnp.int32)
    o_lat = mla_attention(q_lat, q_pe, kv_all, kr_all, pos, k_pos)
    o = jnp.einsum('blhr,rhv->blhv', o_lat, w_vb).reshape(b, L, MLA_HEADS * V_HEAD)
    return o @ w_mla_proj, lat, kpe

def peer(h, wq, keys, u, v):
    b, L, D = h.shape
    n = b * L
    blk = PEER_BLOCK if n % PEER_BLOCK == 0 else n
    half = PEER_D_KEY // 2

    def one(tb):
        q = (tb @ wq).reshape(blk, PEER_HEADS, PEER_D_KEY)
        s1 = jnp.einsum('thd,hkd->thk', q[..., :half], keys[:, 0])
        s2 = jnp.einsum('thd,hkd->thk', q[..., half:], keys[:, 1])
        sc1, i1 = lax.top_k(s1, PEER_TOPK)
        sc2, i2 = lax.top_k(s2, PEER_TOPK)
        cand = (sc1[..., :, None] + sc2[..., None, :]).reshape(blk, PEER_HEADS, PEER_TOPK * PEER_TOPK)
        cidx = (i1[..., :, None] * N_KEYS + i2[..., None, :]).reshape(blk, PEER_HEADS, PEER_TOPK * PEER_TOPK)
        sc, sel = lax.top_k(cand, PEER_TOPK)
        idx = jnp.take_along_axis(cidx, sel, axis=-1)
        g = jax.nn.softmax(sc.astype(jnp.float32), axis=-1)
        act = jax.nn.gelu(jnp.einsum('thkd,td->thk', u[idx], tb), approximate=False)
        wgt = (g * act.astype(jnp.float32)).astype(tb.dtype)
        return jnp.einsum('thk,thkd->td', wgt, v[idx])

    out = lax.map(one, h.reshape(n // blk, blk, D))
    return out.reshape(b, L, D)

def trunk_layer(x, pos, h0, conv_prev, past_lat, past_kr, p):
    (norm_mix, w_in, b_gate, conv_w, conv_b, dt_bias, a_log, d_skip, ssm_norm, w_ssm_proj,
     q_norm, w_qb, kv_norm, w_kvb, w_mla_proj, w_out, norm_ffn, peer_wq, peer_keys, peer_u, peer_v) = p
    h = rmsnorm(x, norm_mix)
    proj = h @ w_in
    gate_a, gate_b, z, xbc, dt_raw, c_q, c_kv, kr_raw = jnp.split(proj, SPLIT_POINTS, axis=-1)
    ya, h_new, conv_new = ssd_branch(z, xbc, dt_raw, h0, conv_prev, conv_w, conv_b, dt_bias, a_log,
                                     d_skip, ssm_norm, w_ssm_proj)
    yb, lat_new, kr_new = mla_branch(c_q, c_kv, kr_raw, pos, past_lat, past_kr, q_norm, w_qb, kv_norm,
                                     w_kvb, w_mla_proj)
    ga = jax.nn.sigmoid(gate_a + b_gate[:D_MODEL])
    gb = jax.nn.sigmoid(gate_b + b_gate[D_MODEL:])
    x = x + (ga * ya + gb * yb) @ w_out
    x = x + peer(rmsnorm(x, norm_ffn), peer_wq, peer_keys, peer_u, peer_v)
    return x, h_new, conv_new, lat_new, kr_new

def setup_inputs(seed: int = 0) -> dict:
    key = jax.random.key(seed)
    ks = jax.random.split(key, 40)
    f32 = jnp.float32
    n_pages = PAST_LEN // PAGE_SIZE
    n_used = DEC_BATCH * n_pages
    n_pool = n_used + max(1, n_used // 4)
    nrm = lambda k, s, sc: jax.random.normal(k, s, f32) * sc
    gain = lambda k, s: 1.0 + 0.02 * jax.random.normal(k, s, f32)
    dt0 = jnp.exp(jax.random.uniform(ks[10], (DEPTH, SSM_HEADS), f32, np.log(1e-3), np.log(1e-1)))
    return {
        "x_prompt": nrm(ks[0], (BATCH, SEQ, D_MODEL), 1.0),
        "x_sample": nrm(ks[1], (DEC_BATCH, DEC_SEQ, D_MODEL), 1.0),
        "cache_latent": nrm(ks[2], (DEPTH, n_pool, PAGE_SIZE, KV_LORA), 1.0),
        "cache_krope": nrm(ks[3], (DEPTH, n_pool, PAGE_SIZE, QK_ROPE), 1.0),
        "state_ssm": nrm(ks[4], (DEPTH, DEC_BATCH, SSM_GROUPS, SSM_HPG, SSM_HEAD_DIM, D_STATE), 0.1),
        "state_conv": nrm(ks[5], (DEPTH, DEC_BATCH, CONV_WIDTH - 1, CONV_DIM), 1.0),
        "page_table": jax.random.permutation(ks[6], n_pool)[:n_used].reshape(DEC_BATCH, n_pages).astype(jnp.int32),
        "norm_mix": gain(ks[7], (DEPTH, D_MODEL)),
        "w_in": nrm(ks[8], (DEPTH, D_MODEL, IN_DIM), D_MODEL ** -0.5),
        "b_gate": nrm(ks[9], (DEPTH, 2 * D_MODEL), 0.02),
        "conv_w": nrm(ks[11], (DEPTH, CONV_WIDTH, CONV_DIM), CONV_WIDTH ** -0.5),
        "conv_b": nrm(ks[12], (DEPTH, CONV_DIM), 0.02),
        "dt_bias": dt0 + jnp.log(-jnp.expm1(-dt0)),
        "a_log": jnp.log(jax.random.uniform(ks[13], (DEPTH, SSM_HEADS), f32, 1.0, 16.0)),
        "d_skip": gain(ks[14], (DEPTH, SSM_HEADS)),
        "ssm_norm": gain(ks[15], (DEPTH, D_INNER)),
        "w_ssm_proj": nrm(ks[16], (DEPTH, D_INNER, D_MODEL), D_INNER ** -0.5),
        "q_norm": gain(ks[17], (DEPTH, Q_LORA)),
        "w_qb": nrm(ks[18], (DEPTH, Q_LORA, MLA_HEADS * (QK_NOPE + QK_ROPE)), Q_LORA ** -0.5),
        "kv_norm": gain(ks[19], (DEPTH, KV_LORA)),
        "w_kvb": nrm(ks[20], (DEPTH, KV_LORA, MLA_HEADS * (QK_NOPE + V_HEAD)), KV_LORA ** -0.5),
        "w_mla_proj": nrm(ks[21], (DEPTH, MLA_HEADS * V_HEAD, D_MODEL), (MLA_HEADS * V_HEAD) ** -0.5),
        "w_out": nrm(ks[22], (DEPTH, D_MODEL, D_MODEL), D_MODEL ** -0.5),
        "norm_ffn": gain(ks[23], (DEPTH, D_MODEL)),
        "peer_wq": nrm(ks[24], (DEPTH, D_MODEL, PEER_HEADS * PEER_D_KEY), D_MODEL ** -0.5),
        "peer_keys": nrm(ks[25], (DEPTH, PEER_HEADS, 2, N_KEYS, PEER_D_KEY // 2), (PEER_D_KEY // 2) ** -0.5),
        "peer_u": nrm(ks[26], (DEPTH, N_EXPERTS, D_MODEL), D_MODEL ** -0.5),
        "peer_v": nrm(ks[27], (DEPTH, N_EXPERTS, D_MODEL), 0.1),
        "norm_final": gain(ks[28], (D_MODEL,)),
    }

def reference(x_prompt, x_sample, cache_latent, cache_krope, state_ssm, state_conv, page_table,
              norm_mix, w_in, b_gate, conv_w, conv_b, dt_bias, a_log, d_skip, ssm_norm, w_ssm_proj,
              q_norm, w_qb, kv_norm, w_kvb, w_mla_proj, w_out, norm_ffn, peer_wq, peer_keys,
              peer_u, peer_v, norm_final):
    bp, sp = x_prompt.shape[:2]
    bs, ss = x_sample.shape[:2]
    past_len = page_table.shape[1] * cache_latent.shape[2]
    pos_p = jnp.arange(sp, dtype=jnp.int32)
    pos_s = past_len + jnp.arange(ss, dtype=jnp.int32)
    h0_p = jnp.zeros((bp, SSM_GROUPS, SSM_HPG, SSM_HEAD_DIM, D_STATE), x_prompt.dtype)
    conv0_p = jnp.zeros((bp, CONV_WIDTH - 1, CONV_DIM), x_prompt.dtype)
    xp, xs = x_prompt, x_sample
    lat_p, kr_p, ssm_p, conv_p = [], [], [], []
    lat_s, kr_s, ssm_s, conv_s = [], [], [], []
    for l in range(DEPTH):
        p = (norm_mix[l], w_in[l], b_gate[l], conv_w[l], conv_b[l], dt_bias[l], a_log[l], d_skip[l],
             ssm_norm[l], w_ssm_proj[l], q_norm[l], w_qb[l], kv_norm[l], w_kvb[l], w_mla_proj[l],
             w_out[l], norm_ffn[l], peer_wq[l], peer_keys[l], peer_u[l], peer_v[l])
        past_lat = cache_latent[l][page_table].reshape(bs, past_len, KV_LORA)
        past_kr = cache_krope[l][page_table].reshape(bs, past_len, QK_ROPE)
        xp, hp, cp, lp, kp = trunk_layer(xp, pos_p, h0_p, conv0_p, None, None, p)
        xs, hs, cs, lsn, ksn = trunk_layer(xs, pos_s, state_ssm[l], state_conv[l], past_lat, past_kr, p)
        lat_p.append(lp); kr_p.append(kp); ssm_p.append(hp); conv_p.append(cp)
        lat_s.append(lsn); kr_s.append(ksn); ssm_s.append(hs); conv_s.append(cs)
    y_prompt = rmsnorm(xp, norm_final)
    y_sample = rmsnorm(xs, norm_final)
    return (y_prompt, y_sample,
            jnp.stack(lat_p), jnp.stack(kr_p), jnp.stack(ssm_p), jnp.stack(conv_p),
            jnp.stack(lat_s), jnp.stack(kr_s), jnp.stack(ssm_s), jnp.stack(conv_s))


_drawn_inputs = setup_inputs


def setup_inputs(seed=0):
    import zlib

    import numpy as np

    out = dict(_drawn_inputs(seed))
    spreads = {}
    factors = {'cache_krope': 3.727,
     'b_gate': 7.901,
     'd_skip': 5.968,
     'ssm_norm': 3.575,
     'q_norm': 8.0,
     'kv_norm': 2.962,
     'norm_ffn': 5.884,
     'norm_final': 2.739}
    for name, (base, spread) in spreads.items():
        noise = np.random.default_rng([zlib.crc32(name.encode()), seed]).standard_normal(out[name].shape)
        drawn = base * np.exp(spread * noise) if base else spread * noise
        out[name] = __import__('jax').numpy.asarray(drawn.astype(out[name].dtype))
    for name, factor in factors.items():
        out[name] = (out[name] * factor).astype(out[name].dtype)
    return out
```

```python
from contextlib import ExitStack

import numpy as np

import concourse.bass as bass
from concourse import mybir

ALU = mybir.AluOpType
ACT = mybir.ActivationFunctionType
AX = mybir.AxisListType
F32 = mybir.dt.float32
I32 = mybir.dt.int32
U32 = mybir.dt.uint32

D_MODEL, SEQ, DEPTH, SAMPLES = 1024, 256, 2, 8
TOKENS = SEQ + SAMPLES
HEADS, GROUPS, HEAD_DIM, D_STATE, CONV = 16, 2, 64, 128, 4
CONV_DIM = D_MODEL + 2 * GROUPS * D_STATE
A_HEADS, NOPE, ROPE, V_HEAD, Q_LORA, KV_LORA = 8, 64, 32, 64, 384, 256
PAST, PAGE = 2048, 128
PAGES = PAST // PAGE
SCALE = (NOPE + ROPE) ** -0.5
P_HEADS, N_KEYS, TOPK = 8, 128, 16
N_EXPERTS = N_KEYS * N_KEYS
EPS = 1e-6
NEG = -1e30
P = 128
TILES = [(0, P), (P, P), (SEQ, SAMPLES)]
DC = D_MODEL // P
C_DT = 3 * D_MODEL + CONV_DIM
IN_DIM = C_DT + HEADS + Q_LORA + KV_LORA + ROPE
BLOCK = 256
MAIN_BLOCKS = C_DT // BLOCK
TAIL = [(0, 272), (272, 256), (528, 160)]
TAIL_W = IN_DIM - C_DT
T_CQ, T_CKV, T_KR = HEADS, HEADS + Q_LORA, HEADS + Q_LORA + KV_LORA
PAD = CONV - 1
CONV_ROW = PAD + SEQ + CONV * SAMPLES
CONV_OUT = CONV_ROW - PAD
S_COL = PAD + SEQ
CC = CONV_DIM // P
PIECE = PAST // P
PIECES = PAGE // PIECE
RING = 8
PE_SLOTS, VECTOR_SLOTS = (0, 1, 2, 4, 5), (3, 6, 7)
TURNS = (P // RING, P // RING, TOPK // RING)
BEFORE = [sum(TURNS[:t]) for t in range(4)]
U_DONE = [RING * (n + 1) for n in BEFORE]
U_USES = [2 * n for n in BEFORE]
V_USES = [2 * BEFORE[t] + TURNS[t] for t in range(3)] + [2 * BEFORE[3]]
PE_USES = [len(PE_SLOTS) * n for n in BEFORE]
VECTOR_USES = [len(VECTOR_SLOTS) * n for n in BEFORE]
VEC_ROWS = CONV * CC + CC + 2 * DC

CONSTS = {}


def constants():
    p = np.arange(P)
    out = {}
    out["ident"] = np.eye(P)
    out["triu"] = (p[:, None] <= p[None, :]) * 1.0
    out["neg"] = np.where(p[:, None] > p[None, :], NEG, 0.0)
    out["ones"] = np.ones((P, P))
    out["causal"] = np.where(p[None, :] > p[:, None], NEG, 0.0)
    newmask = np.zeros((P, SAMPLES))
    newmask[:SAMPLES] = np.where(np.eye(SAMPLES) > 0, 0.0, NEG)
    out["newmask"] = newmask
    out["quarter"] = (p[:, None] // ROPE == np.arange(4)[None, :]) * 1.0
    out["mod8"] = (p[:, None] % SAMPLES == np.arange(SAMPLES)[None, :]) * 1.0
    rep = np.zeros((P, 64))
    rep[:SAMPLES] = np.arange(SAMPLES)[:, None] == np.arange(64)[None, :] % SAMPLES
    out["rep"] = rep
    out["iota"] = np.broadcast_to(np.arange(TOPK)[None, :], (P, TOPK))
    out["piece"] = (p % PIECES)[:, None]
    pos = np.concatenate([np.arange(SEQ), np.full(P, PAST)]).astype(np.float32)
    half = ROPE // 2
    inv = (np.float32(10000.0) ** (-np.arange(half, dtype=np.float32) / np.float32(half))).astype(np.float32)
    ang = (pos[:, None] * inv[None, :]).astype(np.float32).astype(np.float64)
    for name, f in (("cos", np.cos), ("sin", np.sin)):
        out[name] = f(ang).reshape(3, P, half).transpose(1, 0, 2).reshape(P, 3 * half)
    at = 0
    for name, a in out.items():
        CONSTS[name] = (at, at + a.shape[1])
        at += a.shape[1]
    return np.ascontiguousarray(np.concatenate([np.asarray(a, np.float32) for a in out.values()], axis=1))


CONST_ARRAY = constants()


class Ring:

    def __init__(self, eng, full, free, banks):
        self.eng, self.full, self.free, self.banks = eng, full, free, banks
        self.n, self.base = 0, 0

    def fill(self):
        self.eng.wait_ge(self.free, self.base + self.n + 1)
        return self.banks[self.n % 4]

    def filled(self, ins):
        ins.then_inc(self.full, 1)
        self.n += 1

    def all_emptied(self):
        self.eng.wait_ge(self.free, self.base + self.n + 4)

    def read(self):
        self.eng.wait_ge(self.full, self.base + self.n + 1)
        return self.banks[self.n % 4]

    def emptied(self, ins, wait=False):
        ins.then_inc(self.free, 1)
        self.n += 1
        if wait:
            self.eng.wait_ge(self.free, self.base + self.n + 4)

    def enter(self, i, per):
        self.base = i * per
        self.per = per

    def leave(self, turns):
        self.base = 0
        self.n += (turns - 1) * self.per


class Own:

    def __init__(self, eng, sem):
        self.eng, self.sem, self.n, self.base = eng, sem, 0, 0

    def then(self, ins):
        ins.then_inc(self.sem, 1)
        self.n += 1
        self.eng.wait_ge(self.sem, self.base + self.n)

    def enter(self, i, per):
        self.base, self.per, self.at = i * per, per, self.n

    def leave(self, turns):
        assert self.n - self.at == self.per, (self.n - self.at, self.per)
        self.base = 0
        self.n += (turns - 1) * self.per


def cut(names, offset=0):
    out = {}
    for name, size in names:
        out[name] = (offset, offset + size)
        offset += size
    return out, offset


ARENA_SSD, A1 = cut([
    ("vrows", 128), ("cstate", CONV_DIM), ("z", DC * TOKENS), ("pad", CC * CONV_ROW), ("conv", CC * CONV_ROW),
    ("sig", CC * CONV_ROW), ("xt", 3 * D_MODEL), ("bt", 2 * 256), ("bcs", 512), ("xdt", 2 * D_MODEL), ("cb", 512),
    ("hpt", 1024), ("y", 3 * D_MODEL),
])
ARENA_SSD["el"] = (ARENA_SSD["sig"][0], ARENA_SSD["sig"][0] + 2048)
ARENA_SSD["xde"] = (ARENA_SSD["el"][1], ARENA_SSD["el"][1] + 1024)
ARENA_SSD["yt"] = ARENA_SSD["z"]
pad0 = ARENA_SSD["pad"][0]
ARENA_SSD["hs"] = (pad0, pad0 + 1024)
ARENA_SSD["xdf"] = (pad0 + 1024, pad0 + 3072)
s0 = ARENA_SSD["sig"][0]
ARENA_SSD["st"] = (s0, s0 + 2048)
ARENA_SSD["stx"] = (pad0 + 1024, pad0 + 2048)
ARENA_SSD["rawt"] = (ARENA_SSD["xdt"][0], ARENA_SSD["xdt"][0] + CONV_DIM)

ARENA_ATT, A2 = cut([
    ("wkv", 2048), ("wkt", 2048), ("ck", 2 * 4096), ("cr", 2 * 512), ("kt", 4096 + 512), ("qpt", A_HEADS * TOKENS),
    ("ql", 2 * A_HEADS * TOKENS), ("qpad", 256),
])
k0 = ARENA_ATT["kt"][0]
ARENA_ATT["qnt"] = (k0, k0 + A_HEADS * TOKENS)
ARENA_ATT["wqb"] = (k0 + A_HEADS * TOKENS, k0 + A_HEADS * TOKENS + 2304)
ARENA_ATT["s"] = (k0, k0 + 2048)
ARENA_ATT["pt"] = (k0 + 2048, k0 + 4096)
ARENA_ATT["ot"] = (k0, k0 + 4 * TOKENS)
c0 = ARENA_ATT["ck"][0]
ARENA_ATT["qr"] = (c0, c0 + 768)
ARENA_ATT["qpe"] = (c0 + 768, c0 + 1536)
ARENA_ATT["qrep"] = (c0 + 3072, c0 + 4096)
ARENA_ATT["rt"] = (c0 + 1536, c0 + 1536 + 4 * 384)

ARENA_PEER, A3 = cut([
    ("ring", RING * D_MODEL), ("keys", 2048), ("keyst", 2048), ("sc", 2048), ("qz", 2 * 576),
    ("cand", 2048), ("hot", 2048), ("hot2", 2048), ("top", 256), ("topi", 256), ("topf", 256), ("ctop", 128), ("ctopi", 128),
    ("idx", 3 * P), ("wgt", 3 * P), ("dots", P), ("hr", D_MODEL), ("acc", D_MODEL), ("diag", RING * P), ("zero", P), ("dot8", RING),
    ("s0", 256), ("sel1", 128), ("sel2", 128), ("stage", 16), ("i1", 128), ("i2", 128),
])


def build(nc, layers, a, out):
    (o_yp, o_ys, o_latp, o_krp, o_ssmp, o_convp, o_lats, o_krs, o_ssms, o_convs) = out
    with ExitStack() as ctx:
        def sb(name, cols, dt=F32):
            return ctx.enter_context(nc.sbuf_tensor(name, [P, cols], dt))

        sems = {}

        def sem(name):
            if name not in sems:
                sems[name] = ctx.enter_context(nc.semaphore(name))
            return sems[name]

        def bc(ap, axis, n):
            u = ap.unsqueeze(axis)
            shape = list(u.shape)
            shape[axis] = n
            return u.to_broadcast(shape)

        def of_layer(name, l):
            ap = a[name]
            rest = "bcdef"[: len(ap.shape) - 1]
            s = ap[bass.ds(l, 1)] if len(ap.shape) == 1 else ap[(bass.ds(l, 1),) + (slice(None),) * len(rest)]
            return s.rearrange(f"a {' '.join(rest)} -> (a {rest[0]}) {' '.join(rest[1:])}")

        consts = sb("consts", CONST_ARRAY.shape[1])
        cst = lambda name: consts[:, CONSTS[name][0]:CONSTS[name][1]]
        ident, triu, neg, ones = cst("ident"), cst("triu"), cst("neg"), cst("ones")
        cos = cst("cos").rearrange("p (t k) -> p t k", t=3)
        sin = cst("sin").rearrange("p (t k) -> p t k", t=3)

        x = sb("x", 3 * D_MODEL)[:, :].rearrange("p (t d) -> p t d", t=3)
        hbuf = sb("h", 3 * D_MODEL)
        h = hbuf[:, :].rearrange("p (t d) -> p t d", t=3)
        shared = sb("ht_tok", 2 * A_HEADS * TOKENS)
        ht = shared[:, 0:DC * TOKENS].rearrange("p (c t) -> p c t", c=DC)
        tok = shared[:, DC * TOKENS:DC * TOKENS + 3 * TAIL_W].rearrange("p (t n) -> p t n", t=3)
        ol = shared[:, :].rearrange("p (r h t) -> p r h t", r=2, h=A_HEADS)
        wring = sb("wring", 2 * DC * 272)
        gate = sb("gate", 2 * DC * TOKENS)[:, :].rearrange("p (c t) -> p c t", c=2 * DC)
        lat = sb("lat", 3 * KV_LORA)[:, :].rearrange("p (t r) -> p t r", t=3)
        kpe = sb("kpe", 3 * ROPE)[:, :].rearrange("p (t r) -> p t r", t=3)
        latt = sb("latt", 2 * TOKENS)[:, :].rearrange("p (c t) -> p c t", c=2)
        kpet = sb("kpet", TOKENS)
        cqt = sb("cqt", 3 * TOKENS)[:, :].rearrange("p (c t) -> p c t", c=3)
        nrow = sb("nrow", D_MODEL)
        kvn = sb("kvn", KV_LORA)
        qn = sb("qn", 3)
        ssmn = sb("ssmn", DC)
        vt = sb("vt", VEC_ROWS)
        hd = sb("hd", 3 * HEADS)
        st = sb("st", 64)
        dtb = sb("dtb", 8 * 48)
        acs = sb("acs", 64)
        ex = sb("ex", 6 * 32)
        dtt = sb("dtt", 32)
        exs = sb("exs", DC * 16)
        dtx = sb("dtx", DC * SAMPLES)
        ysm = sb("ysm", DC * SAMPLES)
        att = sb("att", 160)
        sd = sb("sd", 17 * 8 * 3)
        page_idx = sb("page_idx", 2 * SAMPLES, I32)
        pagef = sb("pagef", 2 * SAMPLES)
        layer_off = sb("layer_off", 2)
        arena = sb("arena", max(A1, A2, A3))
        ps = ctx.enter_context(nc.psum_tensor("ps", [P, 8, 512], F32))

        def place(table):
            return lambda name: arena[:, table[name][0]:table[name][1]]

        ssd, mla, peer = place(ARENA_SSD), place(ARENA_ATT), place(ARENA_PEER)
        zt = ssd("z").rearrange("p (c t) -> p c t", c=DC)
        yt = zt
        pad = ssd("pad").rearrange("p (c t) -> p c t", c=CC)
        conv = ssd("conv").rearrange("p (c t) -> p c t", c=CC)
        sig = ssd("sig").rearrange("p (c t) -> p c t", c=CC)
        zsig = ssd("sig")[:, 0:DC * TOKENS].rearrange("p (c t) -> p c t", c=DC)
        xt = ssd("xt").rearrange("p (t d) -> p t d", t=3)
        bt = ssd("bt").rearrange("p (t n) -> p t n", t=2)
        bcs = ssd("bcs")
        xdt = ssd("xdt").rearrange("p (t d) -> p t d", t=2)
        cb = ssd("cb").rearrange("p (k l) -> p k l", k=4)
        hpt = ssd("hpt").rearrange("p (g q) -> p g q", g=2)
        y = ssd("y").rearrange("p (t d) -> p t d", t=3)
        el = ssd("el").rearrange("p (h l) -> p h l", h=HEADS)
        xde = ssd("xde")
        hs = ssd("hs")
        xdf = ssd("xdf").rearrange("p (t d) -> p t d", t=2)
        stt = ssd("st").rearrange("p (s c n) -> p s c n", s=2, c=DC)
        stx = ssd("stx")
        rawt = ssd("rawt")
        wkv = mla("wkv").rearrange("p (c n) -> p c n", c=2)
        wkt = mla("wkt").rearrange("p (h r) -> p h r", h=A_HEADS)
        ck = mla("ck").rearrange("p (s j r) -> p s j r", s=2, j=PIECE)
        cr = mla("cr").rearrange("p (s j r) -> p s j r", s=2, j=PIECE)
        kt = mla("kt")[:, 0:4096].rearrange("p (c j t) -> p c j t", c=2, j=PIECE)
        krt = mla("kt")[:, 4096:4608].rearrange("p (q t) -> p q t", q=4)
        qpt = mla("qpt").rearrange("p (h t) -> p h t", h=A_HEADS)
        ql = mla("ql").rearrange("p (c h t) -> p c h t", c=2, h=A_HEADS)
        qpad = mla("qpad").rearrange("p (b q h) -> p b q h", b=SAMPLES, q=4)
        qnt = mla("qnt").rearrange("p (h t) -> p h t", h=A_HEADS)
        wqb = mla("wqb").rearrange("p (c n) -> p c n", c=3)
        sc = mla("s").rearrange("p (h t) -> p h t", h=A_HEADS)
        pt = mla("pt").rearrange("p (k h t) -> p k h t", k=2, h=A_HEADS)
        ot = mla("ot").rearrange("p (c t) -> p c t", c=4)
        qr = mla("qr").rearrange("p (t h k) -> p t h k", t=3, h=A_HEADS)
        qpe = mla("qpe").rearrange("p (t h k) -> p t h k", t=3, h=A_HEADS)
        rtmp = mla("rt").rearrange("p (s t h k) -> p s t h k", s=4, t=3, h=A_HEADS)
        conv_s = conv[:, :, S_COL:S_COL + CONV * SAMPLES].rearrange("p c (b k) -> p c b k", k=CONV)
        pad_s = pad[:, :, S_COL:S_COL + CONV * SAMPLES].rearrange("p c (b k) -> p c b k", k=CONV)
        amax, anm, asum, ainv = (att[:, 8 * k:8 * k + 8] for k in range(4))
        dmx, dm8, dall, dsum, dinv = (att[:, 32 + 16 * k:32 + 16 * k + 8] for k in range(5))
        sraw, sexp = sd[:, 0:136].rearrange("p (j h) -> p j h", h=8), sd[:, 136:272].rearrange("p (j h) -> p j h", h=8)
        qb = sd[:, 272:288].rearrange("p (c h) -> p c h", c=2)
        dt, dta, dtu, dte, dtl, dtw, dtd, dti = (
            dtb[:, 48 * k:48 * k + 48].rearrange("p (t h) -> p t h", t=3) for k in range(8))
        a_cs = acs[:, :].rearrange("p (t k h) -> p t k h", t=2, k=2)
        ea, dec, decf, nacs, tmp16, eend = (ex[:, 32 * k:32 * k + 32].rearrange("p (t h) -> p t h", t=2) for k in range(6))
        exs4 = exs[:, :].rearrange("p (c k b) -> p c k b", c=DC, k=2)
        dtx3 = dtx[:, :].rearrange("p (c b) -> p c b", c=DC)
        ysm3 = ysm[:, :].rearrange("p (c b) -> p c b", c=DC)
        ss, rt, rs = st[:, 0:3], st[:, 3:6], st[:, 6:9]
        ss6, rt6, rs6 = st[:, 9:15], st[:, 15:21], st[:, 21:27]

        wblock = lambda s, chunks, cols: wring[:, s * DC * 272:s * DC * 272 + chunks * cols].rearrange(
            "p (c n) -> p c n", c=chunks)

        marks = {}
        ring = peer("ring").rearrange("p (k d) -> p k d", k=RING)
        keys = peer("keys").rearrange("p (k d) -> p k d", k=2 * P_HEADS)
        keyst = peer("keyst").rearrange("p (k d) -> p k d", k=2 * P_HEADS)
        keysc = peer("sc").rearrange("p (k n) -> p k n", k=2 * P_HEADS)
        qz = peer("qz").rearrange("p (s c) -> p s c", s=2)
        cand, hot, hot2, top, topf, ctop = (peer(n) for n in ("cand", "hot", "hot2", "top", "topf", "ctop"))
        topi, ctopi = peer("topi").bitcast(U32), peer("ctopi").bitcast(U32)
        i1, i2 = peer("i1").bitcast(U32), peer("i2").bitcast(U32)
        sel1, sel2, dots, hr, acc, zero, dot8 = (peer(n) for n in ("sel1", "sel2", "dots", "hr", "acc", "zero", "dot8"))
        idx = peer("idx").bitcast(I32).rearrange("p (t k) -> p t k", t=3)
        wgt = peer("wgt").rearrange("p (t k) -> p t k", t=3)
        diag = peer("diag").rearrange("p (k d) -> p k d", k=RING)
        stage = peer("stage").bitcast(I32)

        settled = st[:, 54:55]

        def turns_of(eng, t):
            if t < 2:
                with eng.Fori(0, TURNS[t]) as i:
                    yield i
            else:
                yield from range(TURNS[t])

        newest = sb("newest", CC * 11)[:, :].rearrange("p (c k) -> p c k", c=CC)
        xsamp = sb("xsamp", CC * SAMPLES)[:, :].rearrange("p (c b) -> p c b", c=CC)
        qrep = mla("qrep").rearrange("p (h q k) -> p h q k", h=A_HEADS, q=4)
        qpb = sd[:, 288:320].rearrange("p (q h) -> p q h", q=4)
        dm1 = sd[:, 320:321]

        def of_layer_out(ap, l):
            rest = "bcdef"[: len(ap.shape) - 1]
            return ap[(bass.ds(l, 1),) + (slice(None),) * len(rest)].rearrange(f"a {' '.join(rest)} -> (a {rest[0]}) {' '.join(rest[1:])}")

        def span(used):
            numbers = [s.num for s in used.values()]
            assert len(numbers) == max(numbers) - min(numbers) + 1
            return range(min(numbers), max(numbers) + 1)

        with nc.Block() as block:
            @block.sync
            def _(sp):
                sp.dma_start(consts[:, :], a["consts"]).then_inc(sem("first_loads"), 16)
                sp.dma_start(x[:, 0:2, :], a["x_prompt"].rearrange("o (t p) d -> p (o t) d", p=P)).then_inc(sem("first_loads"), 16)
                sp.wait_ge(sem("x_zeroed"), 1)
                sp.dma_start(x[0:SAMPLES, 2, :], a["x_sample"].rearrange("b o d -> (b o) d")).then_inc(sem("first_loads"), 16)
                with nc.allow_non_contiguous_dma(reason="page numbers, once"):
                    for b in range(SAMPLES):
                        sp.dma_start(page_idx[:, b:b + 1], bc(a["page_table"][b, :], 1, PIECES).rearrange(
                            "g (r o) -> g r o", o=1)).then_inc(sem("first_loads"), 16)
                sp.wait_ge(sem("first_loads"), 16 * (3 + SAMPLES))

            @block.vector
            def _(dve):
                dve.memset(x[:, 2, :], 0.0).then_inc(sem("x_zeroed"), 1)
                dve.memset(layer_off[:, :], 0.0).then_inc(sem("off_zeroed"), 1)
                dve.wait_ge(sem("first_loads"), 16 * (3 + SAMPLES))
                dve.tensor_copy(pagef[:, 0:SAMPLES], page_idx[:, 0:SAMPLES]).then_inc(sem("pagef"), 1)
                dve.wait_ge(sem("pagef"), 1)
                dve.tensor_scalar(pagef[:, SAMPLES:], pagef[:, 0:SAMPLES], float(PIECES), cst("piece"),
                                  ALU.mult, ALU.add).then_inc(sem("pagef"), 1)
                dve.wait_ge(sem("pagef"), 2)
        nc.all_engine_barrier(sems_to_clear=span(sems))

        with nc.Fori(0, layers) as layer:
            with nc.Block() as block:
                @block.tensor
                def _(pe):
                    wide = Ring(pe, sem("wide_full"), sem("wide_free"), (0, 1, 2, 3))
                    aux = Ring(pe, sem("aux_full"), sem("aux_free"), (4, 5, 6, 7))
                    state = {"n": 0, "fresh": False}
                    pe.nop().then_inc(sem("tensor_slots_used"), len(PE_SLOTS))

                    def next_block(chunks, cols, base=None):
                        n = state["n"]
                        pe.wait_ge(sem(f"block{n % 2}_loads"), (0 if base is None else base) + 16 * (n // 2 + 1))
                        state["n"] += 1
                        state["fresh"] = True
                        return wblock(n % 2, chunks, cols)

                    def product(dst, w, rhs, chunks, start=True, stop=True):
                        for c in range(chunks):
                            last = pe.matmul(dst, w(c), rhs(c), start=start and c == 0, stop=stop and c == chunks - 1)
                            if state["fresh"]:
                                last.then_inc(sem("blocks_begun"), 1)
                                state["fresh"] = False
                        return last

                    def turn(dst, src, rows):
                        return pe.transpose(dst, src, ident[0:rows, 0:rows])

                    def turn_narrow(dst, src, rows):
                        return pe.matmul(dst, src, ident[0:rows, 0:rows], start=True, stop=True)

                    def feature_major(src, chunks=DC):
                        for c in range(chunks):
                            b = aux.fill()
                            for t, (t0, rows) in enumerate(TILES):
                                last = turn(ps[:, b, t0:t0 + rows], src(t)[0:rows, :].rearrange("p (q c) -> p c q", c=chunks)[:, c, :], rows)
                            aux.filled(last)

                    pe.wait_ge(sem("vec_loads"), 48)
                    b = aux.fill()
                    aux.filled(turn(ps[:, b, 0:VEC_ROWS], ssd("vrows")[0:VEC_ROWS, :], VEC_ROWS))
                    pe.wait_ge(sem("h_ready"), 1)
                    feature_major(lambda t: h[:, t, :])
                    aux.all_emptied()

                    with pe.Fori(0, MAIN_BLOCKS // 2) as i:
                        wide.enter(i, 4)
                        for k in range(2):
                            state["n"] = k
                            w = next_block(DC, BLOCK, base=i * 16)
                            for m in range(2):
                                b = wide.fill()
                                wide.filled(product(ps[:, b, 0:TOKENS], lambda c: w[:, c, m * P:(m + 1) * P], lambda c: ht[:, c, :], DC))
                    wide.leave(MAIN_BLOCKS // 2)
                    state["n"] = MAIN_BLOCKS
                    marks["main"] = wide.n
                    for first, cols in TAIL:
                        w = next_block(DC, cols)
                        for t0, rows in TILES:
                            b = wide.fill()
                            wide.filled(product(ps[0:rows, b, 0:cols], lambda c: ht[:, c, t0:t0 + rows], lambda c: w[:, c, :], DC))
                    marks["tail"] = wide.n

                    pe.wait_ge(sem("cstate_load"), 16)
                    b = aux.fill()
                    for c in range(CC):
                        last = turn(ps[:, b, c * 24:c * 24 + 24], ssd("cstate")[0:24, c * P:(c + 1) * P], 24)
                    aux.filled(last)
                    aux.all_emptied()
                    pe.wait_ge(sem("wide_free"), 4 + marks["main"])
                    pe.wait_ge(sem("newest_ready"), 1)
                    for q in range(3):
                        b = aux.fill()
                        for c in range(4 * q, 4 * q + 4):
                            last = turn(ps[0:11, b, (c % 4) * P:(c % 4 + 1) * P], newest[:, c, :], P)
                        aux.filled(last)
                    pe.wait_ge(sem("conv_ready"), 1)
                    for t, (t0, rows) in enumerate(TILES):
                        for q in range(2):
                            b = aux.fill()
                            for c in range(4 * q, 4 * q + 4):
                                src = conv[:, c, t0:t0 + rows] if t < 2 else xsamp[:, c, :]
                                last = turn(ps[0:rows, b, (c % 4) * P:(c % 4 + 1) * P], src, P)
                            aux.filled(last)
                    b = aux.fill()
                    for t in range(2):
                        for g in range(GROUPS):
                            last = turn(ps[:, b, (2 * t + g) * P:(2 * t + g + 1) * P], conv[:, DC + g, t * P:(t + 1) * P], P)
                    aux.filled(last)
                    b = aux.fill()
                    for c in range(4):
                        last = turn(ps[0:SAMPLES, b, c * P:(c + 1) * P], xsamp[:, DC + c, :], P)
                    aux.filled(last)
                    pe.wait_ge(sem("z_ready"), 1)
                    for t, (t0, rows) in enumerate(TILES):
                        for q in range(2):
                            b = aux.fill()
                            for c in range(4 * q, 4 * q + 4):
                                last = turn(ps[0:rows, b, (c % 4) * P:(c % 4 + 1) * P], zt[:, c, t0:t0 + rows], P)
                            aux.filled(last)
                    b = aux.fill()
                    for t in range(2):
                        for g in range(GROUPS):
                            last = pe.matmul(ps[:, b, (2 * t + g) * P:(2 * t + g + 1) * P], conv[:, DC + g, t * P:(t + 1) * P],
                                             conv[:, DC + GROUPS + g, t * P:(t + 1) * P], start=True, stop=True)
                    aux.filled(last)
                    pe.wait_ge(sem("dta_ready"), 1)
                    b = aux.fill()
                    for t in range(2):
                        pe.matmul(ps[:, b, 32 * t:32 * t + 16], triu, dta[:, t, :], start=True, stop=True)
                        last = pe.matmul(ps[:, b, 32 * t + 16:32 * t + 32], ones, dta[:, t, :], start=True, stop=True)
                    aux.filled(last)
                    pe.wait_ge(sem("xde_ready"), 1)
                    for g in range(GROUPS):
                        b = aux.fill()
                        aux.filled(pe.matmul(ps[:, b, :], bt[:, 0, g * P:(g + 1) * P], xde[:, g * 512:(g + 1) * 512], start=True, stop=True))
                    pe.wait_ge(sem("xdf_ready"), 1)
                    for q in range(2):
                        b = aux.fill()
                        for c in range(4 * q, 4 * q + 4):
                            g = c // 4
                            for t in range(2):
                                last = pe.matmul(ps[:, b, (c % 4) * P:(c % 4 + 1) * P], xdf[:, t, c * P:(c + 1) * P], bt[:, t, g * P:(g + 1) * P],
                                                 start=t == 0, stop=t == 1)
                        aux.filled(last)
                    for t in range(2):
                        for q in range(4):
                            b = wide.fill()
                            pe.matmul(ps[:, b, :].rearrange("p (k l) -> p k l", k=4), ident, bc(neg, 1, 4), start=True, stop=False, skip_group_check=True)
                            for k in range(4):
                                hh = 4 * q + k
                                last = pe.matmul(ps[:, b, k * P:(k + 1) * P], dta[:, t, hh:hh + 1].to_broadcast([P, P]), triu,
                                                 start=False, stop=k == 3, skip_group_check=True)
                            wide.filled(last)
                        for g in range(GROUPS):
                            pe.wait_ge(sem("mix_ready"), 2 * t + g + 1)
                            b = aux.fill()
                            for e in range(8):
                                hh = 8 * g + e
                                last = pe.matmul(ps[:, b, e * 64:(e + 1) * 64], el[:, hh, :], xdt[:, t, hh * 64:(hh + 1) * 64], start=True, stop=True)
                            aux.filled(last)
                            if t == 1:
                                b = aux.fill()
                                aux.filled(pe.matmul(ps[:, b, :], conv[:, DC + GROUPS + g, P:2 * P], hpt[:, g, :], start=True, stop=True))
                        if t == 0:
                            marks["ydiag0"] = aux.n
                    marks["scan_wide"] = wide.n
                    pe.wait_ge(sem("da_ready"), 1)
                    b = aux.fill()
                    pe.matmul(ps[0:HEADS, b, 0:8], dt[0:SAMPLES, 2, :], ident[0:SAMPLES, 0:SAMPLES], start=True, stop=True)
                    aux.filled(pe.matmul(ps[0:HEADS, b, 8:16], eend[0:SAMPLES, 0, :], ident[0:SAMPLES, 0:SAMPLES], start=True, stop=True))
                    aux.all_emptied()
                    b = aux.fill()
                    for hh in range(HEADS):
                        c, lo = hh // 2, 64 * (hh % 2)
                        last = pe.matmul(ps[lo:lo + 64, b, c * 16:(c + 1) * 16], ident[0:HEADS, hh:hh + 1].to_broadcast([HEADS, 64]),
                                         dtt[0:HEADS, 0:16], start=True, stop=True)
                    aux.filled(last)
                    for s in range(SAMPLES):
                        b = aux.fill()
                        aux.filled(pe.matmul(ps[:, b, :], ident[0:SAMPLES, s:s + 1].to_broadcast([SAMPLES, P]), bcs[0:SAMPLES, :], start=True, stop=True))
                    pe.wait_ge(sem("ys_ready"), 1)
                    for q in range(2):
                        b = aux.fill()
                        for c in range(4 * q, 4 * q + 4):
                            last = turn(ps[0:SAMPLES, b, (c % 4) * P:(c % 4 + 1) * P], ysm3[:, c, :], P)
                        aux.filled(last)
                    pe.wait_ge(sem("y_ready"), 1)
                    feature_major(lambda t: y[:, t, :])
                    aux.all_emptied()
                    for k in range(4):
                        w = next_block(DC, BLOCK)
                        for m in range(2):
                            b = aux.fill()
                            aux.filled(product(ps[:, b, 0:TOKENS], lambda c: w[:, c, m * P:(m + 1) * P], lambda c: yt[:, c, :], DC))
                    aux.all_emptied()
                    pe.nop().then_inc(sem("scan_done"), 1)

                    pe.wait_ge(sem("cq_ready"), 1)
                    feature_major(lambda t: tok[:, t, T_CQ:T_CKV], chunks=3)
                    pe.wait_ge(sem("lat_ready"), 1)
                    for c in range(2):
                        b = aux.fill()
                        for t, (t0, rows) in enumerate(TILES):
                            last = turn(ps[:, b, t0:t0 + rows], lat[0:rows, t, c * P:(c + 1) * P], rows)
                        aux.filled(last)
                    b = aux.fill()
                    for t, (t0, rows) in enumerate(TILES):
                        last = turn_narrow(ps[0:ROPE, b, t0:t0 + rows], kpe[0:rows, t, :], rows)
                    aux.filled(last)
                    pe.wait_ge(sem("wkv_load"), 16)
                    for q in range(4):
                        b = aux.fill()
                        for k in range(2):
                            for c in range(2):
                                hh = 2 * q + k
                                last = turn(ps[:, b, (2 * k + c) * P:(2 * k + c + 1) * P], wkv[:, c, hh * P:(hh + 1) * P], P)
                        aux.filled(last)
                    aux.all_emptied()
                    pe.wait_ge(sem("wqb_load"), 16)
                    for hh in range(A_HEADS):
                        b = wide.fill()
                        wide.filled(product(ps[0:NOPE, b, 0:TOKENS], lambda c: wqb[:, c, hh * 96:hh * 96 + NOPE], lambda c: cqt[:, c, :], 3))
                    for t0, rows in TILES:
                        b = wide.fill()
                        wide.filled(product(ps[0:rows, b, 0:256].rearrange("p (h k) -> p h k", h=A_HEADS), lambda c: cqt[:, c, t0:t0 + rows],
                                            lambda c: wqb[:, c, :].rearrange("p (h k) -> p h k", h=A_HEADS)[:, :, NOPE:96], 3))
                    marks["q"] = wide.n
                    wide.all_emptied()
                    for c in range(2):
                        for hh in range(A_HEADS):
                            b = wide.fill()
                            wide.filled(pe.matmul(ps[:, b, 0:TOKENS], wkt[0:NOPE, hh, c * P:(c + 1) * P], qnt[0:NOPE, hh, :], start=True, stop=True))
                    pe.wait_ge(sem("qpe_ready"), 1)
                    for hh in range(A_HEADS):
                        b = aux.fill()
                        for t, (t0, rows) in enumerate(TILES):
                            last = turn_narrow(ps[0:ROPE, b, t0:t0 + rows], qpe[0:rows, t, hh, :], rows)
                        aux.filled(last)
                    b = aux.fill()
                    for hh in range(A_HEADS):
                        last = pe.matmul(ps[:, b, hh * 8:hh * 8 + 8], qrep[0:SAMPLES, hh, :, :].rearrange("p q k -> p (q k)"), ident[0:SAMPLES, 0:SAMPLES], start=True, stop=True)
                    aux.filled(last)
                    wide.all_emptied()
                    aux.all_emptied()
                    pe.nop().then_inc(sem("queries_done"), 1)

                    for t in range(2):
                        width = P * (t + 1)
                        for q in range(4):
                            b = aux.fill()
                            for k in range(2):
                                hh = 2 * q + k
                                dst = ps[:, b, k * 256:k * 256 + width]
                                for c in range(2):
                                    pe.matmul(dst, ql[:, c, hh, t * P:(t + 1) * P], latt[:, c, 0:width], start=c == 0, stop=False)
                                last = pe.matmul(dst, qpt[0:ROPE, hh, t * P:(t + 1) * P], kpet[0:ROPE, 0:width], start=False, stop=True)
                            aux.filled(last)
                        pe.wait_ge(sem("probs_ready"), t + 1)
                        for k in range(t + 1):
                            for q in range(2):
                                b = aux.fill()
                                for hh in range(4 * q, 4 * q + 4):
                                    last = turn(ps[:, b, (hh % 4) * P:(hh % 4 + 1) * P], sc[:, hh, k * P:(k + 1) * P], P)
                                aux.filled(last)
                        aux.all_emptied()
                        for c in range(2):
                            for q in range(2):
                                b = aux.fill()
                                for k in range(t + 1):
                                    last = pe.matmul(ps[:, b, :], lat[:, k, c * P:(c + 1) * P], pt[:, k, 4 * q:4 * q + 4, :], start=k == 0, stop=k == t)
                                aux.filled(last)
                    aux.all_emptied()

                    marks["att"] = aux.n
                    with pe.Fori(0, SAMPLES // 2) as i:
                        aux.enter(i, 28)
                        for s in range(2):
                            pe.wait_ge(sem(f"pages{s}_loads"), i * 32 + 32)
                            for c in range(2):
                                for q in range(4):
                                    b = aux.fill()
                                    for j in range(4 * q, 4 * q + 4):
                                        last = turn(ps[:, b, (j % 4) * P:(j % 4 + 1) * P], ck[:, s, j, c * P:(c + 1) * P], P)
                                    aux.filled(last)
                            b = aux.fill()
                            for q in range(4):
                                last = turn(ps[:, b, q * P:(q + 1) * P], cr[:, s, 4 * q:4 * q + 4, :].rearrange("p j r -> p (j r)"), P)
                            aux.filled(last)
                            aux.all_emptied()
                            pe.wait_ge(sem("qb_ready"), i * 2 + s + 1)
                            b = aux.fill()
                            for j in range(PIECE):
                                dst = ps[:, b, j * 8:j * 8 + 8]
                                for c in range(2):
                                    pe.matmul(dst, kt[:, c, j, :], qb[:, c, :], start=c == 0, stop=False)
                                pe.matmul(dst, krt[:, j // 4, :], qpb[:, j % 4, :], start=False, stop=True)
                            dst = ps[0:SAMPLES, b, 128:136]
                            for c in range(2):
                                pe.matmul(dst, latt[:, c, SEQ:TOKENS], qb[:, c, :], start=c == 0, stop=False)
                            aux.filled(pe.matmul(dst, kpet[0:ROPE, SEQ:TOKENS], qpb[0:ROPE, 0, :], start=False, stop=True))
                            pe.wait_ge(sem("max_ready"), i * 2 + s + 1)
                            b = aux.fill()
                            aux.filled(pe.matmul(ps[0:A_HEADS, b, 0:P], dmx, ident, start=True, stop=True))
                            pe.wait_ge(sem("max_diag_ready"), i * 2 + s + 1)
                            b = aux.fill()
                            aux.filled(pe.matmul(ps[:, b, 0:8], ones[0:A_HEADS, :], dm8[0:A_HEADS, :], start=True, stop=True))
                            pe.wait_ge(sem("sum_ready"), i * 2 + s + 1)
                            b = aux.fill()
                            aux.filled(pe.matmul(ps[:, b, 0:8], ones, dsum, start=True, stop=True))
                            b = aux.fill()
                            for c in range(2):
                                dst = ps[:, b, c * 8:c * 8 + 8]
                                for j in range(PIECE):
                                    pe.matmul(dst, ck[:, s, j, c * P:(c + 1) * P], sexp[:, j, :], start=j == 0, stop=False)
                                last = pe.matmul(dst, lat[0:SAMPLES, 2, c * P:(c + 1) * P], sexp[0:SAMPLES, 16, :], start=False, stop=True)
                            aux.filled(last)
                    aux.leave(SAMPLES // 2)
                    aux.all_emptied()

                    for q in range(4):
                        b = aux.fill()
                        for k in range(2):
                            hh = 2 * q + k
                            for c in range(2):
                                last = pe.matmul(ps[k * 64:k * 64 + 64, b, 0:TOKENS], wkv[:, c, hh * P + NOPE:(hh + 1) * P], ol[:, c, hh, :],
                                                 start=c == 0, stop=c == 1)
                        aux.filled(last)
                    aux.all_emptied()
                    for k in range(2):
                        w = next_block(4, 2 * BLOCK)
                        for m in range(4):
                            b = aux.fill()
                            aux.filled(product(ps[:, b, 0:TOKENS], lambda c: w[:, c, m * P:(m + 1) * P], lambda c: ot[:, c, :], 4))
                    pe.wait_ge(sem("mixed"), 1)
                    for k in range(4):
                        w = next_block(DC, BLOCK)
                        for t0, rows in TILES:
                            b = aux.fill()
                            aux.filled(product(ps[0:rows, b, 0:BLOCK], lambda c: gate[:, c, t0:t0 + rows], lambda c: w[:, c, :], DC))
                    aux.all_emptied()
                    pe.nop().then_inc(sem("attention_done"), 1)

                    pe.wait_ge(sem("keys_load"), 16)
                    for q in range(4):
                        b = aux.fill()
                        for k in range(4 * q, 4 * q + 4):
                            last = turn(ps[:, b, (k % 4) * P:(k % 4 + 1) * P], keys[:, k, :], P)
                        aux.filled(last)
                    pe.wait_ge(sem("ph_ready"), 1)
                    feature_major(lambda t: h[:, t, :])
                    for half in range(2):
                        b = aux.fill()
                        aux.filled(pe.matmul(ps[0:64, b, :], cst("rep")[0:SAMPLES, :], h[0:SAMPLES, 2, half * 512:(half + 1) * 512], start=True, stop=True))
                    aux.all_emptied()
                    first = state["n"]
                    marks["wq_block"] = first
                    with pe.Fori(0, 4) as i:
                        wide.enter(i, 4)
                        for k in range(2):
                            state["n"] = first + k
                            w = next_block(DC, BLOCK, base=i * 16)
                            for m in range(2):
                                b = wide.fill()
                                wide.filled(product(ps[:, b, 0:TOKENS], lambda c: w[:, c, m * P:(m + 1) * P], lambda c: ht[:, c, :], DC))
                    wide.leave(4)
                    marks["wq"] = wide.n
                    wide.all_emptied()
                    for t in range(2):
                        for q in range(4):
                            b = wide.fill()
                            for k in range(4 * q, 4 * q + 4):
                                last = pe.matmul(ps[:, b, (k % 4) * P:(k % 4 + 1) * P], gate[:, k, t * P:(t + 1) * P], keyst[:, k, :], start=True, stop=True)
                            wide.filled(last)
                    pe.wait_ge(sem("qz_ready"), 1)
                    b = wide.fill()
                    for half in range(2):
                        for hh in range(P_HEADS):
                            last = pe.matmul(ps[0:64, b, half * P:(half + 1) * P], qz[:, half, hh * 64:(hh + 1) * 64], keyst[:, 2 * hh + half, :],
                                             start=hh == 0, stop=hh == P_HEADS - 1)
                    wide.filled(last)
                    for t in range(3):
                        rows, outs = (P, P) if t < 2 else (64, SAMPLES)
                        banks = [aux.fill()]
                        aux.n += 1
                        banks.append(aux.fill())
                        aux.n -= 1
                        pe.wait_ge(sem("zero_ready"), 1)
                        for half in range(2):
                            pe.matmul(ps[0:outs, banks[half], :], zero[0:rows, 0:outs], consts[0:rows, 0:512], start=True, stop=False, skip_group_check=True)
                        for i in turns_of(pe, t):
                            for n, k in enumerate(PE_SLOTS):
                                pe.wait_ge(sem("diag_ready"), i * len(PE_SLOTS) + (PE_USES[t] + n + 1))
                                pe.wait_ge(sem(f"slot{k}_loads"), i * 16 + 16 * (V_USES[t] + 1))
                                for half in range(2):
                                    last = pe.matmul(ps[0:outs, banks[half], :], diag[0:rows, k, 0:outs], ring[0:rows, k, half * 512:(half + 1) * 512],
                                                     start=False, stop=False, skip_group_check=True)
                                last.then_inc(sem("tensor_slots_used"), 1)
                        pe.wait_ge(sem("acc_ready"), t + 1)
                        close = ident if t < 2 else cst("mod8")
                        for half in range(2):
                            aux.filled(pe.matmul(ps[0:outs, banks[half], :], close[0:rows, 0:outs], acc[0:rows, half * 512:(half + 1) * 512],
                                                 start=False, stop=True, skip_group_check=True))

                @block.vector
                def _(dve):
                    aux = Ring(dve, sem("aux_full"), sem("aux_free"), (4, 5, 6, 7))
                    own = Own(dve, sem("vector_steps"))
                    then = own.then
                    dve.nop().then_inc(sem("aux_free"), 4)
                    dve.nop().then_inc(sem("rows_dotted"), RING)
                    dve.nop().then_inc(sem("vector_slots_used"), len(VECTOR_SLOTS))

                    def copy_out(dst, cols, rows=P):
                        b = aux.read()
                        aux.emptied(dve.tensor_copy(dst, ps[0:rows, b, 0:cols]))

                    def copy4(dst, rows=P):
                        copy_out(dst, 512, rows)

                    def rstd(total, mean, root, inverse, width, square_sem, root_sem):
                        dve.wait_ge(sem(square_sem), 1)
                        dve.tensor_scalar(mean, total, 1.0 / width, EPS, ALU.mult, ALU.add).then_inc(sem(square_sem + "_mean"), 1)
                        dve.wait_ge(sem(root_sem), 1)
                        then(dve.reciprocal(inverse, root))

                    then(dve.memset(pad[:, :, 0:PAD], 0.0))
                    dve.memset(xt[:, 2, :], 0.0)
                    then(dve.memset(y[:, 2, :], 0.0))
                    b = aux.read()
                    aux.emptied(dve.tensor_copy(vt[:, :], ps[:, b, 0:VEC_ROWS]), wait=True)
                    dve.nop().then_inc(sem("vt_ready"), 1)
                    rstd(ss, ss, rt, rs, D_MODEL, "x_squares", "x_root")
                    dve.wait_ge(sem("nrow_load"), 16)
                    for t in range(3):
                        last = dve.scalar_tensor_tensor(out=h[:, t, :], in0=x[:, t, :], scalar=rs[:, t:t + 1], in1=nrow[:, :], op0=ALU.mult, op1=ALU.mult)
                    last.then_inc(sem("h_ready"), 1)
                    for c in range(DC):
                        copy_out(ht[:, c, :], TOKENS)
                    dve.memset(tok[:, 2, :], 0.0).then_inc(sem("tok_zeroed"), 1)
                    dve.nop().then_inc(sem("nrow_used"), 1)

                    dve.wait_ge(sem("z_sigmoid"), 1)
                    dve.tensor_tensor(zt, zt, zsig, ALU.mult).then_inc(sem("z_ready"), 1)
                    b = aux.read()
                    aux.emptied(dve.tensor_copy(pad_s[:, :, :, 0:PAD], ps[:, b, 0:24 * CC].rearrange("p (c b k) -> p c b k", c=CC, b=SAMPLES)), wait=True)
                    dve.wait_ge(sem("wide_free"), 4 + marks["main"])
                    dve.tensor_copy(newest[:, :, 0:PAD], pad[:, :, SEQ:SEQ + PAD])
                    dve.tensor_copy(newest[:, :, PAD:], pad_s[:, :, :, PAD]).then_inc(sem("newest_ready"), 1)
                    with dve.Fori(0, CC) as c:
                        own.enter(c, CONV)
                        dst = conv[:, bass.ds(c, 1), 0:CONV_OUT]
                        then(dve.tensor_scalar(dst, pad[:, bass.ds(c, 1), 0:CONV_OUT], vt[:, bass.ds(c, 1)], vt[:, bass.ds(c + CONV * CC, 1)], ALU.mult, ALU.add))
                        for k in range(1, CONV):
                            then(dve.scalar_tensor_tensor(out=dst, in0=pad[:, bass.ds(c, 1), k:k + CONV_OUT], scalar=vt[:, bass.ds(c + k * CC, 1)],
                                                          in1=dst, op0=ALU.mult, op1=ALU.add))
                    own.leave(CC)
                    dve.nop().then_inc(sem("conv_raw"), 1)
                    dve.wait_ge(sem("wide_free"), 4 + marks["tail"])
                    dve.wait_ge(sem("head_loads"), 96)
                    then(dve.tensor_tensor(dtu, tok[:, :, 0:HEADS], bc(hd[:, 0:HEADS], 1, 3), ALU.add))
                    dve.scalar_tensor_tensor(out=dte, in0=dtu, scalar=-1.0, in1=dtu, op0=ALU.mult, op1=ALU.max).then_inc(sem("abs_ready"), 1)
                    dve.wait_ge(sem("dt_exp"), 1)
                    dve.tensor_scalar(dtw, dte, 1.0, None, ALU.add).then_inc(sem("dtw_ready"), 1)
                    dve.wait_ge(sem("dtw_ready"), 1)
                    then(dve.tensor_scalar(dtd, dtw, 1.0, None, ALU.subtract))
                    then(dve.tensor_tensor(dtd, dte, dtd, ALU.subtract))
                    then(dve.reciprocal(dti, dtw))
                    then(dve.tensor_tensor(dtd, dtd, dti, ALU.mult))
                    dve.wait_ge(sem("dt_log"), 1)
                    then(dve.tensor_tensor(dtl, dtl, dtd, ALU.add))
                    then(dve.scalar_tensor_tensor(out=dt, in0=dtu, scalar=0.0, in1=dtl, op0=ALU.max, op1=ALU.add))
                    dve.scalar_tensor_tensor(out=dta, in0=dt, scalar=-1.0, in1=bc(hd[:, HEADS:2 * HEADS], 1, 3), op0=ALU.mult, op1=ALU.mult).then_inc(sem("dta_ready"), 1)
                    for q in range(3):
                        last = None
                        b = aux.read()
                        aux.emptied(dve.tensor_copy(rawt[0:11, q * 512:(q + 1) * 512], ps[0:11, b, :]), wait=True)
                    dve.nop().then_inc(sem("rawt_ready"), 1)
                    dve.wait_ge(sem("conv_sigmoid"), 1)
                    then(dve.tensor_tensor(conv[:, :, 0:CONV_OUT], conv[:, :, 0:CONV_OUT], sig[:, :, 0:CONV_OUT], ALU.mult))
                    dve.tensor_copy(xsamp, conv_s[:, :, :, 0]).then_inc(sem("conv_ready"), 1)
                    for t, (t0, rows) in enumerate(TILES):
                        for q in range(2):
                            copy4(xt[0:rows, t, q * 512:(q + 1) * 512], rows)
                    copy4(bt.rearrange("p t n -> p (t n)"))
                    copy4(bcs[0:SAMPLES, :], SAMPLES)
                    for t, (t0, rows) in enumerate(TILES):
                        for q in range(2):
                            copy4(h[0:rows, t, q * 512:(q + 1) * 512], rows)
                    copy4(cb.rearrange("p k l -> p (k l)"))
                    b = aux.read()
                    aux.emptied(dve.tensor_copy(acs[:, :], ps[:, b, 0:64]), wait=True)
                    then(dve.tensor_tensor(dec, a_cs[:, :, 1, :], a_cs[:, :, 0, :], ALU.subtract))
                    dve.tensor_scalar(nacs, a_cs[:, :, 0, :], -1.0, None, ALU.mult)
                    dve.tensor_tensor(decf[:, 0, :], dec[:, 0, :], a_cs[:, 1, 1, :], ALU.add)
                    dve.tensor_copy(decf[:, 1, :], dec[:, 1, :]).then_inc(sem("decays_raw"), 1)
                    dve.wait_ge(sem("rawt_stored"), 1)
                    heads = lambda ap: ap.rearrange("p (h k) -> p h k", h=HEADS)
                    for t in range(2):
                        then(dve.tensor_tensor(heads(xdt[:, t, :]), heads(xt[:, t, :]), bc(dt[:, t, :], 2, 64), ALU.mult))
                    dve.wait_ge(sem("decays_ready"), 1)
                    dve.tensor_tensor(heads(xde), heads(xdt[:, 0, :]), bc(dec[:, 0, :], 2, 64), ALU.mult).then_inc(sem("xde_ready"), 1)
                    for t in range(2):
                        last = dve.tensor_tensor(heads(xdf[:, t, :]), heads(xdt[:, t, :]), bc(decf[:, t, :], 2, 64), ALU.mult)
                    last.then_inc(sem("xdf_ready"), 1)
                    for g in range(GROUPS):
                        copy4(hpt[:, g, :])
                    for q in range(2):
                        b = aux.read()
                        aux.emptied(dve.tensor_copy(hs[:, q * 512:(q + 1) * 512], ps[:, b, :]), wait=True)
                    dve.nop().then_inc(sem("hs_ready"), 1)
                    for t in range(3):
                        then(dve.tensor_tensor(heads(y[:, t, :]), heads(xt[:, t, :]), bc(hd[:, 2 * HEADS:3 * HEADS], 2, 64), ALU.mult))
                    for t in range(2):
                        for g in range(GROUPS):
                            dve.wait_ge(sem("wide_free"), 4 + marks["tail"] + 4 * t + 2 * g + 2)
                            dve.tensor_tensor(el[:, 8 * g:8 * g + 8, :], el[:, 8 * g:8 * g + 8, :], bc(cb[:, 2 * t + g, :], 1, 8), ALU.mult).then_inc(sem("mix_ready"), 1)
                        for g in range(GROUPS):
                            yg = y[:, t, g * 512:(g + 1) * 512]
                            b = aux.read()
                            aux.emptied(dve.tensor_tensor(yg, yg, ps[:, b, :], ALU.add), wait=True)
                            if t == 1:
                                b = aux.read()
                                aux.emptied(dve.tensor_tensor(xt[:, 1, g * 512:(g + 1) * 512].rearrange("p (e k) -> p e k", e=8),
                                                              ps[:, b, :].rearrange("p (e k) -> p e k", e=8), bc(ea[:, 1, 8 * g:8 * g + 8], 2, 64), ALU.mult), wait=True)
                                then(dve.tensor_tensor(yg, yg, xt[:, 1, g * 512:(g + 1) * 512], ALU.add))
                    dve.nop().then_inc(sem("el_used"), 1)
                    b = aux.read()
                    aux.emptied(dve.tensor_copy(dtt[0:HEADS, 0:16], ps[0:HEADS, b, 0:16]))
                    b = aux.read()
                    aux.emptied(dve.tensor_copy(exs[:, :], ps[:, b, 0:DC * 16]), wait=True)
                    then(dve.tensor_tensor(dtx3, xsamp[:, 0:DC, :], exs4[:, :, 0, :], ALU.mult))
                    per_group = lambda ap: ap.rearrange("p (g c n) -> p g c n", g=GROUPS, c=4)
                    for s in range(SAMPLES):
                        b = aux.read()
                        bmat = bc(ps[:, b, 0:256].rearrange("p (g n) -> p g n", g=GROUPS), 2, 4)
                        cmat = bc(ps[:, b, 256:512].rearrange("p (g n) -> p g n", g=GROUPS), 2, 4)
                        new = stt[:, s % 2, :, :]
                        new4 = per_group(new.rearrange("p c n -> p (c n)"))
                        then(dve.tensor_tensor(per_group(stx), bmat, bc(dtx3[:, :, s].rearrange("p (g c) -> p g c", g=GROUPS), 3, P), ALU.mult))
                        dve.wait_ge(sem(f"state_load{s % 2}"), 16 * (s // 2 + 1))
                        then(dve.tensor_tensor(new, new, bc(exs4[:, :, 1, s], 2, P), ALU.mult))
                        stx3 = stx.rearrange("p (c n) -> p c n", c=DC)
                        dve.tensor_tensor(new, new, stx3, ALU.add).then_inc(sem("state_ready"), 1)
                        dve.wait_ge(sem("state_ready"), s + 1)
                        aux.emptied(dve.tensor_tensor(per_group(stx), new4, cmat, ALU.mult), wait=True)
                        dve.tensor_reduce(ysm3[:, :, s:s + 1], stx3, AX.X, ALU.add).then_inc(sem("state_used"), 1)
                        dve.wait_ge(sem("state_used"), s + 1)
                    dve.nop().then_inc(sem("ys_ready"), 1)
                    for q in range(2):
                        b = aux.read()
                        yg = y[0:SAMPLES, 2, q * 512:(q + 1) * 512]
                        aux.emptied(dve.tensor_tensor(yg, yg, ps[0:SAMPLES, b, :], ALU.add), wait=True)
                    dve.tensor_tensor(y, y, h, ALU.mult).then_inc(sem("y_gated"), 1)
                    rstd(ss6, ss6, rt6, rs6, D_MODEL // GROUPS, "y_squares", "y_root")
                    for t in range(3):
                        for g in range(GROUPS):
                            yg = y[:, t, g * 512:(g + 1) * 512]
                            last = dve.tensor_scalar(yg, yg, rs6[:, 2 * t + g:2 * t + g + 1], None, ALU.mult)
                    last.then_inc(sem("y_ready"), 1)
                    for c in range(DC):
                        b = aux.read()
                        aux.emptied(dve.tensor_scalar(yt[:, c, :], ps[:, b, 0:TOKENS], ssmn[:, c:c + 1], None, ALU.mult))
                    for m in range(DC):
                        b = aux.read()
                        aux.emptied(dve.tensor_tensor(gate[:, m, :], gate[:, m, :], ps[:, b, 0:TOKENS], ALU.mult))

                    dve.wait_ge(sem("lat_squares"), 1)
                    lsq, lrt, lrs = st[:, 27:33], st[:, 33:39], st[:, 39:45]
                    dve.tensor_scalar(lsq[:, 0:3], lsq[:, 0:3], 1.0 / Q_LORA, EPS, ALU.mult, ALU.add)
                    dve.tensor_scalar(lsq[:, 3:6], lsq[:, 3:6], 1.0 / KV_LORA, EPS, ALU.mult, ALU.add).then_inc(sem("lat_squares_mean"), 1)
                    dve.wait_ge(sem("lat_root"), 1)
                    then(dve.reciprocal(lrs, lrt))
                    for t in range(3):
                        last = dve.tensor_scalar(tok[:, t, T_CQ:T_CKV], tok[:, t, T_CQ:T_CKV], lrs[:, t:t + 1], None, ALU.mult)
                    last.then_inc(sem("cq_ready"), 1)
                    for t in range(3):
                        dve.scalar_tensor_tensor(out=lat[:, t, :], in0=tok[:, t, T_CKV:T_KR], scalar=lrs[:, 3 + t:4 + t], in1=kvn[:, :], op0=ALU.mult, op1=ALU.mult)
                    x1, x2 = tok[:, :, T_KR:T_KR + 16], tok[:, :, T_KR + 16:TAIL_W]
                    r1, r2, r3, r4 = (dtb[:, 48 * k:48 * k + 48].rearrange("p (t k) -> p t k", t=3) for k in range(2, 6))
                    dve.tensor_tensor(r1, x1, cos, ALU.mult)
                    dve.tensor_tensor(r2, x2, sin, ALU.mult)
                    dve.tensor_tensor(r3, x1, sin, ALU.mult)
                    then(dve.tensor_tensor(r4, x2, cos, ALU.mult))
                    dve.tensor_tensor(kpe[:, :, 0:16], r1, r2, ALU.subtract)
                    dve.tensor_tensor(kpe[:, :, 16:32], r3, r4, ALU.add).then_inc(sem("lat_ready"), 1)
                    for c in range(3):
                        b = aux.read()
                        aux.emptied(dve.tensor_scalar(cqt[:, c, :], ps[:, b, 0:TOKENS], qn[:, c:c + 1], None, ALU.mult))
                    for c in range(2):
                        copy_out(latt[:, c, :], TOKENS)
                    b = aux.read()
                    aux.emptied(dve.tensor_copy(kpet[0:ROPE, :], ps[0:ROPE, b, 0:TOKENS]))
                    for q in range(4):
                        b = aux.read()
                        aux.emptied(dve.tensor_copy(wkt[0:NOPE, 2 * q:2 * q + 2, :].rearrange("p h r -> p (h r)"), ps[0:NOPE, b, :]))
                    dve.wait_ge(sem("wide_free"), 4 + marks["q"])
                    q1, q2 = qr[:, :, :, 0:16], qr[:, :, :, 16:32]
                    cosq, sinq = bc(cos, 2, A_HEADS), bc(sin, 2, A_HEADS)
                    for t in range(3):
                        rows = TILES[t][1]
                        dve.tensor_tensor(rtmp[0:rows, 0, t], q1[0:rows, t], cosq[0:rows, t], ALU.mult)
                        dve.tensor_tensor(rtmp[0:rows, 1, t], q2[0:rows, t], sinq[0:rows, t], ALU.mult)
                        dve.tensor_tensor(rtmp[0:rows, 2, t], q1[0:rows, t], sinq[0:rows, t], ALU.mult)
                        then(dve.tensor_tensor(rtmp[0:rows, 3, t], q2[0:rows, t], cosq[0:rows, t], ALU.mult))
                        dve.tensor_tensor(qpe[0:rows, t, :, 0:16], rtmp[0:rows, 0, t], rtmp[0:rows, 1, t], ALU.subtract)
                        last = dve.tensor_tensor(qpe[0:rows, t, :, 16:32], rtmp[0:rows, 2, t], rtmp[0:rows, 3, t], ALU.add)
                    then(last)
                    dve.tensor_copy(qrep[0:SAMPLES, :, :, :], bc(qpe[0:SAMPLES, 2, :, :], 2, 4)).then_inc(sem("qpe_ready"), 1)
                    for hh in range(A_HEADS):
                        b = aux.read()
                        aux.emptied(dve.tensor_copy(qpt[0:ROPE, hh, :], ps[0:ROPE, b, 0:TOKENS]))
                    b = aux.read()
                    for s in range(SAMPLES):
                        last = dve.tensor_tensor(qpad[:, s, :, :], bc(ps[:, b, 0:64].rearrange("p (h b) -> p b h", b=SAMPLES)[:, s, :], 1, 4),
                                                 bc(cst("quarter"), 2, A_HEADS), ALU.mult)
                    aux.emptied(last)

                    for t in range(2):
                        width = P * (t + 1)
                        for q in range(4):
                            b = aux.read()
                            src = ps[:, b, :].rearrange("p (k t) -> p k t", k=2)
                            if t == 1:
                                dve.tensor_copy(sc[:, 2 * q:2 * q + 2, 0:P], src[:, :, 0:P])
                            aux.emptied(dve.tensor_tensor(sc[:, 2 * q:2 * q + 2, t * P:width], src[:, :, t * P:width], bc(cst("causal"), 1, 2), ALU.add), wait=True)
                        scores = sc[:, :, 0:width]
                        then(dve.tensor_reduce(amax, scores, AX.X, ALU.max))
                        dve.tensor_scalar(anm, amax, -SCALE, None, ALU.mult).then_inc(sem("scores_max"), 1)
                        dve.wait_ge(sem("scores_exp"), t + 1)
                        then(dve.reciprocal(ainv, asum))
                        dve.tensor_tensor(scores, scores, bc(ainv, 2, width), ALU.mult).then_inc(sem("probs_ready"), 1)
                        for k in range(t + 1):
                            for q in range(2):
                                copy4(pt[:, k, 4 * q:4 * q + 4, :].rearrange("p h t -> p (h t)"))
                        for c in range(2):
                            for q in range(2):
                                b = aux.read()
                                aux.emptied(dve.tensor_copy(ol[:, c, 4 * q:4 * q + 4, t * P:(t + 1) * P], ps[:, b, :].rearrange("p (h t) -> p h t", h=4)))

                    dve.memset(sraw[:, 16, :], NEG)
                    then(dve.memset(sraw[:, 0:16, :], 0.0))
                    with dve.Fori(0, SAMPLES // 2) as i:
                        aux.enter(i, 28)
                        own.enter(i, 6)
                        for s in range(2):
                            for c in range(2):
                                for q in range(4):
                                    copy4(kt[:, c, 4 * q:4 * q + 4, :].rearrange("p j t -> p (j t)"))
                            copy4(krt.rearrange("p q t -> p (q t)"))
                            at = i * 2 + (SEQ + s)
                            then(dve.tensor_copy(qb, ql[:, :, :, bass.ds(at, 1)].rearrange("p c h o -> p c (h o)")))
                            dve.tensor_copy(qpb, qpad[:, bass.ds(i * 2 + s, 1), :, :].rearrange("p o q h -> p (o q) h")).then_inc(sem("qb_ready"), 1)
                            b = aux.read()
                            then(dve.tensor_copy(sraw[:, 0:16, :].rearrange("p j h -> p (j h)"), ps[:, b, 0:128]))
                            aux.emptied(dve.tensor_scalar(sraw[0:SAMPLES, 16, :], ps[0:SAMPLES, b, 128:136], cst("newmask")[0:SAMPLES, bass.ds(i * 2 + s, 1)], None, ALU.add), wait=True)
                            dve.tensor_reduce(dmx, sraw.rearrange("p j h -> p h j"), AX.X, ALU.max).then_inc(sem("max_ready"), 1)
                            b = aux.read()
                            aux.emptied(dve.tensor_reduce(dm1[0:A_HEADS, :], ps[0:A_HEADS, b, 0:P], AX.X, ALU.max), wait=True)
                            dve.tensor_scalar(dm8[0:A_HEADS, :], ident[0:A_HEADS, 0:A_HEADS], dm1[0:A_HEADS, :], None, ALU.mult).then_inc(sem("max_diag_ready"), 1)
                            b = aux.read()
                            aux.emptied(dve.tensor_copy(dall, ps[:, b, 0:8]), wait=True)
                            then(dve.tensor_tensor(sexp, sraw, bc(dall, 1, 17), ALU.subtract))
                            dve.nop().then_inc(sem("shifted"), 1)
                            dve.wait_ge(sem("sample_exp"), i * 2 + s + 1)
                            dve.tensor_reduce(dsum, sexp.rearrange("p j h -> p h j"), AX.X, ALU.add).then_inc(sem("sum_ready"), 1)
                            b = aux.read()
                            aux.emptied(dve.reciprocal(dinv, ps[:, b, 0:8]), wait=True)
                            b = aux.read()
                            aux.emptied(dve.tensor_tensor(ol[:, :, :, bass.ds(at, 1)].rearrange("p c h o -> p c (h o)"), ps[:, b, 0:16].rearrange("p (c h) -> p c h", c=2),
                                                          bc(dinv, 1, 2), ALU.mult), wait=True)
                    own.leave(SAMPLES // 2)
                    aux.leave(SAMPLES // 2)

                    for q in range(4):
                        copy_out(ot[:, q, :], TOKENS)
                    for m in range(DC):
                        b = aux.read()
                        aux.emptied(dve.tensor_tensor(gate[:, DC + m, :], gate[:, DC + m, :], ps[:, b, 0:TOKENS], ALU.mult), wait=True)
                    dve.tensor_tensor(gate[:, 0:DC, :], gate[:, 0:DC, :], gate[:, DC:, :], ALU.add).then_inc(sem("mixed"), 1)
                    for k in range(4):
                        for t, (t0, rows) in enumerate(TILES):
                            b = aux.read()
                            xs = x[0:rows, t, k * BLOCK:(k + 1) * BLOCK]
                            aux.emptied(dve.tensor_tensor(xs, xs, ps[0:rows, b, 0:BLOCK], ALU.add))

                    dve.wait_ge(sem("aux_free"), 4 + aux.n)
                    dve.nop().then_inc(sem("x_mixed"), 1)
                    dve.wait_ge(sem("attention_done"), 1)
                    dve.memset(zero, 0.0).then_inc(sem("zero_ready"), 1)
                    then(dve.memset(qz.rearrange("p s c -> p (s c)"), 0.0))
                    for q in range(4):
                        copy4(keyst[:, 4 * q:4 * q + 4, :].rearrange("p k d -> p (k d)"))
                    rstd(st[:, 45:48], st[:, 45:48], st[:, 48:51], st[:, 51:54], D_MODEL, "px_squares", "px_root")
                    dve.wait_ge(sem("ffn_row_load"), 16)
                    for t in range(3):
                        last = dve.scalar_tensor_tensor(out=h[:, t, :], in0=x[:, t, :], scalar=st[:, 51 + t:52 + t], in1=nrow[:, :], op0=ALU.mult, op1=ALU.mult)
                    last.then_inc(sem("ph_ready"), 1)
                    for c in range(DC):
                        copy_out(ht[:, c, :], TOKENS)
                    for half in range(2):
                        copy_out(hr[0:64, half * 512:(half + 1) * 512], 512, 64)
                    dve.wait_ge(sem("wide_free"), 4 + marks["wq"])
                    for half in range(2):
                        last = dve.tensor_copy(qz[:, half, :].rearrange("p (h r) -> p h r", r=72)[:, :, 0:SAMPLES],
                                               gate[:, :, SEQ:TOKENS].rearrange("p (h s) t -> p s h t", s=2)[:, half, :, :])
                    last.then_inc(sem("qz_ready"), 1)

                    def sixteen(best, where, values):
                        for k in range(2):
                            then(dve.max(best[:, 8 * k:8 * k + 8], values))
                            then(dve.max_index(where[:, 8 * k:8 * k + 8], best[:, 8 * k:8 * k + 8], values))
                            if k == 0:
                                then(dve.match_replace(values, best[:, 0:8], values, -3e38))

                    for t in range(3):
                        rows, nh = (P, P_HEADS) if t < 2 else (64, 1)
                        dve.wait_ge(sem("wide_free"), 4 + marks["wq"] + (4 * (t + 1) if t < 2 else 9))
                        for k in range(2 * nh):
                            sixteen(top[0:rows, 16 * k:16 * k + 16], topi[0:rows, 16 * k:16 * k + 16], keysc[0:rows, k, :])
                        dve.nop().then_inc(sem("scores_used"), 1)
                        n16 = nh * TOPK
                        then(dve.tensor_copy(topf[0:rows, 0:2 * n16], topi[0:rows, 0:2 * n16]))
                        pair = lambda ap: ap[0:rows, 0:2 * n16].rearrange("p (h s k) -> p s h k", s=2, k=TOPK)
                        grid = lambda ap: ap[0:rows, 0:n16 * TOPK].rearrange("p (h i j) -> p h i j", h=nh, i=TOPK)
                        then(dve.tensor_tensor(grid(cand), bc(pair(top)[:, 0], 3, TOPK), bc(pair(top)[:, 1], 2, TOPK), ALU.add))
                        for k in range(nh):
                            sixteen(ctop[0:rows, 16 * k:16 * k + 16], ctopi[0:rows, 16 * k:16 * k + 16], cand[0:rows, 256 * k:256 * k + 256])
                        best = ctop[0:rows, 0:n16].rearrange("p (h k) -> p h k", h=nh)
                        w = wgt[0:rows, t, 0:n16].rearrange("p (h k) -> p h k", h=nh)
                        dve.tensor_tensor(w, best, bc(best[:, :, 0], 2, TOPK), ALU.subtract).then_inc(sem("experts_shifted"), 1)
                        then(dve.tensor_scalar(i1[0:rows, 0:n16], ctopi[0:rows, 0:n16], 4, None, ALU.logical_shift_right))
                        then(dve.tensor_scalar(i2[0:rows, 0:n16], ctopi[0:rows, 0:n16], 15, None, ALU.bitwise_and))
                        then(dve.tensor_copy(sel1[0:rows, 0:n16], i1[0:rows, 0:n16]))
                        then(dve.tensor_copy(sel2[0:rows, 0:n16], i2[0:rows, 0:n16]))
                        for n, (sel, where) in enumerate(((sel1, hot), (sel2, hot2))):
                            flat = sel[0:rows, 0:n16]
                            hot3 = where[0:rows, 0:n16 * TOPK].rearrange("p (s j) -> p s j", j=TOPK)
                            then(dve.tensor_tensor(hot3, bc(flat, 2, TOPK), bc(cst("iota")[0:rows, :], 1, n16), ALU.is_equal))
                            then(dve.tensor_tensor(grid(where), grid(where), bc(pair(topf)[:, n], 2, TOPK), ALU.mult))
                            then(dve.tensor_reduce(flat, hot3, AX.X, ALU.add))
                        then(dve.scalar_tensor_tensor(out=sel1[0:rows, 0:n16], in0=sel1[0:rows, 0:n16], scalar=float(N_KEYS), in1=sel2[0:rows, 0:n16], op0=ALU.mult, op1=ALU.add))
                        then(dve.tensor_scalar(sel1[0:rows, 0:n16], sel1[0:rows, 0:n16], layer_off[0:rows, 1:2], None, ALU.add))
                        dve.tensor_copy(idx[0:rows, t, 0:n16], sel1[0:rows, 0:n16]).then_inc(sem("idx_ready"), 1)
                        dve.wait_ge(sem("idx_ready"), t + 1)
                        dve.wait_ge(sem("experts_exp"), t + 1)
                        then(dve.tensor_reduce(sel2[0:rows, 0:nh], w, AX.X, ALU.add))
                        then(dve.reciprocal(sel2[0:rows, 16:16 + nh], sel2[0:rows, 0:nh]))
                        then(dve.tensor_tensor(w, w, bc(sel2[0:rows, 16:16 + nh], 2, TOPK), ALU.mult))

                    for t in range(3):
                        rows, turns = (P, P // RING) if t < 2 else (64, TOPK // RING)
                        tokens = h[0:rows, t, :] if t < 2 else hr[0:rows, :]
                        for i in turns_of(dve, t):
                            if t < 2:
                                own.enter(i, 1)
                            for k in range(RING):
                                dve.wait_ge(sem(f"slot{k}_loads"), i * 16 + 16 * (U_USES[t] + 1))
                                dve.tensor_tensor_reduce(ring[0:rows, k, :], ring[0:rows, k, :], tokens, 1.0, 0.0, ALU.mult, ALU.add,
                                                         dot8[0:rows, k:k + 1]).then_inc(sem("rows_dotted"), 1)
                            dve.wait_ge(sem("rows_dotted"), i * RING + (U_DONE[t] + RING))
                            then(dve.tensor_copy(dots[0:rows, bass.ds(i * RING, RING)], dot8[0:rows, :]))
                        if t < 2:
                            own.leave(turns)
                        dve.nop().then_inc(sem("dots_ready"), 1)
                        n16 = P if t < 2 else TOPK
                        then(dve.memset(acc[0:rows, :], 0.0))
                        dve.wait_ge(sem("gelu_ready"), t + 1)
                        then(dve.tensor_tensor(wgt[0:rows, t, 0:n16], wgt[0:rows, t, 0:n16], dots[0:rows, 0:n16], ALU.mult))
                        table = ident if t < 2 else cst("mod8")
                        outs = P if t < 2 else SAMPLES
                        for i in turns_of(dve, t):
                            for n, k in enumerate(PE_SLOTS):
                                dve.wait_ge(sem("tensor_slots_used"), i * len(PE_SLOTS) + (PE_USES[t] + n + 1))
                                dve.tensor_scalar(diag[0:rows, k, 0:outs], table[0:rows, 0:outs], wgt[0:rows, t, bass.ds(i * RING + k, 1)], None, ALU.mult).then_inc(sem("diag_ready"), 1)
                            for n, k in enumerate(VECTOR_SLOTS):
                                dve.wait_ge(sem(f"slot{k}_loads"), i * 16 + 16 * (V_USES[t] + 1))
                                dve.wait_ge(sem("vector_slots_used"), i * len(VECTOR_SLOTS) + (VECTOR_USES[t] + len(VECTOR_SLOTS) + n))
                                dve.scalar_tensor_tensor(out=acc[0:rows, :], in0=ring[0:rows, k, :], scalar=wgt[0:rows, t, bass.ds(i * RING + k, 1)],
                                                         in1=acc[0:rows, :], op0=ALU.mult, op1=ALU.add).then_inc(sem("vector_slots_used"), 1)
                        dve.wait_ge(sem("vector_slots_used"), VECTOR_USES[t + 1] + len(VECTOR_SLOTS))
                        dve.nop().then_inc(sem("acc_ready"), 1)
                        for half in range(2):
                            b = aux.read()
                            r = P if t < 2 else SAMPLES
                            xs = x[0:r, t, half * 512:(half + 1) * 512]
                            aux.emptied(dve.tensor_tensor(xs, xs, ps[0:r, b, :], ALU.add), wait=True)
                    then(dve.tensor_scalar(layer_off[:, 0:1], layer_off[:, 0:1], float(a["cache_latent"].shape[1] * PIECES), None, ALU.add))
                    then(dve.tensor_scalar(layer_off[:, 1:2], layer_off[:, 1:2], float(N_EXPERTS), None, ALU.add))

                @block.scalar
                def _(act):
                    wide = Ring(act, sem("wide_full"), sem("wide_free"), (0, 1, 2, 3))
                    act.nop().then_inc(sem("wide_free"), 4)

                    def squares(junk, src, total, last=None):
                        ins = act.activation(junk, src, ACT.Square, accum_out=total)
                        if last:
                            ins.then_inc(sem(last), 1)

                    def root(dst, mean, name):
                        act.wait_ge(sem(f"{name}_squares_mean"), 1)
                        act.activation(dst, mean, ACT.Sqrt).then_inc(sem(f"{name}_root"), 1)

                    for t in range(3):
                        squares(h[:, t, :], x[:, t, :], ss[:, t:t + 1], "x_squares" if t == 2 else None)
                    root(rt, ss, "x")
                    act.wait_ge(sem("vt_ready"), 1)
                    with act.Fori(0, 4) as i:
                        wide.enter(i, 4)
                        for k in range(4):
                            b = wide.read()
                            m = i * 4 + k
                            wide.emptied(act.activation(gate[:, bass.ds(m, 1), :].rearrange("p o t -> p (o t)"), ps[:, b, 0:TOKENS], ACT.Sigmoid,
                                                        bias=vt[:, bass.ds(m + (CONV + 1) * CC, 1)]))
                    wide.leave(4)
                    with act.Fori(0, 2) as i:
                        wide.base = i * 4
                        wide.per = 4
                        for k in range(4):
                            b = wide.read()
                            wide.emptied(act.copy(zt[:, bass.ds(i * 4 + k, 1), :].rearrange("p o t -> p (o t)"), ps[:, b, 0:TOKENS]))
                    wide.leave(2)
                    with act.Fori(0, 3) as i:
                        wide.base = i * 4
                        for k in range(4):
                            b = wide.read()
                            m = i * 4 + k
                            act.copy(pad[:, bass.ds(m, 1), PAD:PAD + SEQ].rearrange("p o t -> p (o t)"), ps[:, b, 0:SEQ])
                            wide.emptied(act.copy(pad_s[:, bass.ds(m, 1), :, PAD].rearrange("p o t -> p (o t)"), ps[:, b, SEQ:TOKENS]))
                    wide.leave(3)
                    assert wide.n == marks["main"]
                    act.wait_ge(sem("wide_free"), 4 + marks["main"])
                    act.activation(zsig, zt, ACT.Sigmoid).then_inc(sem("z_sigmoid"), 1)
                    act.wait_ge(sem("tok_zeroed"), 1)
                    for first, cols in TAIL:
                        for t, (t0, rows) in enumerate(TILES):
                            b = wide.read()
                            wide.emptied(act.copy(tok[0:rows, t, first:first + cols], ps[0:rows, b, 0:cols]))
                    act.wait_ge(sem("conv_raw"), 1)
                    act.wait_ge(sem("z_ready"), 1)
                    act.activation(sig[:, :, 0:CONV_OUT], conv[:, :, 0:CONV_OUT], ACT.Sigmoid).then_inc(sem("conv_sigmoid"), 1)
                    act.wait_ge(sem("abs_ready"), 1)
                    act.activation(hd[:, HEADS:2 * HEADS], hd[:, HEADS:2 * HEADS], ACT.Exp)
                    act.activation(dte, dte, ACT.Exp, scale=-1.0).then_inc(sem("dt_exp"), 1)
                    act.wait_ge(sem("dtw_ready"), 1)
                    act.activation(dtl, dtw, ACT.Ln).then_inc(sem("dt_log"), 1)
                    act.wait_ge(sem("decays_raw"), 1)
                    act.activation(ea, a_cs[:, :, 0, :], ACT.Exp)
                    act.activation(eend[:, 0, :], dta[:, 2, :], ACT.Exp).then_inc(sem("da_ready"), 1)
                    act.activation(decf, decf, ACT.Exp)
                    act.activation(dec, dec, ACT.Exp).then_inc(sem("decays_ready"), 1)
                    act.wait_ge(sem("conv_ready"), 1)
                    for t in range(2):
                        if t == 1:
                            act.wait_ge(sem("aux_full"), marks["ydiag0"])
                        for q in range(4):
                            b = wide.read()
                            for k in range(4):
                                hh = 4 * q + k
                                last = act.activation(el[:, hh, :], ps[:, b, k * P:(k + 1) * P], ACT.Exp, bias=nacs[:, t, hh:hh + 1])
                            wide.emptied(last)
                    act.wait_ge(sem("y_gated"), 1)
                    for t in range(3):
                        for g in range(GROUPS):
                            squares(h[:, t, g * 512:(g + 1) * 512], y[:, t, g * 512:(g + 1) * 512], ss6[:, 2 * t + g:2 * t + g + 1], "y_squares" if (t, g) == (2, 1) else None)
                    root(rt6, ss6, "y")
                    lsq, lrt = st[:, 27:33], st[:, 33:39]
                    act.wait_ge(sem("wide_free"), 4 + marks["tail"])
                    for t in range(3):
                        squares(h[:, t, 0:Q_LORA], tok[:, t, T_CQ:T_CKV], lsq[:, t:t + 1])
                        squares(h[:, t, 512:512 + KV_LORA], tok[:, t, T_CKV:T_KR], lsq[:, 3 + t:4 + t], "lat_squares" if t == 2 else None)
                    root(lrt, lsq, "lat")
                    for hh in range(A_HEADS):
                        b = wide.read()
                        wide.emptied(act.copy(qnt[0:NOPE, hh, :], ps[0:NOPE, b, 0:TOKENS]))
                    for t, (t0, rows) in enumerate(TILES):
                        b = wide.read()
                        wide.emptied(act.copy(qr[0:rows, t, :, :].rearrange("p h k -> p (h k)"), ps[0:rows, b, 0:256]))
                    for c in range(2):
                        for hh in range(A_HEADS):
                            b = wide.read()
                            wide.emptied(act.copy(ql[:, c, hh, :], ps[:, b, 0:TOKENS]))
                    for t in range(2):
                        act.wait_ge(sem("scores_max"), t + 1)
                        for hh in range(A_HEADS):
                            last = act.activation(sc[:, hh, 0:P * (t + 1)], sc[:, hh, 0:P * (t + 1)], ACT.Exp, scale=SCALE, bias=anm[:, hh:hh + 1], accum_out=asum[:, hh:hh + 1])
                        last.then_inc(sem("scores_exp"), 1)
                    with act.Fori(0, SAMPLES // 2) as i:
                        for s in range(2):
                            act.wait_ge(sem("shifted"), i * 2 + s + 1)
                            act.activation(sexp, sexp, ACT.Exp, scale=SCALE).then_inc(sem("sample_exp"), 1)

                    act.wait_ge(sem("x_mixed"), 1)
                    act.wait_ge(sem("attention_done"), 1)
                    for t in range(3):
                        squares(h[:, t, :], x[:, t, :], st[:, 45 + t:46 + t], "px_squares" if t == 2 else None)
                    root(st[:, 48:51], st[:, 45:48], "px")
                    with act.Fori(0, 4) as i:
                        wide.enter(i, 4)
                        for k in range(4):
                            b = wide.read()
                            wide.emptied(act.copy(gate[:, bass.ds(i * 4 + k, 1), :].rearrange("p o t -> p (o t)"), ps[:, b, 0:TOKENS]))
                    wide.leave(4)
                    for t in range(3):
                        if t:
                            act.wait_ge(sem("scores_used"), t)
                        for q in range(4 if t < 2 else 1):
                            b = wide.read()
                            cols, rows = (512, P) if t < 2 else (256, 64)
                            wide.emptied(act.copy(keysc.rearrange("p k n -> p (k n)")[0:rows, q * 512:q * 512 + cols], ps[0:rows, b, 0:cols]))
                        rows, n16 = (P, P) if t < 2 else (64, TOPK)
                        act.wait_ge(sem("experts_shifted"), t + 1)
                        act.activation(wgt[0:rows, t, 0:n16], wgt[0:rows, t, 0:n16], ACT.Exp).then_inc(sem("experts_exp"), 1)
                    for t in range(3):
                        rows, n16 = (P, P) if t < 2 else (64, TOPK)
                        act.wait_ge(sem("dots_ready"), t + 1)
                        act.activation(dots[0:rows, 0:n16], dots[0:rows, 0:n16], ACT.Gelu).then_inc(sem("gelu_ready"), 1)

                @block.sync
                def _(sp):
                    vr = ssd("vrows")
                    sp.dma_start(vr[0:CONV * CC, :], of_layer("conv_w", layer).rearrange("k (c p) -> (k c) p", p=P)).then_inc(sem("vec_loads"), 16)
                    sp.dma_start(vr[CONV * CC:CONV * CC + CC, :], of_layer("conv_b", layer).rearrange("(c p) -> c p", p=P)).then_inc(sem("vec_loads"), 16)
                    sp.dma_start(vr[CONV * CC + CC:VEC_ROWS, :], of_layer("b_gate", layer).rearrange("(c p) -> c p", p=P)).then_inc(sem("vec_loads"), 16)
                    sp.dma_start(nrow[:, :], of_layer("norm_mix", layer).partition_broadcast(P)).then_inc(sem("nrow_load"), 16)

                    count = [0]

                    def load_block(src, chunks, cols, base=None):
                        n = count[0]
                        if n >= 2 or base is not None:
                            sp.wait_ge(sem("blocks_begun"), n if base is None else base + n)
                        sp.dma_start(wblock(n % 2, chunks, cols), src).then_inc(sem(f"block{n % 2}_loads"), 16)
                        count[0] += 1

                    w_in = of_layer("w_in", layer).rearrange("(p c) n -> p c n", c=DC)
                    for k in range(2):
                        load_block(w_in[:, :, k * BLOCK:(k + 1) * BLOCK], DC, BLOCK)
                    with sp.Fori(1, MAIN_BLOCKS // 2) as i:
                        for k in range(2):
                            count[0] = k
                            load_block(w_in[:, :, bass.ds(i * 2 * BLOCK + k * BLOCK, BLOCK)], DC, BLOCK, base=i * 2)
                    count[0] = MAIN_BLOCKS
                    for v, name in enumerate(("dt_bias", "a_log", "d_skip")):
                        sp.dma_start(hd[:, v * HEADS:(v + 1) * HEADS], of_layer(name, layer).partition_broadcast(P)).then_inc(sem("head_loads"), 16)
                    sp.dma_start(kvn[:, :], of_layer("kv_norm", layer).partition_broadcast(P)).then_inc(sem("head_loads"), 16)
                    sp.dma_start(qn[:, :], of_layer("q_norm", layer).rearrange("(p c) -> p c", c=3)).then_inc(sem("head_loads"), 16)
                    sp.dma_start(ssmn[:, :], of_layer("ssm_norm", layer).rearrange("(p c) -> p c", c=DC)).then_inc(sem("head_loads"), 16)
                    for first, cols in TAIL:
                        load_block(w_in[:, :, C_DT + first:C_DT + first + cols], DC, cols)
                    w_ssm = of_layer("w_ssm_proj", layer).rearrange("(p c) n -> p c n", c=DC)
                    w_out = of_layer("w_out", layer).rearrange("(c p) n -> p c n", p=P)
                    w_mla = of_layer("w_mla_proj", layer).rearrange("(c p) n -> p c n", p=P)
                    for k in range(4):
                        load_block(w_ssm[:, :, k * BLOCK:(k + 1) * BLOCK], DC, BLOCK)
                    for k in range(2):
                        load_block(w_mla[:, :, 2 * k * BLOCK:2 * (k + 1) * BLOCK], 4, 2 * BLOCK)
                    for k in range(4):
                        load_block(w_out[:, :, k * BLOCK:(k + 1) * BLOCK], DC, BLOCK)
                    w_q = of_layer("peer_wq", layer).rearrange("(p c) n -> p c n", c=DC)
                    first = count[0]
                    assert first == marks["wq_block"]
                    with sp.Fori(0, 4) as i:
                        for k in range(2):
                            count[0] = first + k
                            load_block(w_q[:, :, bass.ds(i * 2 * BLOCK + k * BLOCK, BLOCK)], DC, BLOCK, base=i * 2)

                @block.gpsimd
                def _(pool):
                    pages = a["cache_latent"].rearrange("l n (r k) d -> (l n r) (k d)", k=PIECE)
                    kropes = a["cache_krope"].rearrange("l n (r k) d -> (l n r) (k d)", k=PIECE)
                    pool.tensor_scalar(pagef[:, 0:SAMPLES], pagef[:, SAMPLES:], layer_off[:, 0:1], None, ALU.add).then_inc(sem("pool_pages"), 1)
                    pool.wait_ge(sem("pool_pages"), 1)
                    pool.tensor_copy(page_idx[:, SAMPLES:], pagef[:, 0:SAMPLES]).then_inc(sem("pool_pages"), 1)
                    pool.wait_ge(sem("pool_pages"), 2)
                    pool.dma_start(ssd("cstate")[0:PAD * SAMPLES, :], of_layer("state_conv", layer).rearrange("b k c -> (b k) c")).then_inc(sem("cstate_load"), 16)
                    pool.dma_start(of_layer_out(o_convs, layer)[:, 0:PAD - 1, :], of_layer("state_conv", layer)[:, 1:PAD, :]).then_inc(sem("stores"), 16)
                    pool.wait_ge(sem("rawt_ready"), 1)
                    pool.dma_start(of_layer_out(o_convp, layer)[0, :, :], rawt[0:PAD, :]).then_inc(sem("stores"), 16)
                    pool.dma_start(of_layer_out(o_convs, layer)[:, PAD - 1, :], rawt[PAD:PAD + SAMPLES, :]).then_inc(sem("rawt_stores"), 16)
                    pool.wait_ge(sem("stores"), 32)
                    pool.wait_ge(sem("rawt_stores"), 16)
                    pool.nop().then_inc(sem("rawt_stored"), 1)
                    pool.wait_ge(sem("hs_ready"), 1)
                    pool.dma_start(of_layer_out(o_ssmp, layer)[0].rearrange("g e p n -> (g e p) n").rearrange("(c q) n -> q c n", q=P),
                                 hs.rearrange("p (c n) -> p c n", c=DC)).then_inc(sem("stores"), 16)
                    h0 = of_layer("state_ssm", layer).rearrange("b g e p n -> b (g e p) n").rearrange("b (c q) n -> b q c n", q=P)
                    h1 = of_layer_out(o_ssms, layer).rearrange("b g e p n -> b (g e p) n").rearrange("b (c q) n -> b q c n", q=P)
                    pool.wait_ge(sem("el_used"), 1)
                    for b in range(SAMPLES + 2):
                        if b >= 2:
                            pool.wait_ge(sem("state_ready"), b - 1)
                            pool.dma_start(h1[b - 2], stt[:, b % 2, :, :]).then_inc(sem(f"state_store{b % 2}"), 16)
                        if b < SAMPLES:
                            if b >= 2:
                                pool.wait_ge(sem(f"state_store{b % 2}"), 16 * (b // 2))
                                pool.wait_ge(sem("state_used"), b - 1)
                            pool.dma_start(stt[:, b % 2, :, :], h0[b]).then_inc(sem(f"state_load{b % 2}"), 16)
                    pool.wait_ge(sem("lat_ready"), 1)
                    pool.dma_start(of_layer_out(o_latp, layer)[0].rearrange("(t p) r -> p t r", p=P), lat[:, 0:2, :]).then_inc(sem("stores"), 16)
                    pool.dma_start(of_layer_out(o_lats, layer)[:, 0, :], lat[0:SAMPLES, 2, :]).then_inc(sem("stores"), 16)
                    pool.dma_start(of_layer_out(o_krp, layer)[0].rearrange("(t p) r -> p t r", p=P), kpe[:, 0:2, :]).then_inc(sem("stores"), 16)
                    pool.dma_start(of_layer_out(o_krs, layer)[:, 0, :], kpe[0:SAMPLES, 2, :]).then_inc(sem("stores"), 16)
                    pool.wait_ge(sem("scan_done"), 1)
                    for s in range(2):
                        pool.wait_ge(sem(f"state_store{s}"), 16 * (SAMPLES // 2))
                    pool.dma_start(wqb, of_layer("w_qb", layer).rearrange("(p c) n -> p c n", c=3)).then_inc(sem("wqb_load"), 16)
                    pool.dma_start(wkv, of_layer("w_kvb", layer).rearrange("(c p) n -> p c n", p=P)).then_inc(sem("wkv_load"), 16)
                    pool.wait_ge(sem("nrow_used"), 1)
                    pool.dma_start(nrow[:, :], of_layer("norm_ffn", layer).partition_broadcast(P)).then_inc(sem("ffn_row_load"), 16)
                    pool.wait_ge(sem("queries_done"), 1)
                    for b in range(SAMPLES):
                        s = b % 2
                        if b >= 2:
                            pool.wait_ge(sem("aux_full"), marks["att"] + 14 * (b - 1))
                        for dst, src in ((ck, pages), (cr, kropes)):
                            pool.indirect_dma_start(dst[:, s, :, :].rearrange("p j r -> p (j r)"), None, src,
                                                    bass.IndirectOffsetOnAxis(ap=page_idx[:, SAMPLES + b:SAMPLES + b + 1], axis=0)).then_inc(sem(f"pages{s}_loads"), 16)
                    for s in range(2):
                        pool.wait_ge(sem(f"pages{s}_loads"), 32 * (SAMPLES // 2))
                    pool.wait_ge(sem("attention_done"), 1)
                    pool.dma_start(keys, of_layer("peer_keys", layer).rearrange("h s k d -> k (h s) d")).then_inc(sem("keys_load"), 16)
                    tables = [a[name].rearrange("l n d -> (l n) d") for name in ("peer_u", "peer_v")]
                    half = RING // 2
                    pool.memset(settled, 0.0).then_inc(sem("settled_zeroed"), 1)
                    pool.wait_ge(sem("settled_zeroed"), 1)

                    def gather(t, table, used):
                        rows, turns = (P, P // RING) if t < 2 else (64, TOPK // RING)
                        for i in turns_of(pool, t):
                            for g in range(2):
                                for name, value in used(i, g):
                                    pool.wait_ge(sem(name), value)
                                cols = slice(g * half, (g + 1) * half)
                                pool.tensor_copy(stage[0:rows, cols], idx[0:rows, t, bass.ds(i * RING + g * half, half)]).then_inc(sem("staged"), 1)
                                staged[0] += 1
                                pool.wait_ge(sem("staged"), (i * 2 if t < 2 else 0) + staged[0])
                                pool.tensor_tensor(settled, settled, settled, ALU.add)
                                for k in range(g * half, (g + 1) * half):
                                    pool.indirect_dma_start(ring[0:rows, k, :], None, table, bass.IndirectOffsetOnAxis(ap=stage[0:rows, k:k + 1], axis=0)).then_inc(sem(f"slot{k}_loads"), 16)
                        if t < 2:
                            staged[0] += 2 * (turns - 1)

                    staged = [0]
                    for t in range(3):
                        pool.wait_ge(sem("idx_ready"), t + 1)
                        if t:
                            pool.wait_ge(sem("tensor_slots_used"), PE_USES[t] + len(PE_SLOTS))
                            pool.wait_ge(sem("vector_slots_used"), VECTOR_USES[t] + len(VECTOR_SLOTS))
                        gather(t, tables[0], lambda i, g: [("rows_dotted", i * RING + (U_DONE[t] - half + g * half))])
                        pool.wait_ge(sem("rows_dotted"), U_DONE[t + 1])
                        gather(t, tables[1], lambda i, g: [
                            ("tensor_slots_used", i * len(PE_SLOTS) + (PE_USES[t] + sum(k < (g + 1) * half for k in PE_SLOTS))),
                            ("vector_slots_used", i * len(VECTOR_SLOTS) + (VECTOR_USES[t] + sum(k < (g + 1) * half for k in VECTOR_SLOTS)))])
                    for k in range(RING):
                        pool.wait_ge(sem(f"slot{k}_loads"), 16 * V_USES[3])
                    pool.wait_ge(sem("stores"), 16 * 7)
                    for name in ("cstate_load", "wqb_load", "wkv_load", "ffn_row_load", "keys_load"):
                        pool.wait_ge(sem(name), 16)
                    for s in range(2):
                        pool.wait_ge(sem(f"state_load{s}"), 16 * (SAMPLES // 2))
                    pool.dma_reset(span(sems))

            nc.all_engine_barrier(sems_to_clear=span(sems))

        with nc.Block() as block:
            @block.sync
            def _(sp):
                sp.dma_start(nrow[:, :], a["norm_final"].partition_broadcast(P)).then_inc(sem("nrow_load"), 16)
                sp.wait_ge(sem("h_ready"), 1)
                sp.dma_start(o_yp.rearrange("o (t p) d -> p (o t) d", p=P), h[:, 0:2, :]).then_inc(sem("y_stores"), 16)
                sp.dma_start(o_ys.rearrange("b o d -> (b o) d"), h[0:SAMPLES, 2, :]).then_inc(sem("y_stores"), 16)
                sp.wait_ge(sem("y_stores"), 32)

            @block.scalar
            def _(act):
                for t in range(3):
                    last = act.activation(h[:, t, :], x[:, t, :], ACT.Square, accum_out=ss[:, t:t + 1])
                last.then_inc(sem("x_squares"), 1)
                act.wait_ge(sem("x_squares_mean"), 1)
                act.activation(rt, ss, ACT.Sqrt).then_inc(sem("x_root"), 1)

            @block.vector
            def _(dve):
                dve.wait_ge(sem("x_squares"), 1)
                dve.tensor_scalar(ss, ss, 1.0 / D_MODEL, EPS, ALU.mult, ALU.add).then_inc(sem("x_squares_mean"), 1)
                dve.wait_ge(sem("x_root"), 1)
                dve.reciprocal(rs, rt).then_inc(sem("vector_steps"), 1)
                dve.wait_ge(sem("vector_steps"), 1)
                dve.wait_ge(sem("nrow_load"), 16)
                for t in range(3):
                    last = dve.scalar_tensor_tensor(out=h[:, t, :], in0=x[:, t, :], scalar=rs[:, t:t + 1], in1=nrow[:, :], op0=ALU.mult, op1=ALU.mult)
                last.then_inc(sem("h_ready"), 1)


_INPUTS = ["x_prompt", "x_sample", "cache_latent", "cache_krope", "state_ssm", "state_conv", "page_table",
           "norm_mix", "w_in", "b_gate", "conv_w", "conv_b", "dt_bias", "a_log", "d_skip", "ssm_norm", "w_ssm_proj",
           "q_norm", "w_qb", "kv_norm", "w_kvb", "w_mla_proj", "w_out", "norm_ffn", "peer_wq", "peer_keys",
           "peer_u", "peer_v", "norm_final"]
_OUTPUTS = [(1, SEQ, D_MODEL), (SAMPLES, 1, D_MODEL), (DEPTH, 1, SEQ, KV_LORA), (DEPTH, 1, SEQ, ROPE),
            (DEPTH, 1, GROUPS, HEADS // GROUPS, HEAD_DIM, D_STATE), (DEPTH, 1, PAD, CONV_DIM),
            (DEPTH, SAMPLES, 1, KV_LORA), (DEPTH, SAMPLES, 1, ROPE),
            (DEPTH, SAMPLES, GROUPS, HEADS // GROUPS, HEAD_DIM, D_STATE), (DEPTH, SAMPLES, PAD, CONV_DIM)]


def kernel(**inputs):
    import concourse.bacc as bacc
    from concourse.bass_utils import run_bass_kernel_spmd

    nc = bacc.Bacc("TRN2", target_bir_lowering=False, num_devices=1)
    arrays, args = {}, {}
    for name in _INPUTS + ["consts"]:
        arr = CONST_ARRAY if name == "consts" else np.ascontiguousarray(inputs[name])
        arrays["in_" + name] = arr
        args[name] = nc.dram_tensor("in_" + name, arr.shape, mybir.dt.from_np(arr.dtype), kind="ExternalInput").ap()
    outs = [nc.dram_tensor(f"out_{i}", s, F32, kind="ExternalOutput").ap() for i, s in enumerate(_OUTPUTS)]
    build(nc, DEPTH, args, outs)
    r = run_bass_kernel_spmd(nc, [arrays], core_ids=[0])
    return tuple(r.results[0][f"out_{i}"] for i in range(len(_OUTPUTS)))
```

```python
from contextlib import ExitStack
from itertools import chain

import numpy as np

import concourse.bass as bass
from concourse import mybir

ALU = mybir.AluOpType
ACT = mybir.ActivationFunctionType
AX = mybir.AxisListType
F32 = mybir.dt.float32
I32 = mybir.dt.int32
U32 = mybir.dt.uint32

D_MODEL, SEQ, DEPTH, SAMPLES = 1024, 256, 2, 8
TOKENS = SEQ + SAMPLES
HEADS, GROUPS, HEAD_DIM, D_STATE, CONV = 16, 2, 64, 128, 4
CONV_DIM = D_MODEL + 2 * GROUPS * D_STATE
A_HEADS, NOPE, ROPE, V_HEAD, Q_LORA, KV_LORA = 8, 64, 32, 64, 384, 256
PAST, PAGE = 2048, 128
PAGES = PAST // PAGE
SCALE = (NOPE + ROPE) ** -0.5
P_HEADS, N_KEYS, TOPK = 8, 128, 16
N_EXPERTS = N_KEYS * N_KEYS
EPS = 1e-6
NEG = -1e30
P = 128
TILES = [(0, P), (P, P), (SEQ, SAMPLES)]
DC = D_MODEL // P
C_DT = 3 * D_MODEL + CONV_DIM
IN_DIM = C_DT + HEADS + Q_LORA + KV_LORA + ROPE
BLOCK = 256
MAIN_BLOCKS = C_DT // BLOCK
TAIL = [(0, 272), (272, 256), (528, 160)]
TAIL_W = IN_DIM - C_DT
T_CQ, T_CKV, T_KR = HEADS, HEADS + Q_LORA, HEADS + Q_LORA + KV_LORA
PAD = CONV - 1
CONV_ROW = PAD + SEQ + CONV * SAMPLES
CONV_OUT = CONV_ROW - PAD
S_COL = PAD + SEQ
CC = CONV_DIM // P
PIECE = PAST // P
PIECES = PAGE // PIECE
RING = 8
PE_SLOTS, VECTOR_SLOTS = (0, 2, 3, 5, 6), (1, 4, 7)
REST = 4
TURNS = (P // RING, P // RING, TOPK // RING)
ORDER = (2, 0, 1)
PLACE = [ORDER.index(t) for t in range(3)]
BEFORE = [sum(TURNS[o] for o in ORDER[:PLACE[t]]) for t in range(3)]
U_DONE = [RING * (n + 1) for n in BEFORE]
U_USES = [2 * n for n in BEFORE]
V_USES = [2 * BEFORE[t] + TURNS[t] for t in range(3)]
PE_USES = [len(PE_SLOTS) * n for n in BEFORE]
VECTOR_USES = [len(VECTOR_SLOTS) * n for n in BEFORE]
VEC_ROWS = CONV * CC + CC + 2 * DC

CONSTS = {}


def constants():
    p = np.arange(P)
    out = {}
    out["ident"] = np.eye(P)
    out["triu"] = (p[:, None] <= p[None, :]) * 1.0
    out["neg"] = np.where(p[:, None] > p[None, :], NEG, 0.0)
    out["ones"] = np.ones((P, P))
    out["causal"] = np.where(p[None, :] > p[:, None], NEG, 0.0)
    out["newmask"] = np.broadcast_to(np.where(np.eye(SAMPLES) > 0, 0.0, NEG).reshape(1, -1), (P, SAMPLES * SAMPLES))
    out["quarter"] = (p[:, None] // ROPE == np.arange(4)[None, :]) * 1.0
    out["mod8"] = (p[:, None] % SAMPLES == np.arange(SAMPLES)[None, :]) * 1.0
    rep = np.zeros((P, 64))
    rep[:SAMPLES] = np.arange(SAMPLES)[:, None] == np.arange(64)[None, :] % SAMPLES
    out["rep"] = rep
    out["iota"] = np.broadcast_to(np.arange(TOPK)[None, :], (P, TOPK))
    out["piece"] = (p % PIECES)[:, None]
    pos = np.concatenate([np.arange(SEQ), np.full(P, PAST)]).astype(np.float32)
    half = ROPE // 2
    inv = (np.float32(10000.0) ** (-np.arange(half, dtype=np.float32) / np.float32(half))).astype(np.float32)
    ang = (pos[:, None] * inv[None, :]).astype(np.float32).astype(np.float64)
    for name, f in (("cos", np.cos), ("sin", np.sin)):
        out[name] = f(ang).reshape(3, P, half).transpose(1, 0, 2).reshape(P, 3 * half)
    at = 0
    for name, a in out.items():
        CONSTS[name] = (at, at + a.shape[1])
        at += a.shape[1]
    return np.ascontiguousarray(np.concatenate([np.asarray(a, np.float32) for a in out.values()], axis=1))


CONST_ARRAY = constants()


class Ring:

    def __init__(self, eng, full, free, banks):
        self.eng, self.full, self.free, self.banks = eng, full, free, banks
        self.n, self.base = 0, 0

    def fill(self, ahead=0):
        self.eng.wait_ge(self.free, self.base + self.n + ahead + 1)
        return self.banks[(self.n + ahead) % 4]

    def filled(self, ins):
        ins.then_inc(self.full, 1)
        self.n += 1

    def all_emptied(self):
        self.eng.wait_ge(self.free, self.base + self.n + 4)

    def read(self, ahead=0):
        self.eng.wait_ge(self.full, self.base + self.n + ahead + 1)
        return self.banks[(self.n + ahead) % 4]

    def emptied(self, ins, wait=False, banks=1):
        ins.then_inc(self.free, banks)
        self.n += banks
        if wait:
            self.eng.wait_ge(self.free, self.base + self.n + 4)

    def enter(self, i, per):
        self.base = i * per
        self.per = per

    def leave(self, turns):
        self.base = 0
        self.n += (turns - 1) * self.per


class Own:

    def __init__(self, eng, sem):
        self.eng, self.sem, self.n, self.base = eng, sem, 0, 0

    def then(self, ins):
        ins.then_inc(self.sem, 1)
        self.n += 1
        self.eng.wait_ge(self.sem, self.base + self.n)

    def enter(self, i, per):
        self.base, self.per, self.at = i * per, per, self.n

    def leave(self, turns):
        assert self.n - self.at == self.per, (self.n - self.at, self.per)
        self.base = 0
        self.n += (turns - 1) * self.per


def cut(names, offset=0):
    out = {}
    for name, size in names:
        out[name] = (offset, offset + size)
        offset += size
    return out, offset


ARENA_SSD, A1 = cut([
    ("vrows", 128), ("cstate", CONV_DIM), ("z", DC * TOKENS), ("pad", CC * CONV_ROW), ("conv", CC * CONV_ROW),
    ("sig", CC * CONV_ROW), ("xt", 3 * D_MODEL), ("bt", 2 * 256), ("bcs", 512), ("xdt", 2 * D_MODEL), ("cb", 512),
    ("hpt", 1024), ("y", 3 * D_MODEL),
])
ARENA_SSD["el"] = (ARENA_SSD["sig"][0], ARENA_SSD["sig"][0] + 2048)
ARENA_SSD["xde"] = (ARENA_SSD["el"][1], ARENA_SSD["el"][1] + 1024)
ARENA_SSD["yt"] = ARENA_SSD["z"]
pad0 = ARENA_SSD["pad"][0]
ARENA_SSD["hs"] = (pad0, pad0 + 1024)
ARENA_SSD["xdf"] = (pad0 + 1024, pad0 + 3072)
s0 = ARENA_SSD["sig"][0]
ARENA_SSD["st"] = (s0, s0 + 2048)
ARENA_SSD["stx"] = ARENA_SSD["xdf"]
ARENA_SSD["stc"] = ARENA_SSD["xde"]
ARENA_SSD["rawt"] = (ARENA_SSD["xdt"][0], ARENA_SSD["xdt"][0] + CONV_DIM)

ARENA_ATT, A2 = cut([
    ("wkt", 2048), ("ck", 2 * 4096), ("cr", 2 * 512), ("kt", 4096 + 512), ("qpt", A_HEADS * TOKENS),
    ("ql", 2 * A_HEADS * TOKENS), ("qpad", 256), ("srow", PAST + SAMPLES),
])
ARENA_ATT["wkv"] = (A1, A1 + 2048)
assert A2 + 2048 >= A1 >= A2
ARENA_ATT["osamp"] = ARENA_ATT["wkt"]
k0 = ARENA_ATT["kt"][0]
ARENA_ATT["qnt"] = (k0, k0 + A_HEADS * TOKENS)
ARENA_ATT["wqb"] = (k0 + A_HEADS * TOKENS, k0 + A_HEADS * TOKENS + 2304)
ARENA_ATT["s"] = (k0, k0 + 2048)
ARENA_ATT["pt"] = (k0 + 2048, k0 + 4096)
ARENA_ATT["ot"] = (k0, k0 + 4 * TOKENS)
c0 = ARENA_ATT["ck"][0]
ARENA_ATT["qr"] = (c0, c0 + 768)
ARENA_ATT["qpe"] = (c0 + 768, c0 + 1536)
ARENA_ATT["qrep"] = (c0 + 3072, c0 + 4096)
ARENA_ATT["rt"] = (c0 + 1536, c0 + 1536 + 4 * 384)

ARENA_PEER, A3 = cut([
    ("ring", RING * D_MODEL), ("keys", 2048), ("keyst", 2048), ("sc", 2048), ("qz", 2 * 576),
    ("cand", 2048), ("hot", 2048), ("top", 256), ("topi", 256), ("topf", 256), ("ctop", 128), ("ctopi", 128),
    ("idx", 3 * P), ("wgt", 3 * P), ("dots", P), ("hr", D_MODEL), ("acc", D_MODEL), ("diag", RING * P), ("zero", P), ("dot8", RING),
    ("sel1", 128), ("sel2", 128), ("stage", 16), ("i1", 128), ("settled", 2 * RING + 1),
])


def build(nc, layers, a, out):
    (o_yp, o_ys, o_latp, o_krp, o_ssmp, o_convp, o_lats, o_krs, o_ssms, o_convs) = out
    with ExitStack() as ctx:
        def sb(name, cols, dt=F32):
            return ctx.enter_context(nc.sbuf_tensor(name, [P, cols], dt))

        sems = {}

        def sem(name):
            if name not in sems:
                sems[name] = ctx.enter_context(nc.semaphore(name))
            return sems[name]

        def bc(ap, axis, n):
            u = ap.unsqueeze(axis)
            shape = list(u.shape)
            shape[axis] = n
            return u.to_broadcast(shape)

        def of_layer(name, l):
            ap = a[name]
            rest = "bcdef"[: len(ap.shape) - 1]
            s = ap[bass.ds(l, 1)] if len(ap.shape) == 1 else ap[(bass.ds(l, 1),) + (slice(None),) * len(rest)]
            return s.rearrange(f"a {' '.join(rest)} -> (a {rest[0]}) {' '.join(rest[1:])}")

        consts = sb("consts", CONST_ARRAY.shape[1])
        cst = lambda name: consts[:, CONSTS[name][0]:CONSTS[name][1]]
        ident, triu, neg, ones = cst("ident"), cst("triu"), cst("neg"), cst("ones")
        cos = cst("cos").rearrange("p (t k) -> p t k", t=3)
        sin = cst("sin").rearrange("p (t k) -> p t k", t=3)

        x = sb("x", 3 * D_MODEL)[:, :].rearrange("p (t d) -> p t d", t=3)
        hbuf = sb("h", 3 * D_MODEL)
        h = hbuf[:, :].rearrange("p (t d) -> p t d", t=3)
        shared = sb("ht_tok", 2 * A_HEADS * TOKENS)
        ht = shared[:, 0:DC * TOKENS].rearrange("p (c t) -> p c t", c=DC)
        tok = shared[:, DC * TOKENS:DC * TOKENS + 3 * TAIL_W].rearrange("p (t n) -> p t n", t=3)
        ol = shared[:, :].rearrange("p (r h t) -> p r h t", r=2, h=A_HEADS)
        wring = sb("wring", 2 * DC * 272)
        gate = sb("gate", 2 * DC * TOKENS)[:, :].rearrange("p (c t) -> p c t", c=2 * DC)
        lat = sb("lat", 3 * KV_LORA)[:, :].rearrange("p (t r) -> p t r", t=3)
        kpe = sb("kpe", 3 * ROPE)[:, :].rearrange("p (t r) -> p t r", t=3)
        latt = sb("latt", 2 * TOKENS)[:, :].rearrange("p (c t) -> p c t", c=2)
        kpet = sb("kpet", TOKENS)
        cqt = sb("cqt", 3 * TOKENS)[:, :].rearrange("p (c t) -> p c t", c=3)
        nrow = sb("nrow", D_MODEL)
        kvn = sb("kvn", KV_LORA)
        qn = sb("qn", 3)
        ssmn = sb("ssmn", DC)
        vt = sb("vt", VEC_ROWS)
        hd = sb("hd", 3 * HEADS)
        st = sb("st", 64)
        dtb = sb("dtb", 8 * 48)
        acs = sb("acs", 64)
        ex = sb("ex", 5 * 32)
        dtt = sb("dtt", 32)
        exs = sb("exs", DC * 16)
        dtx = sb("dtx", DC * SAMPLES)
        ysm = sb("ysm", DC * SAMPLES)
        att = sb("att", 48)
        sd = sb("sd", 17 * 8 * 3)
        page_idx = sb("page_idx", 2 * SAMPLES, I32)
        pagef = sb("pagef", 2 * SAMPLES)
        layer_off = sb("layer_off", 2)
        arena = sb("arena", max(A1 + 2048, A3))
        ps = ctx.enter_context(nc.psum_tensor("ps", [P, 8, 512], F32))

        def place(table):
            return lambda name: arena[:, table[name][0]:table[name][1]]

        ssd, mla, peer = place(ARENA_SSD), place(ARENA_ATT), place(ARENA_PEER)
        zt = ssd("z").rearrange("p (c t) -> p c t", c=DC)
        yt = zt
        pad = ssd("pad").rearrange("p (c t) -> p c t", c=CC)
        conv = ssd("conv").rearrange("p (c t) -> p c t", c=CC)
        sig = ssd("sig").rearrange("p (c t) -> p c t", c=CC)
        zsig = ssd("sig")[:, 0:DC * TOKENS].rearrange("p (c t) -> p c t", c=DC)
        xt = ssd("xt").rearrange("p (t d) -> p t d", t=3)
        bt = ssd("bt").rearrange("p (t n) -> p t n", t=2)
        bcs = ssd("bcs")
        xdt = ssd("xdt").rearrange("p (t d) -> p t d", t=2)
        cb = ssd("cb").rearrange("p (k l) -> p k l", k=4)
        hpt = ssd("hpt").rearrange("p (g q) -> p g q", g=2)
        y = ssd("y").rearrange("p (t d) -> p t d", t=3)
        el = ssd("el").rearrange("p (h l) -> p h l", h=HEADS)
        xde = ssd("xde")
        hs = ssd("hs")
        xdf = ssd("xdf").rearrange("p (t d) -> p t d", t=2)
        places = [ssd(name)[:, k * D_MODEL:(k + 1) * D_MODEL].rearrange("p (c n) -> p c n", c=DC) for name in ("st", "xdt") for k in range(2)]
        stx = ssd("stx").rearrange("p (s c n) -> p s c n", s=2, c=DC)
        stc = ssd("stc")
        rawt = ssd("rawt")
        wkv = mla("wkv").rearrange("p (c n) -> p c n", c=2)
        wkt = mla("wkt").rearrange("p (h r) -> p h r", h=A_HEADS)
        ck = mla("ck").rearrange("p (s j r) -> p s j r", s=2, j=PIECE)
        cr = mla("cr").rearrange("p (s j r) -> p s j r", s=2, j=PIECE)
        kt = mla("kt")[:, 0:4096].rearrange("p (c j t) -> p c j t", c=2, j=PIECE)
        krt = mla("kt")[:, 4096:4608].rearrange("p (q t) -> p q t", q=4)
        qpt = mla("qpt").rearrange("p (h t) -> p h t", h=A_HEADS)
        ql = mla("ql").rearrange("p (c h t) -> p c h t", c=2, h=A_HEADS)
        qpad = mla("qpad").rearrange("p (b q h) -> p b q h", b=SAMPLES, q=4)
        qnt = mla("qnt").rearrange("p (h t) -> p h t", h=A_HEADS)
        wqb = mla("wqb").rearrange("p (c n) -> p c n", c=3)
        sc = mla("s").rearrange("p (h t) -> p h t", h=A_HEADS)
        pt = mla("pt").rearrange("p (k h t) -> p k h t", k=2, h=A_HEADS)
        ot = mla("ot").rearrange("p (c t) -> p c t", c=4)
        qr = mla("qr").rearrange("p (t h k) -> p t h k", t=3, h=A_HEADS)
        qpe = mla("qpe").rearrange("p (t h k) -> p t h k", t=3, h=A_HEADS)
        rtmp = mla("rt").rearrange("p (s t h k) -> p s t h k", s=4, t=3, h=A_HEADS)
        conv_s = conv[:, :, S_COL:S_COL + CONV * SAMPLES].rearrange("p c (b k) -> p c b k", k=CONV)
        pad_s = pad[:, :, S_COL:S_COL + CONV * SAMPLES].rearrange("p c (b k) -> p c b k", k=CONV)
        amax, anm, asum, ainv = (att[:, 8 * k:8 * k + 8] for k in range(4))
        smax, sbest, sneg, ssum, sinv = att[:, 32:44], att[:, 44:45], att[:, 45:46], att[:, 46:47], att[:, 47:48]
        sexp = sd[:, 136:272].rearrange("p (j h) -> p j h", h=8)
        srow, osamp = mla("srow"), mla("osamp")
        qb = sd[:, 272:288].rearrange("p (c h) -> p c h", c=2)
        dt, dta, dtu, dte, dtl, dtw, dtd, dti = (
            dtb[:, 48 * k:48 * k + 48].rearrange("p (t h) -> p t h", t=3) for k in range(8))
        a_cs = acs[:, :].rearrange("p (t k h) -> p t k h", t=2, k=2)
        ea, dec, decf, nacs, eend = (ex[:, 32 * k:32 * k + 32].rearrange("p (t h) -> p t h", t=2) for k in range(5))
        exs4 = exs[:, :].rearrange("p (c k b) -> p c k b", c=DC, k=2)
        dtx3 = dtx[:, :].rearrange("p (c b) -> p c b", c=DC)
        ysm3 = ysm[:, :].rearrange("p (c b) -> p c b", c=DC)
        ss, rt, rs = st[:, 0:3], st[:, 3:6], st[:, 6:9]
        ss6, rt6, rs6 = st[:, 9:15], st[:, 15:21], st[:, 21:27]

        wblock = lambda s, chunks, cols: wring[:, s * DC * 272:s * DC * 272 + chunks * cols].rearrange(
            "p (c n) -> p c n", c=chunks)

        marks = {}
        ring = peer("ring").rearrange("p (k d) -> p k d", k=RING)
        keys = peer("keys").rearrange("p (k d) -> p k d", k=2 * P_HEADS)
        keyst = peer("keyst").rearrange("p (k d) -> p k d", k=2 * P_HEADS)
        keysc = peer("sc").rearrange("p (k n) -> p k n", k=2 * P_HEADS)
        qz = peer("qz").rearrange("p (s c) -> p s c", s=2)
        cand, hot, top, topf, ctop = (peer(n) for n in ("cand", "hot", "top", "topf", "ctop"))
        topi, ctopi = peer("topi").bitcast(U32), peer("ctopi").bitcast(U32)
        i1 = peer("i1").bitcast(U32)
        sel1, sel2, dots, hr, acc, zero, dot8 = (peer(n) for n in ("sel1", "sel2", "dots", "hr", "acc", "zero", "dot8"))
        idx = peer("idx").bitcast(I32).rearrange("p (t k) -> p t k", t=3)
        wgt = peer("wgt").rearrange("p (t k) -> p t k", t=3)
        diag = peer("diag").rearrange("p (k d) -> p k d", k=RING)
        stage = peer("stage").bitcast(I32)

        settled = peer("settled")

        def turns_of(eng, t):
            if t < 2:
                with eng.Fori(0, TURNS[t]) as i:
                    yield i
            else:
                yield from range(TURNS[t])

        def pairs_of_turns(eng, t):
            if t < 2:
                with eng.Fori(0, TURNS[t] // 2) as i:
                    yield i
            else:
                yield from range(TURNS[t] // 2)

        newest = sb("newest", CC * 11)[:, :].rearrange("p (c k) -> p c k", c=CC)
        xsamp = sb("xsamp", CC * SAMPLES)[:, :].rearrange("p (c b) -> p c b", c=CC)
        qrep = mla("qrep").rearrange("p (h q k) -> p h q k", h=A_HEADS, q=4)
        qpb = sd[:, 288:320].rearrange("p (q h) -> p q h", q=4)

        def of_layer_out(ap, l):
            rest = "bcdef"[: len(ap.shape) - 1]
            return ap[(bass.ds(l, 1),) + (slice(None),) * len(rest)].rearrange(f"a {' '.join(rest)} -> (a {rest[0]}) {' '.join(rest[1:])}")

        def span(used):
            numbers = [s.num for s in used.values()]
            assert len(numbers) == max(numbers) - min(numbers) + 1
            return range(min(numbers), max(numbers) + 1)

        with nc.Block() as block:
            @block.sync
            def _(sp):
                sp.dma_start(consts[:, :], a["consts"]).then_inc(sem("first_loads"), 16)
                sp.dma_start(x[:, 0:2, :], a["x_prompt"].rearrange("o (t p) d -> p (o t) d", p=P)).then_inc(sem("first_loads"), 16)
                sp.wait_ge(sem("x_zeroed"), 1)
                sp.dma_start(x[0:SAMPLES, 2, :], a["x_sample"].rearrange("b o d -> (b o) d")).then_inc(sem("first_loads"), 16)
                with nc.allow_non_contiguous_dma(reason="page numbers, once"):
                    for b in range(SAMPLES):
                        sp.dma_start(page_idx[:, b:b + 1], bc(a["page_table"][b, :], 1, PIECES).rearrange(
                            "g (r o) -> g r o", o=1)).then_inc(sem("first_loads"), 16)
                sp.wait_ge(sem("first_loads"), 16 * (3 + SAMPLES))

            @block.vector
            def _(dve):
                dve.memset(x[:, 2, :], 0.0).then_inc(sem("x_zeroed"), 1)
                dve.memset(layer_off[:, :], 0.0).then_inc(sem("off_zeroed"), 1)
                dve.wait_ge(sem("first_loads"), 16 * (3 + SAMPLES))
                dve.tensor_copy(pagef[:, 0:SAMPLES], page_idx[:, 0:SAMPLES]).then_inc(sem("pagef"), 1)
                dve.wait_ge(sem("pagef"), 1)
                dve.tensor_scalar(pagef[:, SAMPLES:], pagef[:, 0:SAMPLES], float(PIECES), cst("piece"),
                                  ALU.mult, ALU.add).then_inc(sem("pagef"), 1)
                dve.wait_ge(sem("pagef"), 2)
        nc.all_engine_barrier(sems_to_clear=span(sems))

        with nc.Fori(0, layers) as layer:
            with nc.Block() as block:
                @block.tensor
                def _(pe):
                    wide = Ring(pe, sem("wide_full"), sem("wide_free"), (0, 1, 2, 3))
                    aux = Ring(pe, sem("aux_full"), sem("aux_free"), (4, 5, 6, 7))
                    state = {"n": 0, "fresh": False}
                    pe.nop().then_inc(sem("tensor_slots_used"), len(PE_SLOTS))

                    def next_block(chunks, cols, base=None):
                        n = state["n"]
                        pe.wait_ge(sem(f"block{n % 2}_loads"), (0 if base is None else base) + 16 * (n // 2 + 1))
                        state["n"] += 1
                        state["fresh"] = True
                        return wblock(n % 2, chunks, cols)

                    def product(dst, w, rhs, chunks, start=True, stop=True):
                        for c in range(chunks):
                            last = pe.matmul(dst, w(c), rhs(c), start=start and c == 0, stop=stop and c == chunks - 1)
                            if state["fresh"]:
                                last.then_inc(sem("blocks_begun"), 1)
                                state["fresh"] = False
                        return last

                    def turn(dst, src, rows):
                        return pe.transpose(dst, src, ident[0:rows, 0:rows])

                    def turn_narrow(dst, src, rows):
                        return pe.matmul(dst, src, ident[0:rows, 0:rows], start=True, stop=True)

                    def feature_major(src, chunks=DC):
                        for c in range(chunks):
                            b = aux.fill()
                            for t, (t0, rows) in enumerate(TILES):
                                last = turn(ps[:, b, t0:t0 + rows], src(t)[0:rows, :].rearrange("p (q c) -> p c q", c=chunks)[:, c, :], rows)
                            aux.filled(last)

                    pe.wait_ge(sem("vec_loads"), 48)
                    b = aux.fill()
                    aux.filled(turn(ps[:, b, 0:VEC_ROWS], ssd("vrows")[0:VEC_ROWS, :], VEC_ROWS))
                    pe.wait_ge(sem("h_ready"), 1)
                    feature_major(lambda t: h[:, t, :])
                    aux.all_emptied()

                    with pe.Fori(0, MAIN_BLOCKS // 2) as i:
                        wide.enter(i, 4)
                        for k in range(2):
                            state["n"] = k
                            w = next_block(DC, BLOCK, base=i * 16)
                            for m in range(2):
                                b = wide.fill()
                                wide.filled(product(ps[:, b, 0:TOKENS], lambda c: w[:, c, m * P:(m + 1) * P], lambda c: ht[:, c, :], DC))
                    wide.leave(MAIN_BLOCKS // 2)
                    state["n"] = MAIN_BLOCKS
                    marks["main"] = wide.n
                    pe.wait_ge(sem("cstate_load"), 16)
                    b = aux.fill()
                    for c in range(CC):
                        last = turn(ps[:, b, c * 24:c * 24 + 24], ssd("cstate")[0:24, c * P:(c + 1) * P], 24)
                    aux.filled(last)
                    for first, cols in TAIL:
                        w = next_block(DC, cols)
                        for t0, rows in TILES:
                            b = wide.fill()
                            wide.filled(product(ps[0:rows, b, 0:cols], lambda c: ht[:, c, t0:t0 + rows], lambda c: w[:, c, :], DC))
                    marks["tail"] = wide.n

                    aux.all_emptied()
                    pe.wait_ge(sem("wide_free"), 4 + marks["main"])
                    pe.wait_ge(sem("newest_ready"), 1)
                    for q in range(3):
                        b = aux.fill()
                        for c in range(4 * q, 4 * q + 4):
                            last = turn(ps[0:11, b, (c % 4) * P:(c % 4 + 1) * P], newest[:, c, :], P)
                        aux.filled(last)
                    pe.wait_ge(sem("conv_ready"), 1)
                    for t, (t0, rows) in enumerate(TILES):
                        for q in range(2):
                            b = aux.fill()
                            for c in range(4 * q, 4 * q + 4):
                                src = conv[:, c, t0:t0 + rows] if t < 2 else xsamp[:, c, :]
                                last = turn(ps[0:rows, b, (c % 4) * P:(c % 4 + 1) * P], src, P)
                            aux.filled(last)
                    b = aux.fill()
                    for t in range(2):
                        for g in range(GROUPS):
                            last = turn(ps[:, b, (2 * t + g) * P:(2 * t + g + 1) * P], conv[:, DC + g, t * P:(t + 1) * P], P)
                    aux.filled(last)
                    b = aux.fill()
                    for c in range(4):
                        last = turn(ps[0:SAMPLES, b, c * P:(c + 1) * P], xsamp[:, DC + c, :], P)
                    aux.filled(last)
                    pe.wait_ge(sem("z_ready"), 1)
                    for t, (t0, rows) in enumerate(TILES):
                        for q in range(2):
                            b = aux.fill()
                            for c in range(4 * q, 4 * q + 4):
                                last = turn(ps[0:rows, b, (c % 4) * P:(c % 4 + 1) * P], zt[:, c, t0:t0 + rows], P)
                            aux.filled(last)
                    b = aux.fill()
                    for t in range(2):
                        for g in range(GROUPS):
                            last = pe.matmul(ps[:, b, (2 * t + g) * P:(2 * t + g + 1) * P], conv[:, DC + g, t * P:(t + 1) * P],
                                             conv[:, DC + GROUPS + g, t * P:(t + 1) * P], start=True, stop=True)
                    aux.filled(last)
                    pe.wait_ge(sem("dta_ready"), 1)
                    b = aux.fill()
                    for t in range(2):
                        pe.matmul(ps[:, b, 32 * t:32 * t + 16], triu, dta[:, t, :], start=True, stop=True)
                        last = pe.matmul(ps[:, b, 32 * t + 16:32 * t + 32], ones, dta[:, t, :], start=True, stop=True)
                    aux.filled(last)
                    pe.wait_ge(sem("xde_ready"), 1)
                    for g in range(GROUPS):
                        b = aux.fill()
                        aux.filled(pe.matmul(ps[:, b, :], bt[:, 0, g * P:(g + 1) * P], xde[:, g * 512:(g + 1) * 512], start=True, stop=True))
                    pe.wait_ge(sem("xdf_ready"), 1)
                    for q in range(2):
                        b = aux.fill()
                        for c in range(4 * q, 4 * q + 4):
                            g = c // 4
                            for t in range(2):
                                last = pe.matmul(ps[:, b, (c % 4) * P:(c % 4 + 1) * P], xdf[:, t, c * P:(c + 1) * P], bt[:, t, g * P:(g + 1) * P],
                                                 start=t == 0, stop=t == 1)
                        aux.filled(last)
                    for t in range(2):
                        for q in range(4):
                            b = wide.fill()
                            pe.matmul(ps[:, b, :].rearrange("p (k l) -> p k l", k=4), ident, bc(neg, 1, 4), start=True, stop=False, skip_group_check=True)
                            for k in range(4):
                                hh = 4 * q + k
                                last = pe.matmul(ps[:, b, k * P:(k + 1) * P], dta[:, t, hh:hh + 1].to_broadcast([P, P]), triu,
                                                 start=False, stop=k == 3, skip_group_check=True)
                            wide.filled(last)
                        for g in range(GROUPS):
                            pe.wait_ge(sem("mix_ready"), 2 * t + g + 1)
                            b = aux.fill()
                            for e in range(8):
                                hh = 8 * g + e
                                last = pe.matmul(ps[:, b, e * 64:(e + 1) * 64], el[:, hh, :], xdt[:, t, hh * 64:(hh + 1) * 64], start=True, stop=True)
                            aux.filled(last)
                            if t == 1:
                                b = aux.fill()
                                aux.filled(pe.matmul(ps[:, b, :], conv[:, DC + GROUPS + g, P:2 * P], hpt[:, g, :], start=True, stop=True))
                        if t == 0:
                            marks["ydiag0"] = aux.n
                    pe.wait_ge(sem("da_ready"), 1)
                    b = aux.fill()
                    pe.matmul(ps[0:HEADS, b, 0:8], dt[0:SAMPLES, 2, :], ident[0:SAMPLES, 0:SAMPLES], start=True, stop=True)
                    aux.filled(pe.matmul(ps[0:HEADS, b, 8:16], eend[0:SAMPLES, 0, :], ident[0:SAMPLES, 0:SAMPLES], start=True, stop=True))
                    aux.all_emptied()
                    b = aux.fill()
                    for hh in range(HEADS):
                        c, lo = hh // 2, 64 * (hh % 2)
                        last = pe.matmul(ps[lo:lo + 64, b, c * 16:(c + 1) * 16], ident[0:HEADS, hh:hh + 1].to_broadcast([HEADS, 64]),
                                         dtt[0:HEADS, 0:16], start=True, stop=True)
                    aux.filled(last)
                    for s in range(SAMPLES):
                        for ring_, lo in ((wide, 0), (aux, 256)):
                            b = ring_.fill()
                            ring_.filled(pe.matmul(ps[:, b, 0:256], ident[0:SAMPLES, s:s + 1].to_broadcast([SAMPLES, P]), bcs[0:SAMPLES, lo:lo + 256], start=True, stop=True))
                    pe.wait_ge(sem("ys_ready"), 1)
                    for q in range(2):
                        b = aux.fill()
                        for c in range(4 * q, 4 * q + 4):
                            last = turn(ps[0:SAMPLES, b, (c % 4) * P:(c % 4 + 1) * P], ysm3[:, c, :], P)
                        aux.filled(last)
                    pe.wait_ge(sem("y_ready"), 1)
                    feature_major(lambda t: y[:, t, :])
                    aux.all_emptied()
                    for k in range(4):
                        w = next_block(DC, BLOCK)
                        for m in range(2):
                            b = aux.fill()
                            aux.filled(product(ps[:, b, 0:TOKENS], lambda c: w[:, c, m * P:(m + 1) * P], lambda c: yt[:, c, :], DC))
                    aux.all_emptied()
                    pe.nop().then_inc(sem("scan_done"), 1)

                    pe.wait_ge(sem("cq_ready"), 1)
                    feature_major(lambda t: tok[:, t, T_CQ:T_CKV], chunks=3)
                    pe.wait_ge(sem("lat_ready"), 1)
                    for c in range(2):
                        b = aux.fill()
                        for t, (t0, rows) in enumerate(TILES):
                            last = turn(ps[:, b, t0:t0 + rows], lat[0:rows, t, c * P:(c + 1) * P], rows)
                        aux.filled(last)
                    b = aux.fill()
                    for t, (t0, rows) in enumerate(TILES):
                        last = turn_narrow(ps[0:ROPE, b, t0:t0 + rows], kpe[0:rows, t, :], rows)
                    aux.filled(last)
                    pe.wait_ge(sem("wkv_load"), 16)
                    for q in range(4):
                        b = aux.fill()
                        for k in range(2):
                            for c in range(2):
                                hh = 2 * q + k
                                last = turn(ps[:, b, (2 * k + c) * P:(2 * k + c + 1) * P], wkv[:, c, hh * P:(hh + 1) * P], P)
                        aux.filled(last)
                    aux.all_emptied()
                    pe.wait_ge(sem("wqb_load"), 16)
                    for hh in range(A_HEADS):
                        b = wide.fill()
                        wide.filled(product(ps[0:NOPE, b, 0:TOKENS], lambda c: wqb[:, c, hh * 96:hh * 96 + NOPE], lambda c: cqt[:, c, :], 3))
                    for t0, rows in TILES:
                        b = wide.fill()
                        wide.filled(product(ps[0:rows, b, 0:256].rearrange("p (h k) -> p h k", h=A_HEADS), lambda c: cqt[:, c, t0:t0 + rows],
                                            lambda c: wqb[:, c, :].rearrange("p (h k) -> p h k", h=A_HEADS)[:, :, NOPE:96], 3))
                    marks["q"] = wide.n
                    wide.all_emptied()
                    for c in range(2):
                        for hh in range(A_HEADS):
                            b = wide.fill()
                            wide.filled(pe.matmul(ps[:, b, 0:TOKENS], wkt[0:NOPE, hh, c * P:(c + 1) * P], qnt[0:NOPE, hh, :], start=True, stop=True))
                    pe.wait_ge(sem("qpe_ready"), 1)
                    for hh in range(A_HEADS):
                        b = aux.fill()
                        for t, (t0, rows) in enumerate(TILES):
                            last = turn_narrow(ps[0:ROPE, b, t0:t0 + rows], qpe[0:rows, t, hh, :], rows)
                        aux.filled(last)
                    b = aux.fill()
                    for hh in range(A_HEADS):
                        last = pe.matmul(ps[:, b, hh * 8:hh * 8 + 8], qrep[0:SAMPLES, hh, :, :].rearrange("p q k -> p (q k)"), ident[0:SAMPLES, 0:SAMPLES], start=True, stop=True)
                    aux.filled(last)
                    wide.all_emptied()
                    aux.all_emptied()
                    pe.nop().then_inc(sem("queries_done"), 1)

                    for t in range(2):
                        width = P * (t + 1)
                        for q in range(4):
                            b = aux.fill()
                            for k in range(2):
                                hh = 2 * q + k
                                dst = ps[:, b, k * 256:k * 256 + width]
                                for c in range(2):
                                    pe.matmul(dst, ql[:, c, hh, t * P:(t + 1) * P], latt[:, c, 0:width], start=c == 0, stop=False)
                                last = pe.matmul(dst, qpt[0:ROPE, hh, t * P:(t + 1) * P], kpet[0:ROPE, 0:width], start=False, stop=True)
                            aux.filled(last)
                        pe.wait_ge(sem("probs_ready"), t + 1)
                        for k in range(t + 1):
                            for q in range(2):
                                b = aux.fill()
                                for hh in range(4 * q, 4 * q + 4):
                                    last = turn(ps[:, b, (hh % 4) * P:(hh % 4 + 1) * P], sc[:, hh, k * P:(k + 1) * P], P)
                                aux.filled(last)
                        aux.all_emptied()
                        for c in range(2):
                            for q in range(2):
                                b = aux.fill()
                                for k in range(t + 1):
                                    last = pe.matmul(ps[:, b, :], lat[:, k, c * P:(c + 1) * P], pt[:, k, 4 * q:4 * q + 4, :], start=k == 0, stop=k == t)
                                aux.filled(last)
                    aux.all_emptied()

                    def page_transposes(s):
                        for n, (c, q) in enumerate([(c, q) for c in range(2) for q in range(4)]):
                            ring_ = aux if n % 2 == 0 else wide
                            b = ring_.fill()
                            for j in range(4 * q, 4 * q + 4):
                                last = turn(ps[:, b, (j % 4) * P:(j % 4 + 1) * P], ck[:, s, j, c * P:(c + 1) * P], P)
                            ring_.filled(last)
                            yield
                        b = aux.fill()
                        for q in range(4):
                            last = turn(ps[:, b, q * P:(q + 1) * P], cr[:, s, 4 * q:4 * q + 4, :].rearrange("p j r -> p (j r)"), P)
                        aux.filled(last)
                        yield

                    def sample(s, turn_no, more):
                        rest = page_transposes(1 - s) if more else iter(())

                        def some(n):
                            for _ in range(n):
                                next(rest, None)
                        aux.all_emptied()
                        wide.all_emptied()
                        pe.wait_ge(sem("qb_ready"), turn_no * 2 + s + 1)
                        b = aux.fill()
                        for c in range(2):
                            pe.matmul(ps[0:A_HEADS, b, 0:SAMPLES], qb[:, c, :], latt[:, c, SEQ:TOKENS], start=c == 0, stop=False)
                        aux.filled(pe.matmul(ps[0:A_HEADS, b, 0:SAMPLES], qpb[0:ROPE, 0, :], kpet[0:ROPE, SEQ:TOKENS], start=False, stop=True))
                        for q in range(4):
                            b = aux.fill()
                            for c in range(2):
                                pe.matmul(ps[0:A_HEADS, b, :], qb[:, c, :], kt[:, c, 4 * q:4 * q + 4, :], start=c == 0, stop=False, skip_group_check=True)
                            for j in range(4):
                                last = pe.matmul(ps[0:A_HEADS, b, j * P:(j + 1) * P], qpb[:, j, :], krt[:, q, :], start=False, stop=j == 3, skip_group_check=True)
                            aux.filled(last)
                        if more:
                            pe.wait_ge(sem(f"pages{1 - s}_loads"), turn_no * 32 + (32 if s == 0 else 64))
                        some(7)
                        pe.wait_ge(sem("sample_exp"), turn_no * 2 + s + 1)
                        b = aux.fill()
                        for j in range(PIECE):
                            (turn if j else turn_narrow)(ps[:, b, j * 8:j * 8 + 8], srow[0:A_HEADS, j * P:(j + 1) * P], A_HEADS)
                        aux.filled(turn(ps[0:SAMPLES, b, 128:136], srow[0:A_HEADS, PAST:PAST + SAMPLES], A_HEADS))
                        some(2)
                        aux.all_emptied()
                        b = aux.fill()
                        for j in range(PIECE):
                            pe.matmul(ps[0:A_HEADS, b, 0:KV_LORA], sexp[:, j, :], ck[:, s, j, :], start=j == 0, stop=False)
                        aux.filled(pe.matmul(ps[0:A_HEADS, b, 0:KV_LORA], sexp[0:SAMPLES, 16, :], lat[0:SAMPLES, 2, :], start=False, stop=True))

                    pe.wait_ge(sem("pages0_loads"), 32)
                    for _ in page_transposes(0):
                        pass
                    marks["att"] = aux.n
                    with pe.Fori(0, SAMPLES // 2 - 1) as i:
                        aux.enter(i, 24)
                        wide.enter(i, 8)
                        for s in range(2):
                            sample(s, i, True)
                    aux.leave(SAMPLES // 2 - 1)
                    wide.leave(SAMPLES // 2 - 1)
                    for s in range(2):
                        sample(s, SAMPLES // 2 - 1, s == 0)
                    aux.all_emptied()
                    b = aux.fill()
                    for c in range(2):
                        for s in range(SAMPLES):
                            at = (c * SAMPLES + s) * A_HEADS
                            last = turn(ps[:, b, at:at + A_HEADS], osamp[0:A_HEADS, s * KV_LORA + c * P:s * KV_LORA + (c + 1) * P], A_HEADS)
                    aux.filled(last)
                    aux.all_emptied()

                    for q in range(4):
                        b = aux.fill()
                        for k in range(2):
                            hh = 2 * q + k
                            for c in range(2):
                                last = pe.matmul(ps[k * 64:k * 64 + 64, b, 0:TOKENS], wkv[:, c, hh * P + NOPE:(hh + 1) * P], ol[:, c, hh, :],
                                                 start=c == 0, stop=c == 1)
                        aux.filled(last)
                    aux.all_emptied()
                    for k in range(2):
                        w = next_block(4, 2 * BLOCK)
                        for m in range(4):
                            b = aux.fill()
                            aux.filled(product(ps[:, b, 0:TOKENS], lambda c: w[:, c, m * P:(m + 1) * P], lambda c: ot[:, c, :], 4))
                    pe.wait_ge(sem("mixed"), 1)
                    for k in range(4):
                        w = next_block(DC, BLOCK)
                        for t0, rows in TILES:
                            b = aux.fill()
                            aux.filled(product(ps[0:rows, b, 0:BLOCK], lambda c: gate[:, c, t0:t0 + rows], lambda c: w[:, c, :], DC))
                    aux.all_emptied()
                    pe.nop().then_inc(sem("attention_done"), 1)

                    pe.wait_ge(sem("keys_load"), 16)
                    for q in range(4):
                        b = aux.fill()
                        for k in range(4 * q, 4 * q + 4):
                            last = turn(ps[:, b, (k % 4) * P:(k % 4 + 1) * P], keys[:, k, :], P)
                        aux.filled(last)
                    pe.wait_ge(sem("ph_ready"), 1)
                    feature_major(lambda t: h[:, t, :])
                    for half in range(2):
                        b = aux.fill()
                        aux.filled(pe.matmul(ps[0:64, b, :], cst("rep")[0:SAMPLES, :], h[0:SAMPLES, 2, half * 512:(half + 1) * 512], start=True, stop=True))
                    aux.all_emptied()
                    first = state["n"]
                    marks["wq_block"] = first
                    with pe.Fori(0, 4) as i:
                        wide.enter(i, 4)
                        for k in range(2):
                            state["n"] = first + k
                            w = next_block(DC, BLOCK, base=i * 16)
                            for m in range(2):
                                b = wide.fill()
                                wide.filled(product(ps[:, b, 0:TOKENS], lambda c: w[:, c, m * P:(m + 1) * P], lambda c: ht[:, c, :], DC))
                    wide.leave(4)
                    marks["wq"] = wide.n
                    wide.all_emptied()
                    pe.wait_ge(sem("qz_ready"), 1)
                    b = wide.fill()
                    for half in range(2):
                        for hh in range(P_HEADS):
                            last = pe.matmul(ps[0:64, b, half * P:(half + 1) * P], qz[:, half, hh * 64:(hh + 1) * 64], keyst[:, 2 * hh + half, :],
                                             start=hh == 0, stop=hh == P_HEADS - 1)
                    wide.filled(last)
                    for t in range(2):
                        for q in range(4):
                            b = wide.fill()
                            for k in range(4 * q, 4 * q + 4):
                                last = pe.matmul(ps[:, b, (k % 4) * P:(k % 4 + 1) * P], gate[:, k, t * P:(t + 1) * P], keyst[:, k, :], start=True, stop=True)
                            wide.filled(last)
                    for t in ORDER:
                        rows, outs = (P, P) if t < 2 else (64, SAMPLES)
                        banks = [aux.fill(), aux.fill(1)]
                        pe.wait_ge(sem("zero_ready"), 1)
                        for half in range(2):
                            pe.matmul(ps[0:outs, banks[half], :], zero[0:rows, 0:outs], consts[0:rows, 0:512], start=True, stop=False, skip_group_check=True)
                        for i in turns_of(pe, t):
                            for n, k in enumerate(PE_SLOTS):
                                pe.wait_ge(sem("diag_ready"), i * len(PE_SLOTS) + (PE_USES[t] + n + 1))
                                pe.wait_ge(sem(f"slot{k}_loads"), i * 16 + 16 * (V_USES[t] + 1))
                                for half in range(2):
                                    last = pe.matmul(ps[0:outs, banks[half], :], diag[0:rows, k, 0:outs], ring[0:rows, k, half * 512:(half + 1) * 512],
                                                     start=False, stop=False, skip_group_check=True)
                                last.then_inc(sem("tensor_slots_used"), 1)
                        pe.wait_ge(sem("acc_ready"), PLACE[t] + 1)
                        close = ident if t < 2 else cst("mod8")
                        for half in range(2):
                            aux.filled(pe.matmul(ps[0:outs, banks[half], :], close[0:rows, 0:outs], acc[0:rows, half * 512:(half + 1) * 512],
                                                 start=False, stop=True, skip_group_check=True))

                @block.vector
                def _(dve):
                    aux = Ring(dve, sem("aux_full"), sem("aux_free"), (4, 5, 6, 7))
                    own = Own(dve, sem("vector_steps"))
                    then = own.then
                    dve.nop().then_inc(sem("aux_free"), 4)
                    dve.nop().then_inc(sem("rows_dotted"), RING)
                    dve.nop().then_inc(sem("vector_slots_used"), len(VECTOR_SLOTS))

                    def copy_out(dst, cols, rows=P):
                        b = aux.read()
                        aux.emptied(dve.tensor_copy(dst, ps[0:rows, b, 0:cols]))

                    def copy4(dst, rows=P):
                        copy_out(dst, 512, rows)

                    def rstd(total, mean, root, inverse, width, square_sem, root_sem):
                        dve.wait_ge(sem(square_sem), 1)
                        dve.tensor_scalar(mean, total, 1.0 / width, EPS, ALU.mult, ALU.add).then_inc(sem(square_sem + "_mean"), 1)
                        dve.wait_ge(sem(root_sem), 1)
                        then(dve.reciprocal(inverse, root))

                    then(dve.memset(pad[:, :, 0:PAD], 0.0))
                    dve.memset(xt[:, 2, :], 0.0)
                    then(dve.memset(y[:, 2, :], 0.0))
                    b = aux.read()
                    aux.emptied(dve.tensor_copy(vt[:, :], ps[:, b, 0:VEC_ROWS]), wait=True)
                    dve.nop().then_inc(sem("vt_ready"), 1)
                    rstd(ss, ss, rt, rs, D_MODEL, "x_squares", "x_root")
                    dve.wait_ge(sem("nrow_load"), 16)
                    for t in range(3):
                        last = dve.scalar_tensor_tensor(out=h[:, t, :], in0=x[:, t, :], scalar=rs[:, t:t + 1], in1=nrow[:, :], op0=ALU.mult, op1=ALU.mult)
                    last.then_inc(sem("h_ready"), 1)
                    for c in range(DC):
                        copy_out(ht[:, c, :], TOKENS)
                    dve.memset(tok[:, 2, :], 0.0).then_inc(sem("tok_zeroed"), 1)
                    dve.nop().then_inc(sem("nrow_used"), 1)

                    dve.wait_ge(sem("z_sigmoid"), 1)
                    dve.tensor_tensor(zt, zt, zsig, ALU.mult).then_inc(sem("z_ready"), 1)
                    b = aux.read()
                    aux.emptied(dve.tensor_copy(pad_s[:, :, :, 0:PAD], ps[:, b, 0:24 * CC].rearrange("p (c b k) -> p c b k", c=CC, b=SAMPLES)), wait=True)
                    dve.wait_ge(sem("wide_free"), 4 + marks["main"])
                    dve.tensor_copy(newest[:, :, 0:PAD], pad[:, :, SEQ:SEQ + PAD])
                    dve.tensor_copy(newest[:, :, PAD:], pad_s[:, :, :, PAD]).then_inc(sem("newest_ready"), 1)
                    with dve.Fori(0, CC // 4) as i:
                        for k in range(CONV):
                            for q in range(4):
                                c = i * 4 + q
                                dst = conv[:, bass.ds(c, 1), 0:CONV_OUT]
                                if k == 0:
                                    last = dve.tensor_scalar(dst, pad[:, bass.ds(c, 1), 0:CONV_OUT], vt[:, bass.ds(c, 1)], vt[:, bass.ds(c + CONV * CC, 1)], ALU.mult, ALU.add)
                                else:
                                    dve.wait_ge(sem("taps_added"), i * 4 * CONV + (4 * k - 3 + q))
                                    last = dve.scalar_tensor_tensor(out=dst, in0=pad[:, bass.ds(c, 1), k:k + CONV_OUT], scalar=vt[:, bass.ds(c + k * CC, 1)],
                                                                    in1=dst, op0=ALU.mult, op1=ALU.add)
                                last.then_inc(sem("taps_added"), 1)
                    dve.wait_ge(sem("taps_added"), CC * CONV)
                    dve.nop().then_inc(sem("conv_raw"), 1)
                    dve.wait_ge(sem("wide_free"), 4 + marks["tail"])
                    dve.wait_ge(sem("head_loads"), 96)
                    then(dve.tensor_tensor(dtu, tok[:, :, 0:HEADS], bc(hd[:, 0:HEADS], 1, 3), ALU.add))
                    dve.scalar_tensor_tensor(out=dte, in0=dtu, scalar=-1.0, in1=dtu, op0=ALU.mult, op1=ALU.max).then_inc(sem("abs_ready"), 1)
                    dve.wait_ge(sem("dt_exp"), 1)
                    dve.tensor_scalar(dtw, dte, 1.0, None, ALU.add).then_inc(sem("dtw_ready"), 1)
                    dve.wait_ge(sem("dtw_ready"), 1)
                    then(dve.tensor_scalar(dtd, dtw, 1.0, None, ALU.subtract))
                    then(dve.tensor_tensor(dtd, dte, dtd, ALU.subtract))
                    then(dve.reciprocal(dti, dtw))
                    then(dve.tensor_tensor(dtd, dtd, dti, ALU.mult))
                    dve.wait_ge(sem("dt_log"), 1)
                    then(dve.tensor_tensor(dtl, dtl, dtd, ALU.add))
                    then(dve.scalar_tensor_tensor(out=dt, in0=dtu, scalar=0.0, in1=dtl, op0=ALU.max, op1=ALU.add))
                    dve.scalar_tensor_tensor(out=dta, in0=dt, scalar=-1.0, in1=bc(hd[:, HEADS:2 * HEADS], 1, 3), op0=ALU.mult, op1=ALU.mult).then_inc(sem("dta_ready"), 1)
                    for q in range(3):
                        b = aux.read()
                        aux.emptied(dve.tensor_copy(rawt[0:11, q * 512:(q + 1) * 512], ps[0:11, b, :]), wait=True)
                    dve.nop().then_inc(sem("rawt_ready"), 1)
                    dve.wait_ge(sem("conv_sigmoid"), 1)
                    then(dve.tensor_tensor(conv[:, :, 0:CONV_OUT], conv[:, :, 0:CONV_OUT], sig[:, :, 0:CONV_OUT], ALU.mult))
                    dve.tensor_copy(xsamp, conv_s[:, :, :, 0]).then_inc(sem("conv_ready"), 1)
                    for t, (t0, rows) in enumerate(TILES):
                        for q in range(2):
                            copy4(xt[0:rows, t, q * 512:(q + 1) * 512], rows)
                    copy4(bt.rearrange("p t n -> p (t n)"))
                    copy4(bcs[0:SAMPLES, :], SAMPLES)
                    for t, (t0, rows) in enumerate(TILES):
                        for q in range(2):
                            copy4(h[0:rows, t, q * 512:(q + 1) * 512], rows)
                    copy4(cb.rearrange("p k l -> p (k l)"))
                    b = aux.read()
                    aux.emptied(dve.tensor_copy(acs[:, :], ps[:, b, 0:64]), wait=True)
                    then(dve.tensor_tensor(dec, a_cs[:, :, 1, :], a_cs[:, :, 0, :], ALU.subtract))
                    dve.tensor_scalar(nacs, a_cs[:, :, 0, :], -1.0, None, ALU.mult)
                    dve.tensor_tensor(decf[:, 0, :], dec[:, 0, :], a_cs[:, 1, 1, :], ALU.add)
                    dve.tensor_copy(decf[:, 1, :], dec[:, 1, :]).then_inc(sem("decays_raw"), 1)
                    dve.wait_ge(sem("rawt_stored"), 1)
                    heads = lambda ap: ap.rearrange("p (h k) -> p h k", h=HEADS)
                    for t in range(2):
                        then(dve.tensor_tensor(heads(xdt[:, t, :]), heads(xt[:, t, :]), bc(dt[:, t, :], 2, 64), ALU.mult))
                    dve.wait_ge(sem("decays_ready"), 1)
                    dve.tensor_tensor(heads(xde), heads(xdt[:, 0, :]), bc(dec[:, 0, :], 2, 64), ALU.mult).then_inc(sem("xde_ready"), 1)
                    for t in range(2):
                        last = dve.tensor_tensor(heads(xdf[:, t, :]), heads(xdt[:, t, :]), bc(decf[:, t, :], 2, 64), ALU.mult)
                    last.then_inc(sem("xdf_ready"), 1)
                    for g in range(GROUPS):
                        copy4(hpt[:, g, :])
                    for q in range(2):
                        b = aux.read()
                        aux.emptied(dve.tensor_copy(hs[:, q * 512:(q + 1) * 512], ps[:, b, :]), wait=True)
                    dve.nop().then_inc(sem("hs_ready"), 1)
                    for t in range(3):
                        then(dve.tensor_tensor(heads(y[:, t, :]), heads(xt[:, t, :]), bc(hd[:, 2 * HEADS:3 * HEADS], 2, 64), ALU.mult))
                    for t in range(2):
                        for g in range(GROUPS):
                            dve.wait_ge(sem("wide_free"), 4 + marks["tail"] + 4 * t + 2 * g + 2)
                            dve.tensor_tensor(el[:, 8 * g:8 * g + 8, :], el[:, 8 * g:8 * g + 8, :], bc(cb[:, 2 * t + g, :], 1, 8), ALU.mult).then_inc(sem("mix_ready"), 1)
                        for g in range(GROUPS):
                            yg = y[:, t, g * 512:(g + 1) * 512]
                            b = aux.read()
                            aux.emptied(dve.tensor_tensor(yg, yg, ps[:, b, :], ALU.add), wait=True)
                            if t == 1:
                                b = aux.read()
                                aux.emptied(dve.tensor_tensor(xt[:, 1, g * 512:(g + 1) * 512].rearrange("p (e k) -> p e k", e=8),
                                                              ps[:, b, :].rearrange("p (e k) -> p e k", e=8), bc(ea[:, 1, 8 * g:8 * g + 8], 2, 64), ALU.mult), wait=True)
                                then(dve.tensor_tensor(yg, yg, xt[:, 1, g * 512:(g + 1) * 512], ALU.add))
                    dve.nop().then_inc(sem("el_used"), 1)
                    b = aux.read()
                    aux.emptied(dve.tensor_copy(dtt[0:HEADS, 0:16], ps[0:HEADS, b, 0:16]))
                    b = aux.read()
                    aux.emptied(dve.tensor_copy(exs[:, :], ps[:, b, 0:DC * 16]), wait=True)
                    then(dve.tensor_tensor(dtx3, xsamp[:, 0:DC, :], exs4[:, :, 0, :], ALU.mult))
                    dve.nop().then_inc(sem("dtx_ready"), 1)
                    per_group = lambda ap: ap.rearrange("p (g c n) -> p g c n", g=GROUPS, c=4)
                    for s in range(SAMPLES):
                        b = aux.read()
                        cmat = bc(ps[:, b, 0:256].rearrange("p (g n) -> p g n", g=GROUPS), 2, 4)
                        new = places[s % 4]
                        dve.wait_ge(sem("state_decayed"), s + 1)
                        dve.tensor_tensor(new, new, stx[:, s % 2, :, :], ALU.add).then_inc(sem("state_ready"), 1)
                        dve.wait_ge(sem("state_ready"), s + 1)
                        aux.emptied(dve.tensor_tensor(per_group(stc), per_group(new.rearrange("p c n -> p (c n)")), cmat, ALU.mult), wait=True)
                        dve.tensor_reduce(ysm3[:, :, s:s + 1], stc.rearrange("p (c n) -> p c n", c=DC), AX.X, ALU.add).then_inc(sem("state_used"), 1)
                        dve.wait_ge(sem("state_used"), s + 1)
                    dve.nop().then_inc(sem("ys_ready"), 1)
                    for q in range(2):
                        b = aux.read()
                        yg = y[0:SAMPLES, 2, q * 512:(q + 1) * 512]
                        aux.emptied(dve.tensor_tensor(yg, yg, ps[0:SAMPLES, b, :], ALU.add), wait=True)
                    dve.tensor_tensor(y, y, h, ALU.mult).then_inc(sem("y_gated"), 1)
                    rstd(ss6, ss6, rt6, rs6, D_MODEL // GROUPS, "y_squares", "y_root")
                    for t in range(3):
                        for g in range(GROUPS):
                            yg = y[:, t, g * 512:(g + 1) * 512]
                            last = dve.tensor_scalar(yg, yg, rs6[:, 2 * t + g:2 * t + g + 1], None, ALU.mult)
                    last.then_inc(sem("y_ready"), 1)
                    for c in range(DC):
                        b = aux.read()
                        aux.emptied(dve.tensor_scalar(yt[:, c, :], ps[:, b, 0:TOKENS], ssmn[:, c:c + 1], None, ALU.mult))
                    for m in range(DC):
                        b = aux.read()
                        aux.emptied(dve.tensor_tensor(gate[:, m, :], gate[:, m, :], ps[:, b, 0:TOKENS], ALU.mult))

                    dve.wait_ge(sem("lat_squares"), 1)
                    lsq, lrt, lrs = st[:, 27:33], st[:, 33:39], st[:, 39:45]
                    dve.tensor_scalar(lsq[:, 0:3], lsq[:, 0:3], 1.0 / Q_LORA, EPS, ALU.mult, ALU.add)
                    dve.tensor_scalar(lsq[:, 3:6], lsq[:, 3:6], 1.0 / KV_LORA, EPS, ALU.mult, ALU.add).then_inc(sem("lat_squares_mean"), 1)
                    dve.wait_ge(sem("lat_root"), 1)
                    then(dve.reciprocal(lrs, lrt))
                    for t in range(3):
                        last = dve.tensor_scalar(tok[:, t, T_CQ:T_CKV], tok[:, t, T_CQ:T_CKV], lrs[:, t:t + 1], None, ALU.mult)
                    last.then_inc(sem("cq_ready"), 1)
                    for t in range(3):
                        dve.scalar_tensor_tensor(out=lat[:, t, :], in0=tok[:, t, T_CKV:T_KR], scalar=lrs[:, 3 + t:4 + t], in1=kvn[:, :], op0=ALU.mult, op1=ALU.mult)
                    x1, x2 = tok[:, :, T_KR:T_KR + 16], tok[:, :, T_KR + 16:TAIL_W]
                    r1, r2, r3, r4 = (dtb[:, 48 * k:48 * k + 48].rearrange("p (t k) -> p t k", t=3) for k in range(2, 6))
                    dve.tensor_tensor(r1, x1, cos, ALU.mult)
                    dve.tensor_tensor(r2, x2, sin, ALU.mult)
                    dve.tensor_tensor(r3, x1, sin, ALU.mult)
                    then(dve.tensor_tensor(r4, x2, cos, ALU.mult))
                    dve.tensor_tensor(kpe[:, :, 0:16], r1, r2, ALU.subtract)
                    dve.tensor_tensor(kpe[:, :, 16:32], r3, r4, ALU.add).then_inc(sem("lat_ready"), 1)
                    for c in range(3):
                        b = aux.read()
                        aux.emptied(dve.tensor_scalar(cqt[:, c, :], ps[:, b, 0:TOKENS], qn[:, c:c + 1], None, ALU.mult))
                    for c in range(2):
                        copy_out(latt[:, c, :], TOKENS)
                    b = aux.read()
                    aux.emptied(dve.tensor_copy(kpet[0:ROPE, :], ps[0:ROPE, b, 0:TOKENS]))
                    for q in range(4):
                        b = aux.read()
                        aux.emptied(dve.tensor_copy(wkt[0:NOPE, 2 * q:2 * q + 2, :].rearrange("p h r -> p (h r)"), ps[0:NOPE, b, :]))
                    dve.wait_ge(sem("wide_free"), 4 + marks["q"])
                    q1, q2 = qr[:, :, :, 0:16], qr[:, :, :, 16:32]
                    cosq, sinq = bc(cos, 2, A_HEADS), bc(sin, 2, A_HEADS)
                    for t in range(3):
                        rows = TILES[t][1]
                        dve.tensor_tensor(rtmp[0:rows, 0, t], q1[0:rows, t], cosq[0:rows, t], ALU.mult)
                        dve.tensor_tensor(rtmp[0:rows, 1, t], q2[0:rows, t], sinq[0:rows, t], ALU.mult)
                        dve.tensor_tensor(rtmp[0:rows, 2, t], q1[0:rows, t], sinq[0:rows, t], ALU.mult)
                        then(dve.tensor_tensor(rtmp[0:rows, 3, t], q2[0:rows, t], cosq[0:rows, t], ALU.mult))
                        dve.tensor_tensor(qpe[0:rows, t, :, 0:16], rtmp[0:rows, 0, t], rtmp[0:rows, 1, t], ALU.subtract)
                        last = dve.tensor_tensor(qpe[0:rows, t, :, 16:32], rtmp[0:rows, 2, t], rtmp[0:rows, 3, t], ALU.add)
                    then(last)
                    dve.tensor_copy(qrep[0:SAMPLES, :, :, :], bc(qpe[0:SAMPLES, 2, :, :], 2, 4)).then_inc(sem("qpe_ready"), 1)
                    for hh in range(A_HEADS):
                        b = aux.read()
                        aux.emptied(dve.tensor_copy(qpt[0:ROPE, hh, :], ps[0:ROPE, b, 0:TOKENS]))
                    b = aux.read()
                    for s in range(SAMPLES):
                        last = dve.tensor_tensor(qpad[:, s, :, :], bc(ps[:, b, 0:64].rearrange("p (h b) -> p b h", b=SAMPLES)[:, s, :], 1, 4),
                                                 bc(cst("quarter"), 2, A_HEADS), ALU.mult)
                    aux.emptied(last)

                    for t in range(2):
                        width = P * (t + 1)
                        for q in range(4):
                            b = aux.read()
                            src = ps[:, b, :].rearrange("p (k t) -> p k t", k=2)
                            if t == 1:
                                dve.tensor_copy(sc[:, 2 * q:2 * q + 2, 0:P], src[:, :, 0:P])
                            aux.emptied(dve.tensor_tensor(sc[:, 2 * q:2 * q + 2, t * P:width], src[:, :, t * P:width], bc(cst("causal"), 1, 2), ALU.add), wait=True)
                        scores = sc[:, :, 0:width]
                        then(dve.tensor_reduce(amax, scores, AX.X, ALU.max))
                        dve.tensor_scalar(anm, amax, -SCALE, None, ALU.mult).then_inc(sem("scores_max"), 1)
                        dve.wait_ge(sem("scores_exp"), t + 1)
                        then(dve.reciprocal(ainv, asum))
                        dve.tensor_tensor(scores, scores, bc(ainv, 2, width), ALU.mult).then_inc(sem("probs_ready"), 1)
                        for k in range(t + 1):
                            for q in range(2):
                                copy4(pt[:, k, 4 * q:4 * q + 4, :].rearrange("p h t -> p (h t)"))
                        for c in range(2):
                            for q in range(2):
                                b = aux.read()
                                aux.emptied(dve.tensor_copy(ol[:, c, 4 * q:4 * q + 4, t * P:(t + 1) * P], ps[:, b, :].rearrange("p (h t) -> p h t", h=4)))

                    def page_copies():
                        for n, (c, q) in enumerate([(c, q) for c in range(2) for q in range(4)]):
                            if n % 2 == 0:
                                copy4(kt[:, c, 4 * q:4 * q + 4, :].rearrange("p j t -> p (j t)"))
                                yield
                        copy4(krt.rearrange("p q t -> p (q t)"))
                        yield

                    def queries_of(token, number):
                        dve.tensor_copy(qb, ql[:, :, :, token].rearrange("p c h o -> p c (h o)"))
                        dve.tensor_copy(qpb, qpad[:, number, :, :].rearrange("p o q h -> p (o q) h")).then_inc(sem("qb_ready"), 1)

                    def sample(s, turn_no, more):
                        rest = page_copies() if more else iter(())
                        at = turn_no * 2 + s
                        b = aux.read()
                        mask = cst("newmask")[0:A_HEADS, bass.ds(at * SAMPLES, SAMPLES)]
                        dve.tensor_tensor(srow[0:A_HEADS, PAST:], ps[0:A_HEADS, b, 0:SAMPLES], mask, ALU.add)
                        aux.emptied(dve.tensor_tensor(smax[0:A_HEADS, 4:12], ps[0:A_HEADS, b, 0:SAMPLES], mask, ALU.add))
                        for q in range(4):
                            b = aux.read()
                            dve.tensor_copy(srow[0:A_HEADS, q * 512:(q + 1) * 512], ps[0:A_HEADS, b, :])
                            aux.emptied(dve.tensor_reduce(smax[0:A_HEADS, q:q + 1], ps[0:A_HEADS, b, :], AX.X, ALU.max), wait=q == 3)
                        then(dve.tensor_reduce(sbest[0:A_HEADS, :], smax[0:A_HEADS, :], AX.X, ALU.max))
                        dve.tensor_scalar(sneg[0:A_HEADS, :], sbest[0:A_HEADS, :], -SCALE, None, ALU.mult).then_inc(sem("max_ready"), 1)
                        if more:
                            queries_of(bass.ds(at + (SEQ + 1), 1), bass.ds(at + 1, 1))
                        for _ in range(4):
                            next(rest, None)
                        b = aux.read()
                        dve.tensor_copy(sexp[:, 0:16, :].rearrange("p j h -> p (j h)"), ps[:, b, 0:128])
                        aux.emptied(dve.tensor_copy(sexp[0:SAMPLES, 16, :], ps[0:SAMPLES, b, 128:136]))
                        next(rest, None)
                        dve.wait_ge(sem("sample_exp"), turn_no * 2 + s + 1)
                        then(dve.reciprocal(sinv[0:A_HEADS, :], ssum[0:A_HEADS, :]))
                        b = aux.read()
                        aux.emptied(dve.tensor_scalar(osamp[0:A_HEADS, bass.ds(at * KV_LORA, KV_LORA)], ps[0:A_HEADS, b, 0:KV_LORA], sinv[0:A_HEADS, :], None, ALU.mult))

                    queries_of(slice(SEQ, SEQ + 1), slice(0, 1))
                    for _ in page_copies():
                        pass
                    with dve.Fori(0, SAMPLES // 2 - 1) as i:
                        aux.enter(i, 24)
                        own.enter(i, 4)
                        for s in range(2):
                            sample(s, i, True)
                    own.leave(SAMPLES // 2 - 1)
                    aux.leave(SAMPLES // 2 - 1)
                    for s in range(2):
                        sample(s, SAMPLES // 2 - 1, s == 0)
                    b = aux.read()
                    aux.emptied(dve.tensor_copy(ol[:, :, :, SEQ:], ps[:, b, 0:2 * SAMPLES * A_HEADS].rearrange("p (c s h) -> p c h s", c=2, h=A_HEADS)))

                    for q in range(4):
                        copy_out(ot[:, q, :], TOKENS)
                    for m in range(DC):
                        b = aux.read()
                        aux.emptied(dve.tensor_tensor(gate[:, DC + m, :], gate[:, DC + m, :], ps[:, b, 0:TOKENS], ALU.mult), wait=True)
                    dve.tensor_tensor(gate[:, 0:DC, :], gate[:, 0:DC, :], gate[:, DC:, :], ALU.add).then_inc(sem("mixed"), 1)
                    for k in range(4):
                        for t, (t0, rows) in enumerate(TILES):
                            b = aux.read()
                            xs = x[0:rows, t, k * BLOCK:(k + 1) * BLOCK]
                            aux.emptied(dve.tensor_tensor(xs, xs, ps[0:rows, b, 0:BLOCK], ALU.add))

                    dve.wait_ge(sem("aux_free"), 4 + aux.n)
                    dve.nop().then_inc(sem("x_mixed"), 1)
                    dve.wait_ge(sem("attention_done"), 1)
                    dve.memset(zero, 0.0).then_inc(sem("zero_ready"), 1)
                    then(dve.memset(qz.rearrange("p s c -> p (s c)"), 0.0))
                    for q in range(4):
                        copy4(keyst[:, 4 * q:4 * q + 4, :].rearrange("p k d -> p (k d)"))
                    rstd(st[:, 45:48], st[:, 45:48], st[:, 48:51], st[:, 51:54], D_MODEL, "px_squares", "px_root")
                    dve.wait_ge(sem("ffn_row_load"), 16)
                    for t in range(3):
                        last = dve.scalar_tensor_tensor(out=h[:, t, :], in0=x[:, t, :], scalar=st[:, 51 + t:52 + t], in1=nrow[:, :], op0=ALU.mult, op1=ALU.mult)
                    last.then_inc(sem("ph_ready"), 1)
                    for c in range(DC):
                        copy_out(ht[:, c, :], TOKENS)
                    for half in range(2):
                        copy_out(hr[0:64, half * 512:(half + 1) * 512], 512, 64)
                    dve.wait_ge(sem("wide_free"), 4 + marks["wq"])
                    for half in range(2):
                        last = dve.tensor_copy(qz[:, half, :].rearrange("p (h r) -> p h r", r=72)[:, :, 0:SAMPLES],
                                               gate[:, :, SEQ:TOKENS].rearrange("p (h s) t -> p s h t", s=2)[:, half, :, :])
                    last.then_inc(sem("qz_ready"), 1)

                    def sixteen(*items):
                        for k in range(2):
                            eight = slice(8 * k, 8 * k + 8)
                            for best, where, values in items:
                                last = dve.max(best[:, eight], values)
                            then(last)
                            for best, where, values in items:
                                last = dve.max_index(where[:, eight], best[:, eight], values)
                            then(last)
                            if k == 0:
                                for best, where, values in items:
                                    last = dve.match_replace(values, best[:, eight], values, -3e38)
                                then(last)

                    def sixteen_of_two(i, best, where, values, width):
                        copy, top16, where16 = hot[:, 0:2 * width], hot[:, 1024:1024 + 2 * TOPK], i1[:, 0:2 * TOPK]
                        dve.tensor_copy(copy, values[:, bass.ds(i * 2 * width, 2 * width)])
                        dve.drain()
                        item = [copy[:, 0:width], copy[:, width:]]
                        for k in range(2):
                            eight = [slice(TOPK * n + 8 * k, TOPK * n + 8 * k + 8) for n in range(2)]
                            for n in range(2):
                                dve.max(top16[:, eight[n]], item[n])
                            dve.drain()
                            for n in range(2):
                                dve.max_index(where16[:, eight[n]], top16[:, eight[n]], item[n])
                            dve.drain()
                            if k == 0:
                                yield
                                for n in range(2):
                                    dve.match_replace(item[n], top16[:, eight[n]], item[n], -3e38)
                                dve.drain()
                        dve.tensor_copy(best[:, bass.ds(i * 2 * TOPK, 2 * TOPK)], top16)
                        dve.tensor_copy(where[:, bass.ds(i * 2 * TOPK, 2 * TOPK)], where16)
                        dve.drain()

                    def of_tile(t):
                        return (P, P_HEADS) if t < 2 else (64, 1)

                    def scores_there(t):
                        dve.wait_ge(sem("wide_free"), 4 + marks["wq"] + 1 + 4 * PLACE[t])

                    def best_keys(t):
                        rows, nh = of_tile(t)
                        for k0 in range(0, 2 * nh, 2):
                            sixteen(*[(top[0:rows, 16 * k:16 * k + 16], topi[0:rows, 16 * k:16 * k + 16], keysc[0:rows, k, :]) for k in (k0, k0 + 1)])

                    def pair_of(ap, t):
                        rows, nh = of_tile(t)
                        return ap[0:rows, 0:2 * nh * TOPK].rearrange("p (h s k) -> p s h k", s=2, k=TOPK)

                    def grid_of(ap, t):
                        rows, nh = of_tile(t)
                        return ap[0:rows, 0:nh * TOPK * TOPK].rearrange("p (h i j) -> p h i j", h=nh, i=TOPK)

                    def candidates(t):
                        rows, nh = of_tile(t)
                        dve.tensor_copy(topf[0:rows, 0:2 * nh * TOPK], topi[0:rows, 0:2 * nh * TOPK]).then_inc(sem("scores_used"), 1)
                        then(dve.tensor_tensor(grid_of(cand, t), bc(pair_of(top, t)[:, 0], 3, TOPK), bc(pair_of(top, t)[:, 1], 2, TOPK), ALU.add))

                    def best_pairs(t):
                        rows, nh = of_tile(t)
                        for k0 in range(0, nh, 2):
                            sixteen(*[(ctop[0:rows, 16 * k:16 * k + 16], ctopi[0:rows, 16 * k:16 * k + 16], cand[0:rows, 256 * k:256 * k + 256])
                                      for k in range(k0, min(k0 + 2, nh))])

                    def keys_of_pairs(t, n):
                        rows, nh = of_tile(t)
                        n16 = nh * TOPK
                        if n == 0:
                            best = ctop[0:rows, 0:n16].rearrange("p (h k) -> p h k", h=nh)
                            w = wgt[0:rows, t, 0:n16].rearrange("p (h k) -> p h k", h=nh)
                            dve.tensor_tensor(w, best, bc(best[:, :, 0], 2, TOPK), ALU.subtract).then_inc(sem("experts_shifted"), 1)
                            then(dve.tensor_scalar(i1[0:rows, 0:n16], ctopi[0:rows, 0:n16], 4, None, ALU.logical_shift_right))
                        else:
                            then(dve.tensor_scalar(i1[0:rows, 0:n16], ctopi[0:rows, 0:n16], 15, None, ALU.bitwise_and))
                        sel = (sel1, sel2)[n]
                        then(dve.tensor_copy(sel[0:rows, 0:n16], i1[0:rows, 0:n16]))
                        flat = sel[0:rows, 0:n16]
                        hot3 = hot[0:rows, 0:n16 * TOPK].rearrange("p (s j) -> p s j", j=TOPK)
                        then(dve.tensor_tensor(hot3, bc(flat, 2, TOPK), bc(cst("iota")[0:rows, :], 1, n16), ALU.is_equal))
                        yield
                        then(dve.tensor_tensor(grid_of(hot, t), grid_of(hot, t), bc(pair_of(topf, t)[:, n], 2, TOPK), ALU.mult))
                        yield
                        then(dve.tensor_reduce(flat, hot3, AX.X, ALU.add))
                        yield

                    def experts_and_weights(t):
                        rows, nh = of_tile(t)
                        n16 = nh * TOPK
                        w = wgt[0:rows, t, 0:n16].rearrange("p (h k) -> p h k", h=nh)
                        then(dve.scalar_tensor_tensor(out=sel1[0:rows, 0:n16], in0=sel1[0:rows, 0:n16], scalar=float(N_KEYS), in1=sel2[0:rows, 0:n16], op0=ALU.mult, op1=ALU.add))
                        then(dve.tensor_scalar(sel1[0:rows, 0:n16], sel1[0:rows, 0:n16], layer_off[0:rows, 1:2], None, ALU.add))
                        dve.tensor_copy(idx[0:rows, t, 0:n16], sel1[0:rows, 0:n16]).then_inc(sem("idx_ready"), 1)
                        dve.wait_ge(sem("idx_ready"), PLACE[t] + 1)
                        dve.wait_ge(sem("experts_exp"), PLACE[t] + 1)
                        then(dve.tensor_reduce(sel2[0:rows, 0:nh], w, AX.X, ALU.add))
                        then(dve.reciprocal(sel2[0:rows, 16:16 + nh], sel2[0:rows, 0:nh]))
                        then(dve.tensor_tensor(w, w, bc(sel2[0:rows, 16:16 + nh], 2, TOPK), ALU.mult))

                    def inputs_turn(t, i):
                        rows = P if t < 2 else 64
                        tokens = h[0:rows, t, :] if t < 2 else hr[0:rows, :]
                        if t < 2:
                            own.enter(i, 1)
                        for k in range(RING):
                            dve.wait_ge(sem(f"slot{k}_loads"), i * 16 + 16 * (U_USES[t] + 1))
                            dve.tensor_tensor_reduce(ring[0:rows, k, :], ring[0:rows, k, :], tokens, 1.0, 0.0, ALU.mult, ALU.add,
                                                     dot8[0:rows, k:k + 1]).then_inc(sem("rows_dotted"), 1)
                        dve.wait_ge(sem("rows_dotted"), i * RING + (U_DONE[t] + RING))
                        then(dve.tensor_copy(dots[0:rows, bass.ds(i * RING, RING)], dot8[0:rows, :]))

                    def outputs_turn(t, i, between=iter(())):
                        rows, table, outs = (P, ident, P) if t < 2 else (64, cst("mod8"), SAMPLES)
                        for n, k in enumerate(PE_SLOTS):
                            dve.wait_ge(sem("tensor_slots_used"), i * len(PE_SLOTS) + (PE_USES[t] + n + 1))
                            dve.tensor_scalar(diag[0:rows, k, 0:outs], table[0:rows, 0:outs], wgt[0:rows, t, bass.ds(i * RING + k, 1)], None, ALU.mult).then_inc(sem("diag_ready"), 1)
                        for n, k in enumerate(VECTOR_SLOTS):
                            dve.wait_ge(sem(f"slot{k}_loads"), i * 16 + 16 * (V_USES[t] + 1))
                            dve.wait_ge(sem("vector_slots_used"), i * len(VECTOR_SLOTS) + (VECTOR_USES[t] + len(VECTOR_SLOTS) + n))
                            dve.scalar_tensor_tensor(out=acc[0:rows, :], in0=ring[0:rows, k, :], scalar=wgt[0:rows, t, bass.ds(i * RING + k, 1)],
                                                     in1=acc[0:rows, :], op0=ALU.mult, op1=ALU.add).then_inc(sem("vector_slots_used"), 1)
                            next(between, None)

                    def activations(t):
                        rows, n16 = (P, P) if t < 2 else (64, TOPK)
                        dve.nop().then_inc(sem("dots_ready"), 1)
                        dve.wait_ge(sem("gelu_ready"), PLACE[t] + 1)
                        then(dve.tensor_tensor(wgt[0:rows, t, 0:n16], wgt[0:rows, t, 0:n16], dots[0:rows, 0:n16], ALU.mult))

                    def tile_sum(t):
                        dve.wait_ge(sem("vector_slots_used"), VECTOR_USES[t] + len(VECTOR_SLOTS) * (TURNS[t] + 1))
                        dve.nop().then_inc(sem("acc_ready"), 1)
                        for half in range(2):
                            b = aux.read()
                            r = P if t < 2 else SAMPLES
                            xs = x[0:r, t, half * 512:(half + 1) * 512]
                            aux.emptied(dve.tensor_tensor(xs, xs, ps[0:r, b, :], ALU.add), wait=True)

                    def run(steps):
                        for _ in steps:
                            pass

                    scores_there(2)
                    best_keys(2)
                    candidates(2)
                    best_pairs(2)
                    run(keys_of_pairs(2, 0))
                    run(keys_of_pairs(2, 1))
                    experts_and_weights(2)
                    then(dve.memset(acc[0:64, :], 0.0))
                    scores_there(0)
                    best_keys(0)
                    inputs_turn(2, 0)
                    candidates(0)
                    inputs_turn(2, 1)
                    activations(2)
                    best_pairs(0)
                    outputs_turn(2, 0)
                    run(keys_of_pairs(0, 0))
                    run(keys_of_pairs(0, 1))
                    outputs_turn(2, 1)
                    experts_and_weights(0)
                    tile_sum(2)

                    for t in range(2):
                        then(dve.memset(acc, 0.0))
                        with dve.Fori(0, TURNS[t]) as i:
                            inputs_turn(t, i)
                        own.leave(TURNS[t])
                        activations(t)
                        if t == 0:
                            scores_there(1)
                            with dve.Fori(0, P_HEADS) as i:
                                outputs_turn(0, i, sixteen_of_two(i, top, topi, keysc.rearrange("p k n -> p (k n)"), N_KEYS))
                            candidates(1)
                            with dve.Fori(P_HEADS, TURNS[0] - REST) as i:
                                outputs_turn(0, i, sixteen_of_two(i - P_HEADS, ctop, ctopi, cand, TOPK * TOPK))
                            rest = chain(keys_of_pairs(1, 0), keys_of_pairs(1, 1))
                            for i in range(TURNS[0] - REST, TURNS[0]):
                                if i == TURNS[0] - 1:
                                    run(rest)
                                    experts_and_weights(1)
                                outputs_turn(0, i, rest)
                        else:
                            with dve.Fori(0, TURNS[1]) as i:
                                outputs_turn(1, i)
                        tile_sum(t)
                    then(dve.tensor_scalar(layer_off[:, 0:1], layer_off[:, 0:1], float(a["cache_latent"].shape[1] * PIECES), None, ALU.add))
                    then(dve.tensor_scalar(layer_off[:, 1:2], layer_off[:, 1:2], float(N_EXPERTS), None, ALU.add))

                @block.scalar
                def _(act):
                    wide = Ring(act, sem("wide_full"), sem("wide_free"), (0, 1, 2, 3))
                    act.nop().then_inc(sem("wide_free"), 4)

                    def squares(junk, src, total, last=None):
                        ins = act.activation(junk, src, ACT.Square, accum_out=total)
                        if last:
                            ins.then_inc(sem(last), 1)

                    def root(dst, mean, name):
                        act.wait_ge(sem(f"{name}_squares_mean"), 1)
                        act.activation(dst, mean, ACT.Sqrt).then_inc(sem(f"{name}_root"), 1)

                    for t in range(3):
                        squares(h[:, t, :], x[:, t, :], ss[:, t:t + 1], "x_squares" if t == 2 else None)
                    root(rt, ss, "x")
                    act.wait_ge(sem("vt_ready"), 1)
                    with act.Fori(0, 4) as i:
                        wide.enter(i, 4)
                        for k in range(4):
                            b = wide.read()
                            m = i * 4 + k
                            wide.emptied(act.activation(gate[:, bass.ds(m, 1), :].rearrange("p o t -> p (o t)"), ps[:, b, 0:TOKENS], ACT.Sigmoid,
                                                        bias=vt[:, bass.ds(m + (CONV + 1) * CC, 1)]))
                    wide.leave(4)
                    with act.Fori(0, 2) as i:
                        wide.base = i * 4
                        wide.per = 4
                        for k in range(4):
                            b = wide.read()
                            wide.emptied(act.copy(zt[:, bass.ds(i * 4 + k, 1), :].rearrange("p o t -> p (o t)"), ps[:, b, 0:TOKENS]))
                    wide.leave(2)
                    with act.Fori(0, 3) as i:
                        wide.base = i * 4
                        for k in range(4):
                            b = wide.read()
                            m = i * 4 + k
                            act.copy(pad[:, bass.ds(m, 1), PAD:PAD + SEQ].rearrange("p o t -> p (o t)"), ps[:, b, 0:SEQ])
                            wide.emptied(act.copy(pad_s[:, bass.ds(m, 1), :, PAD].rearrange("p o t -> p (o t)"), ps[:, b, SEQ:TOKENS]))
                    wide.leave(3)
                    assert wide.n == marks["main"]
                    act.wait_ge(sem("wide_free"), 4 + marks["main"])
                    act.activation(zsig, zt, ACT.Sigmoid).then_inc(sem("z_sigmoid"), 1)
                    act.wait_ge(sem("tok_zeroed"), 1)
                    for n, (first, cols) in enumerate(TAIL):
                        if n == 2:
                            act.wait_ge(sem("conv_raw"), 1)
                            act.wait_ge(sem("z_ready"), 1)
                            act.activation(sig[:, :, 0:CONV_OUT], conv[:, :, 0:CONV_OUT], ACT.Sigmoid).then_inc(sem("conv_sigmoid"), 1)
                        for t, (t0, rows) in enumerate(TILES):
                            b = wide.read()
                            wide.emptied(act.copy(tok[0:rows, t, first:first + cols], ps[0:rows, b, 0:cols]))
                    act.wait_ge(sem("abs_ready"), 1)
                    act.activation(hd[:, HEADS:2 * HEADS], hd[:, HEADS:2 * HEADS], ACT.Exp)
                    act.activation(dte, dte, ACT.Exp, scale=-1.0).then_inc(sem("dt_exp"), 1)
                    act.wait_ge(sem("dtw_ready"), 1)
                    act.activation(dtl, dtw, ACT.Ln).then_inc(sem("dt_log"), 1)
                    act.wait_ge(sem("decays_raw"), 1)
                    act.activation(ea, a_cs[:, :, 0, :], ACT.Exp)
                    act.activation(eend[:, 0, :], dta[:, 2, :], ACT.Exp).then_inc(sem("da_ready"), 1)
                    act.activation(decf, decf, ACT.Exp)
                    act.activation(dec, dec, ACT.Exp).then_inc(sem("decays_ready"), 1)
                    act.wait_ge(sem("conv_ready"), 1)
                    for t in range(2):
                        if t == 1:
                            act.wait_ge(sem("aux_full"), marks["ydiag0"])
                        for q in range(4):
                            b = wide.read()
                            for k in range(4):
                                hh = 4 * q + k
                                last = act.activation(el[:, hh, :], ps[:, b, k * P:(k + 1) * P], ACT.Exp, bias=nacs[:, t, hh:hh + 1])
                            wide.emptied(last)
                    act.wait_ge(sem("dtx_ready"), 1)
                    for s in range(SAMPLES):
                        if s >= 2:
                            act.wait_ge(sem("state_ready"), s - 1)
                        b = wide.read()
                        for k in range(DC):
                            g = k // 4
                            last = act.activation(stx[:, s % 2, k, :], ps[:, b, g * P:(g + 1) * P], ACT.Copy, scale=dtx3[:, k, s:s + 1])
                        wide.emptied(last)
                        act.wait_ge(sem(f"state_load{s % 4}"), 16 * (s // 4 + 1))
                        for k in range(DC):
                            last = act.activation(places[s % 4][:, k, :], places[s % 4][:, k, :], ACT.Copy, scale=exs4[:, k, 1, s:s + 1])
                        last.then_inc(sem("state_decayed"), 1)
                    act.wait_ge(sem("y_gated"), 1)
                    for t in range(3):
                        for g in range(GROUPS):
                            squares(h[:, t, g * 512:(g + 1) * 512], y[:, t, g * 512:(g + 1) * 512], ss6[:, 2 * t + g:2 * t + g + 1], "y_squares" if (t, g) == (2, 1) else None)
                    root(rt6, ss6, "y")
                    lsq, lrt = st[:, 27:33], st[:, 33:39]
                    act.wait_ge(sem("wide_free"), 4 + marks["tail"])
                    for t in range(3):
                        squares(h[:, t, 0:Q_LORA], tok[:, t, T_CQ:T_CKV], lsq[:, t:t + 1])
                        squares(h[:, t, 512:512 + KV_LORA], tok[:, t, T_CKV:T_KR], lsq[:, 3 + t:4 + t], "lat_squares" if t == 2 else None)
                    root(lrt, lsq, "lat")
                    for hh in range(A_HEADS):
                        b = wide.read()
                        wide.emptied(act.copy(qnt[0:NOPE, hh, :], ps[0:NOPE, b, 0:TOKENS]))
                    for t, (t0, rows) in enumerate(TILES):
                        b = wide.read()
                        wide.emptied(act.copy(qr[0:rows, t, :, :].rearrange("p h k -> p (h k)"), ps[0:rows, b, 0:256]))
                    for c in range(2):
                        for hh in range(A_HEADS):
                            b = wide.read()
                            wide.emptied(act.copy(ql[:, c, hh, :], ps[:, b, 0:TOKENS]))
                    for t in range(2):
                        act.wait_ge(sem("scores_max"), t + 1)
                        for hh in range(A_HEADS):
                            last = act.activation(sc[:, hh, 0:P * (t + 1)], sc[:, hh, 0:P * (t + 1)], ACT.Exp, scale=SCALE, bias=anm[:, hh:hh + 1], accum_out=asum[:, hh:hh + 1])
                        last.then_inc(sem("scores_exp"), 1)
                    def page_copy(n):
                        c, q = n // 2, 2 * (n % 2) + 1
                        b = wide.read()
                        wide.emptied(act.copy(kt[:, c, 4 * q:4 * q + 4, :].rearrange("p j t -> p (j t)"), ps[:, b, :]))

                    def sample(s, turn_no, more):
                        if more:
                            for n in range(2):
                                page_copy(n)
                        act.wait_ge(sem("max_ready"), turn_no * 2 + s + 1)
                        act.activation(srow[0:A_HEADS, :], srow[0:A_HEADS, :], ACT.Exp, scale=SCALE, bias=sneg[0:A_HEADS, :],
                                       accum_out=ssum[0:A_HEADS, :]).then_inc(sem("sample_exp"), 1)
                        if more:
                            for n in range(2, 4):
                                page_copy(n)

                    for n in range(4):
                        page_copy(n)
                    with act.Fori(0, SAMPLES // 2 - 1) as i:
                        wide.enter(i, 8)
                        for s in range(2):
                            sample(s, i, True)
                    wide.leave(SAMPLES // 2 - 1)
                    for s in range(2):
                        sample(s, SAMPLES // 2 - 1, s == 0)

                    act.wait_ge(sem("x_mixed"), 1)
                    act.wait_ge(sem("attention_done"), 1)
                    for t in range(3):
                        squares(h[:, t, :], x[:, t, :], st[:, 45 + t:46 + t], "px_squares" if t == 2 else None)
                    root(st[:, 48:51], st[:, 45:48], "px")
                    with act.Fori(0, 4) as i:
                        wide.enter(i, 4)
                        for k in range(4):
                            b = wide.read()
                            wide.emptied(act.copy(gate[:, bass.ds(i * 4 + k, 1), :].rearrange("p o t -> p (o t)"), ps[:, b, 0:TOKENS]))
                    wide.leave(4)
                    def scores_out(t):
                        if PLACE[t]:
                            act.wait_ge(sem("scores_used"), PLACE[t])
                        for q in range(4 if t < 2 else 1):
                            b = wide.read()
                            cols, rows = (512, P) if t < 2 else (256, 64)
                            wide.emptied(act.copy(keysc.rearrange("p k n -> p (k n)")[0:rows, q * 512:q * 512 + cols], ps[0:rows, b, 0:cols]))

                    def weights(t):
                        rows, n16 = (P, P) if t < 2 else (64, TOPK)
                        act.wait_ge(sem("experts_shifted"), PLACE[t] + 1)
                        act.activation(wgt[0:rows, t, 0:n16], wgt[0:rows, t, 0:n16], ACT.Exp).then_inc(sem("experts_exp"), 1)

                    def gelu(t):
                        rows, n16 = (P, P) if t < 2 else (64, TOPK)
                        act.wait_ge(sem("dots_ready"), PLACE[t] + 1)
                        act.activation(dots[0:rows, 0:n16], dots[0:rows, 0:n16], ACT.Gelu).then_inc(sem("gelu_ready"), 1)

                    scores_out(2)
                    weights(2)
                    scores_out(0)
                    gelu(2)
                    scores_out(1)
                    weights(0)
                    gelu(0)
                    weights(1)
                    gelu(1)

                @block.sync
                def _(sp):
                    vr = ssd("vrows")
                    sp.dma_start(vr[0:CONV * CC, :], of_layer("conv_w", layer).rearrange("k (c p) -> (k c) p", p=P)).then_inc(sem("vec_loads"), 16)
                    sp.dma_start(vr[CONV * CC:CONV * CC + CC, :], of_layer("conv_b", layer).rearrange("(c p) -> c p", p=P)).then_inc(sem("vec_loads"), 16)
                    sp.dma_start(vr[CONV * CC + CC:VEC_ROWS, :], of_layer("b_gate", layer).rearrange("(c p) -> c p", p=P)).then_inc(sem("vec_loads"), 16)
                    sp.dma_start(nrow[:, :], of_layer("norm_mix", layer).partition_broadcast(P)).then_inc(sem("nrow_load"), 16)

                    count = [0]

                    def load_block(src, chunks, cols, base=None):
                        n = count[0]
                        if n >= 2 or base is not None:
                            sp.wait_ge(sem("blocks_begun"), n if base is None else base + n)
                        sp.dma_start(wblock(n % 2, chunks, cols), src).then_inc(sem(f"block{n % 2}_loads"), 16)
                        count[0] += 1

                    w_in = of_layer("w_in", layer).rearrange("(p c) n -> p c n", c=DC)
                    for k in range(2):
                        load_block(w_in[:, :, k * BLOCK:(k + 1) * BLOCK], DC, BLOCK)
                    with sp.Fori(1, MAIN_BLOCKS // 2) as i:
                        for k in range(2):
                            count[0] = k
                            load_block(w_in[:, :, bass.ds(i * 2 * BLOCK + k * BLOCK, BLOCK)], DC, BLOCK, base=i * 2)
                    count[0] = MAIN_BLOCKS
                    for v, name in enumerate(("dt_bias", "a_log", "d_skip")):
                        sp.dma_start(hd[:, v * HEADS:(v + 1) * HEADS], of_layer(name, layer).partition_broadcast(P)).then_inc(sem("head_loads"), 16)
                    sp.dma_start(kvn[:, :], of_layer("kv_norm", layer).partition_broadcast(P)).then_inc(sem("head_loads"), 16)
                    sp.dma_start(qn[:, :], of_layer("q_norm", layer).rearrange("(p c) -> p c", c=3)).then_inc(sem("head_loads"), 16)
                    sp.dma_start(ssmn[:, :], of_layer("ssm_norm", layer).rearrange("(p c) -> p c", c=DC)).then_inc(sem("head_loads"), 16)
                    for first, cols in TAIL:
                        load_block(w_in[:, :, C_DT + first:C_DT + first + cols], DC, cols)
                    w_ssm = of_layer("w_ssm_proj", layer).rearrange("(p c) n -> p c n", c=DC)
                    w_out = of_layer("w_out", layer).rearrange("(c p) n -> p c n", p=P)
                    w_mla = of_layer("w_mla_proj", layer).rearrange("(c p) n -> p c n", p=P)
                    for k in range(4):
                        load_block(w_ssm[:, :, k * BLOCK:(k + 1) * BLOCK], DC, BLOCK)
                    for k in range(2):
                        load_block(w_mla[:, :, 2 * k * BLOCK:2 * (k + 1) * BLOCK], 4, 2 * BLOCK)
                    for k in range(4):
                        load_block(w_out[:, :, k * BLOCK:(k + 1) * BLOCK], DC, BLOCK)
                    w_q = of_layer("peer_wq", layer).rearrange("(p c) n -> p c n", c=DC)
                    first = count[0]
                    assert first == marks["wq_block"]
                    with sp.Fori(0, 4) as i:
                        for k in range(2):
                            count[0] = first + k
                            load_block(w_q[:, :, bass.ds(i * 2 * BLOCK + k * BLOCK, BLOCK)], DC, BLOCK, base=i * 2)

                @block.gpsimd
                def _(pool):
                    pages = a["cache_latent"].rearrange("l n (r k) d -> (l n r) (k d)", k=PIECE)
                    kropes = a["cache_krope"].rearrange("l n (r k) d -> (l n r) (k d)", k=PIECE)
                    pool.tensor_scalar(pagef[:, 0:SAMPLES], pagef[:, SAMPLES:], layer_off[:, 0:1], None, ALU.add).then_inc(sem("pool_pages"), 1)
                    pool.wait_ge(sem("pool_pages"), 1)
                    pool.tensor_copy(page_idx[:, SAMPLES:], pagef[:, 0:SAMPLES]).then_inc(sem("pool_pages"), 1)
                    pool.wait_ge(sem("pool_pages"), 2)
                    pool.dma_start(wkv, of_layer("w_kvb", layer).rearrange("(c p) n -> p c n", p=P)).then_inc(sem("wkv_load"), 16)
                    pool.dma_start(ssd("cstate")[0:PAD * SAMPLES, :], of_layer("state_conv", layer).rearrange("b k c -> (b k) c")).then_inc(sem("cstate_load"), 16)
                    pool.dma_start(of_layer_out(o_convs, layer)[:, 0:PAD - 1, :], of_layer("state_conv", layer)[:, 1:PAD, :]).then_inc(sem("stores"), 16)
                    pool.wait_ge(sem("rawt_ready"), 1)
                    pool.dma_start(of_layer_out(o_convp, layer)[0, :, :], rawt[0:PAD, :]).then_inc(sem("stores"), 16)
                    pool.dma_start(of_layer_out(o_convs, layer)[:, PAD - 1, :], rawt[PAD:PAD + SAMPLES, :]).then_inc(sem("rawt_stores"), 16)
                    pool.wait_ge(sem("stores"), 32)
                    pool.wait_ge(sem("rawt_stores"), 16)
                    pool.nop().then_inc(sem("rawt_stored"), 1)
                    pool.wait_ge(sem("hs_ready"), 1)
                    pool.dma_start(of_layer_out(o_ssmp, layer)[0].rearrange("g e p n -> (g e p) n").rearrange("(c q) n -> q c n", q=P),
                                 hs.rearrange("p (c n) -> p c n", c=DC)).then_inc(sem("stores"), 16)
                    h0 = of_layer("state_ssm", layer).rearrange("b g e p n -> b (g e p) n").rearrange("b (c q) n -> b q c n", q=P)
                    h1 = of_layer_out(o_ssms, layer).rearrange("b g e p n -> b (g e p) n").rearrange("b (c q) n -> b q c n", q=P)
                    pool.wait_ge(sem("el_used"), 1)
                    for b in range(4):
                        pool.dma_start(places[b], h0[b]).then_inc(sem(f"state_load{b}"), 16)
                    for b in range(SAMPLES):
                        pool.wait_ge(sem("state_ready"), b + 1)
                        pool.dma_start(h1[b], places[b % 4]).then_inc(sem(f"state_store{b % 4}"), 16)
                        if 1 <= b < 5:
                            pool.wait_ge(sem(f"state_store{b - 1}"), 16)
                            pool.wait_ge(sem("state_used"), b)
                            pool.dma_start(places[b - 1], h0[b + 3]).then_inc(sem(f"state_load{b - 1}"), 16)
                    pool.wait_ge(sem("y_gated"), 1)
                    for s in range(4):
                        pool.wait_ge(sem(f"state_store{s}"), 16 * (SAMPLES // 4))
                    pool.dma_start(wqb, of_layer("w_qb", layer).rearrange("(p c) n -> p c n", c=3)).then_inc(sem("wqb_load"), 16)
                    pool.wait_ge(sem("lat_ready"), 1)
                    pool.dma_start(of_layer_out(o_latp, layer)[0].rearrange("(t p) r -> p t r", p=P), lat[:, 0:2, :]).then_inc(sem("stores"), 16)
                    pool.dma_start(of_layer_out(o_lats, layer)[:, 0, :], lat[0:SAMPLES, 2, :]).then_inc(sem("stores"), 16)
                    pool.dma_start(of_layer_out(o_krp, layer)[0].rearrange("(t p) r -> p t r", p=P), kpe[:, 0:2, :]).then_inc(sem("stores"), 16)
                    pool.dma_start(of_layer_out(o_krs, layer)[:, 0, :], kpe[0:SAMPLES, 2, :]).then_inc(sem("stores"), 16)
                    pool.wait_ge(sem("scan_done"), 1)
                    pool.wait_ge(sem("nrow_used"), 1)
                    pool.dma_start(nrow[:, :], of_layer("norm_ffn", layer).partition_broadcast(P)).then_inc(sem("ffn_row_load"), 16)
                    pool.wait_ge(sem("queries_done"), 1)
                    for b in range(SAMPLES):
                        s = b % 2
                        if b >= 2:
                            pool.wait_ge(sem("aux_full"), marks["att"] + 12 * (b - 1))
                        for dst, src in ((ck, pages), (cr, kropes)):
                            pool.indirect_dma_start(dst[:, s, :, :].rearrange("p j r -> p (j r)"), None, src,
                                                    bass.IndirectOffsetOnAxis(ap=page_idx[:, SAMPLES + b:SAMPLES + b + 1], axis=0)).then_inc(sem(f"pages{s}_loads"), 16)
                    for s in range(2):
                        pool.wait_ge(sem(f"pages{s}_loads"), 32 * (SAMPLES // 2))
                    pool.wait_ge(sem("attention_done"), 1)
                    pool.dma_start(keys, of_layer("peer_keys", layer).rearrange("h s k d -> k (h s) d")).then_inc(sem("keys_load"), 16)
                    tables = [a[name].rearrange("l n d -> (l n) d") for name in ("peer_u", "peer_v")]
                    pool.memset(settled, 0.0).then_inc(sem("settled_zeroed"), 1)
                    pool.wait_ge(sem("settled_zeroed"), 1)

                    def outputs_used(turn, t, k):
                        name, slots, uses = (("tensor_slots_used", PE_SLOTS, PE_USES) if k in PE_SLOTS else
                                             ("vector_slots_used", VECTOR_SLOTS, VECTOR_USES))
                        return sem(name), turn * len(slots) + (uses[t] + slots.index(k) + 1)

                    def inputs_used(turn, t, k):
                        return sem("rows_dotted"), turn * RING + (U_DONE[t] - RING + k + 1)

                    def gather(t, table, used, used_before):
                        rows = P if t < 2 else 64
                        for ii in pairs_of_turns(pool, t):
                            for u in range(2):
                                i = ii * 2 + u
                                pool.tensor_copy(stage[0:rows, u * RING:(u + 1) * RING], idx[0:rows, t, bass.ds(i * RING, RING)]).then_inc(sem("staged"), 1)
                                for k in range(RING):
                                    if k == 0:
                                        pool.wait_ge(sem("staged"), i + (staged[0] + 1))
                                    pool.wait_ge(*used(i, t, k))
                                    if used_before is not None:
                                        pool.wait_ge(*used_before(k))
                                    step = slice(u * RING + k, u * RING + k + 1)
                                    pool.tensor_tensor(settled[:, step], settled[:, 2 * RING:], settled[:, 2 * RING:], ALU.add)
                                    pool.indirect_dma_start(ring[0:rows, k, :], None, table,
                                                            bass.IndirectOffsetOnAxis(ap=stage[0:rows, step], axis=0)).then_inc(sem(f"slot{k}_loads"), 16)
                        staged[0] += TURNS[t]

                    staged = [0]
                    for t in ORDER:
                        pool.wait_ge(sem("idx_ready"), PLACE[t] + 1)
                        gather(t, tables[0], inputs_used, (lambda k: outputs_used(0, t, k)) if PLACE[t] else None)
                        gather(t, tables[1], outputs_used, lambda k: inputs_used(TURNS[t], t, k))
                    for k in range(RING):
                        pool.wait_ge(sem(f"slot{k}_loads"), 16 * 2 * sum(TURNS))
                    pool.wait_ge(sem("stores"), 16 * 7)
                    for name in ("cstate_load", "wqb_load", "wkv_load", "ffn_row_load", "keys_load"):
                        pool.wait_ge(sem(name), 16)
                    for s in range(4):
                        pool.wait_ge(sem(f"state_load{s}"), 16 * (SAMPLES // 4))
                    pool.dma_reset(span(sems))

            nc.all_engine_barrier(sems_to_clear=span(sems))

        with nc.Block() as block:
            @block.sync
            def _(sp):
                sp.dma_start(nrow[:, :], a["norm_final"].partition_broadcast(P)).then_inc(sem("nrow_load"), 16)
                sp.wait_ge(sem("h_ready"), 1)
                sp.dma_start(o_yp.rearrange("o (t p) d -> p (o t) d", p=P), h[:, 0:2, :]).then_inc(sem("y_stores"), 16)
                sp.dma_start(o_ys.rearrange("b o d -> (b o) d"), h[0:SAMPLES, 2, :]).then_inc(sem("y_stores"), 16)
                sp.wait_ge(sem("y_stores"), 32)

            @block.scalar
            def _(act):
                for t in range(3):
                    last = act.activation(h[:, t, :], x[:, t, :], ACT.Square, accum_out=ss[:, t:t + 1])
                last.then_inc(sem("x_squares"), 1)
                act.wait_ge(sem("x_squares_mean"), 1)
                act.activation(rt, ss, ACT.Sqrt).then_inc(sem("x_root"), 1)

            @block.vector
            def _(dve):
                dve.wait_ge(sem("x_squares"), 1)
                dve.tensor_scalar(ss, ss, 1.0 / D_MODEL, EPS, ALU.mult, ALU.add).then_inc(sem("x_squares_mean"), 1)
                dve.wait_ge(sem("x_root"), 1)
                dve.reciprocal(rs, rt).then_inc(sem("vector_steps"), 1)
                dve.wait_ge(sem("vector_steps"), 1)
                dve.wait_ge(sem("nrow_load"), 16)
                for t in range(3):
                    last = dve.scalar_tensor_tensor(out=h[:, t, :], in0=x[:, t, :], scalar=rs[:, t:t + 1], in1=nrow[:, :], op0=ALU.mult, op1=ALU.mult)
                last.then_inc(sem("h_ready"), 1)


_INPUTS = ["x_prompt", "x_sample", "cache_latent", "cache_krope", "state_ssm", "state_conv", "page_table",
           "norm_mix", "w_in", "b_gate", "conv_w", "conv_b", "dt_bias", "a_log", "d_skip", "ssm_norm", "w_ssm_proj",
           "q_norm", "w_qb", "kv_norm", "w_kvb", "w_mla_proj", "w_out", "norm_ffn", "peer_wq", "peer_keys",
           "peer_u", "peer_v", "norm_final"]
_OUTPUTS = [(1, SEQ, D_MODEL), (SAMPLES, 1, D_MODEL), (DEPTH, 1, SEQ, KV_LORA), (DEPTH, 1, SEQ, ROPE),
            (DEPTH, 1, GROUPS, HEADS // GROUPS, HEAD_DIM, D_STATE), (DEPTH, 1, PAD, CONV_DIM),
            (DEPTH, SAMPLES, 1, KV_LORA), (DEPTH, SAMPLES, 1, ROPE),
            (DEPTH, SAMPLES, GROUPS, HEADS // GROUPS, HEAD_DIM, D_STATE), (DEPTH, SAMPLES, PAD, CONV_DIM)]


def kernel(**inputs):
    import concourse.bacc as bacc
    from concourse.bass_utils import run_bass_kernel_spmd

    nc = bacc.Bacc("TRN2", target_bir_lowering=False, num_devices=1)
    arrays, args = {}, {}
    for name in _INPUTS + ["consts"]:
        arr = CONST_ARRAY if name == "consts" else np.ascontiguousarray(inputs[name])
        arrays["in_" + name] = arr
        args[name] = nc.dram_tensor("in_" + name, arr.shape, mybir.dt.from_np(arr.dtype), kind="ExternalInput").ap()
    outs = [nc.dram_tensor(f"out_{i}", s, F32, kind="ExternalOutput").ap() for i, s in enumerate(_OUTPUTS)]
    build(nc, DEPTH, args, outs)
    r = run_bass_kernel_spmd(nc, [arrays], core_ids=[0])
    return tuple(r.results[0][f"out_{i}"] for i in range(len(_OUTPUTS)))
```
